# Optimizing a Trainium2 kernel written in Bass

```python
import math
import jax
import jax.numpy as jnp
from jax import lax
import numpy as np

D_MODEL = 1024
BATCH = 1
SEQ = 128
DEPTH = 1
DEC_BATCH = 1
DEC_SEQ = 512
PAST_LEN = 128

GRID_W = 64
BRANCH_WIDTH = 512
N_BRANCH = 3

A_DK = 128
A_DV = 128
A_HEADS = BRANCH_WIDTH // A_DV
A_CHUNK = 16

B_WIDTH = BRANCH_WIDTH
HY_BANDS = 16
HY_EMB = 1 + 2 * HY_BANDS
HY_FFN = 64

C_HEAD_DIM = 64
C_HEADS = BRANCH_WIDTH // C_HEAD_DIM
C_WIDTH = BRANCH_WIDTH
C_DECAY_LORA = 64
C_AAA_LORA = 64
C_GATE_LORA = 128

A_COLS = 3 * A_HEADS * A_DK + A_HEADS * A_DV + BRANCH_WIDTH
B_COLS = 3 * B_WIDTH
C_COLS = 3 * C_WIDTH + 2 * C_DECAY_LORA + 2 * C_AAA_LORA + C_GATE_LORA
IN_COLS = A_COLS + B_COLS + C_COLS + N_BRANCH * D_MODEL

P_HEADS = 8
P_NKEYS = 128
P_EXPERTS = P_NKEYS * P_NKEYS
P_TOPK = 16
P_KEY_DIM = 128
P_BLOCK = 128

EPS = 1e-6
RWKV_GN_EPS = 64e-5

kernel_name = 'hybrid_flow_prefix_trunk_step'

def rms_norm(x, gain):
    xf = x.astype(jnp.float32)
    return xf * lax.rsqrt(jnp.mean(xf * xf, axis=-1, keepdims=True) + EPS) * gain

def adaln(cvec, w, b):
    m = jax.nn.silu(cvec) @ w + b
    return jnp.split(m[..., None, :], 6, axis=-1)

def shift_prev(x):
    return jnp.pad(x, ((0, 0), (1, 0), (0, 0)))[:, :-1]

def shift_next(x):
    return jnp.pad(x, ((0, 0), (0, 1), (0, 0)))[:, 1:]

def neighbour_mean(x, latent):
    if not latent:
        return 0.5 * (shift_prev(x) + shift_next(x))
    B, T, C = x.shape
    rows = T // GRID_W
    gp = jnp.pad(x.reshape(B, rows, GRID_W, C), ((0, 0), (1, 1), (1, 1), (0, 0)))
    s = gp[:, :-2, 1:-1] + gp[:, 2:, 1:-1] + gp[:, 1:-1, :-2] + gp[:, 1:-1, 2:]
    return (0.25 * s).reshape(B, T, C)

def hgrn2_chunkwise(q, k, v, logf, S0):
    B, T, H, K = q.shape
    V = v.shape[-1]
    C = A_CHUNK
    N = T // C
    q, k, logf = (a.reshape(B, N, C, H, K) for a in (q, k, logf))
    v = v.reshape(B, N, C, H, V)
    b = jnp.cumsum(logf.astype(jnp.float32), axis=2)
    causal = jnp.tril(jnp.ones((C, C), dtype=bool))[:, :, None, None]
    diff = b[:, :, :, None] - b[:, :, None, :]
    decay = jnp.exp(jnp.where(causal, diff, -jnp.inf))
    attn = jnp.einsum('bnthk,bnshk,bntshk->bnhts', q, k, decay)
    o_intra = jnp.einsum('bnhts,bnshv->bnthv', attn, v)
    b_last = b[:, :, -1]
    ds = jnp.einsum('bnshk,bnshv->bnhkv', k * jnp.exp(b_last[:, :, None] - b), v)

    def step(S, inp):
        dec, dS = inp
        return S * dec[..., None] + dS, S

    S_fin, S_start = lax.scan(step, S0.astype(jnp.float32),
                              (jnp.moveaxis(jnp.exp(b_last), 1, 0), jnp.moveaxis(ds, 1, 0)))
    o_inter = jnp.einsum('bnthk,bnhkv->bnthv', q * jnp.exp(b), jnp.moveaxis(S_start, 0, 1))
    return (o_intra + o_inter).reshape(B, T, H, V), S_fin

def hgrn2_branch(pa, S0, lp):
    B, T, _ = pa.shape
    hk = A_HEADS * A_DK
    q, f_fwd, f_bwd, i, g = jnp.split(pa, [hk, 2 * hk, 3 * hk, 3 * hk + A_HEADS * A_DV], axis=-1)
    q = jax.nn.silu(q).reshape(B, T, A_HEADS, A_DK)
    i = i.reshape(B, T, A_HEADS, A_DV)
    outs, finals = [], []
    for d, fz in enumerate((f_fwd, f_bwd)):
        lb = lp['lb'][d]
        f = lb + (1.0 - lb) * jax.nn.sigmoid(fz.astype(jnp.float32))
        seq = (q, (1.0 - f).reshape(B, T, A_HEADS, A_DK), i, jnp.log(f).reshape(B, T, A_HEADS, A_DK))
        if d == 1:
            seq = tuple(z[:, ::-1] for z in seq)
        o, S = hgrn2_chunkwise(*seq, S0[:, d])
        outs.append(o if d == 0 else o[:, ::-1])
        finals.append(S)
    o = rms_norm(outs[0] + outs[1], lp['hgrn_norm']).reshape(B, T, BRANCH_WIDTH)
    return o * jax.nn.silu(g), jnp.stack(finals, axis=1)

def hyena_kernel_freq(L, lp):
    t = jnp.linspace(0.0, 1.0, L, dtype=jnp.float32)[:, None]
    bands = jnp.linspace(1e-4, HY_BANDS - 1, HY_BANDS, dtype=jnp.float32)[None, :]
    ang = (2 * math.pi / L) * jnp.arange(L, dtype=jnp.float32)[:, None] * bands
    z = jnp.concatenate([t, jnp.cos(ang), -jnp.sin(ang)], axis=-1)
    hf = jnp.sin(lp['hy_freq1'] * (z @ lp['hy_w1'] + lp['hy_b1']))
    hf = jnp.sin(lp['hy_freq2'] * (hf @ lp['hy_w2'] + lp['hy_b2']))
    hf = (hf @ lp['hy_w3']).reshape(L, 2, B_WIDTH) * jnp.exp(-t * jnp.abs(lp['hy_delta']))[:, None, :]
    kern = jnp.concatenate([hf[:, 0], jnp.zeros((1, B_WIDTH), hf.dtype), hf[:0:-1, 1]], axis=0)
    kern = kern / jnp.sum(jnp.abs(kern), axis=0, keepdims=True)
    return jnp.fft.rfft(kern.astype(jnp.float32), axis=0)

def hyena_branch(pb, lp):
    B, L, _ = pb.shape
    cw = lp['hy_conv_w']
    u = shift_prev(pb) * cw[0] + pb * cw[1] + shift_next(pb) * cw[2] + lp['hy_conv_b']
    x0, x1, v = jnp.split(u, 3, axis=-1)
    z = (v * x1).astype(jnp.float32)
    y = jnp.fft.irfft(jnp.fft.rfft(z, n=2 * L, axis=1) * hyena_kernel_freq(L, lp), n=2 * L, axis=1)[:, :L]
    return x0 * (y + z * lp['hy_bias'])

def rwkv7_scan(seq, S0):
    def step(S, inp):
        r_t, w_t, k_t, v_t, a_t, b_t = inp
        sa = jnp.einsum('bhvk,bhk->bhv', S, a_t)
        S = S * w_t[:, :, None, :] + sa[..., None] * b_t[:, :, None, :] + v_t[..., None] * k_t[:, :, None, :]
        return S, jnp.einsum('bhvk,bhk->bhv', S, r_t)

    S, ys = lax.scan(step, S0.astype(jnp.float32), tuple(jnp.swapaxes(z, 0, 1) for z in seq))
    return jnp.swapaxes(ys, 0, 1), S

def rwkv7_branch(pc, S0, lp, latent):
    B, T, _ = pc.shape
    pc = pc + (neighbour_mean(pc, latent) - pc) * lp['rw_mu']
    cut = [C_WIDTH, 2 * C_WIDTH, 3 * C_WIDTH, 3 * C_WIDTH + 2 * C_DECAY_LORA,
           3 * C_WIDTH + 2 * C_DECAY_LORA + 2 * C_AAA_LORA]
    r, k, v, wd, ad, gd = jnp.split(pc, cut, axis=-1)
    heads = lambda z: z.reshape(B, T, C_HEADS, C_HEAD_DIM)
    kk = heads(k * lp['rw_kk']).astype(jnp.float32)
    kk = kk * lax.rsqrt(jnp.sum(kk * kk, axis=-1, keepdims=True) + 1e-12)
    g = jax.nn.sigmoid(gd) @ lp['rw_g2']
    wd = wd.reshape(B, T, 2, C_DECAY_LORA)
    ad = ad.reshape(B, T, 2, C_AAA_LORA)
    ys, finals = [], []
    for d in range(2):
        w = -jax.nn.softplus(-(lp['rw_w0'][d] + jnp.tanh(wd[:, :, d]) @ lp['rw_w2'][d])) - 0.5
        decay = jnp.exp(-jnp.exp(w.astype(jnp.float32)))
        a = jax.nn.sigmoid(lp['rw_a0'][d] + ad[:, :, d] @ lp['rw_a2'][d])
        kd = k * (1 + (a - 1) * lp['rw_ka'])
        seq = (heads(r), heads(decay), heads(kd), heads(v), -kk, kk * heads(a))
        if d == 1:
            seq = tuple(z[:, ::-1] for z in seq)
        y, S = rwkv7_scan(seq, S0[:, d])
        ys.append(y if d == 0 else y[:, ::-1])
        finals.append(S)
    y = (ys[0] + ys[1]).astype(jnp.float32)
    mu = jnp.mean(y, axis=-1, keepdims=True)
    var = jnp.mean(jnp.square(y - mu), axis=-1, keepdims=True)
    y = ((y - mu) * lax.rsqrt(var + RWKV_GN_EPS)).reshape(B, T, C_WIDTH) * lp['rw_ln_g'] + lp['rw_ln_b']
    bonus = jnp.sum(heads(r) * heads(k) * lp['rw_rk'], axis=-1, keepdims=True) * heads(v)
    return (y + bonus.reshape(B, T, C_WIDTH)) * g, jnp.stack(finals, axis=1)

def token_mixers(h, lp, S_a0, S_c0, latent):
    proj = h @ lp['w_in']
    pa, pb, pc, pg = jnp.split(proj, [A_COLS, A_COLS + B_COLS, A_COLS + B_COLS + C_COLS], axis=-1)
    ya, S_a = hgrn2_branch(pa, S_a0, lp)
    yb = hyena_branch(pb, lp)
    yc, S_c = rwkv7_branch(pc, S_c0, lp, latent)
    ga, gb, gc = jnp.split(jax.nn.sigmoid(pg), N_BRANCH, axis=-1)
    wb = lp['w_branch']
    merged = ga * (ya @ wb[0]) + gb * (yb @ wb[1]) + gc * (yc @ wb[2])
    return merged @ lp['w_out'], S_a, S_c

def peer_ffn(h, lp):
    B, T, D = h.shape
    u_tab, v_tab = lp['p_u'], lp['p_v']

    def block(hb):
        q = (hb @ lp['p_wq']).reshape(P_BLOCK, P_HEADS, 2, P_KEY_DIM // 2)
        s1 = jnp.einsum('thd,nd->thn', q[:, :, 0], lp['p_key1'])
        s2 = jnp.einsum('thd,nd->thn', q[:, :, 1], lp['p_key2'])
        v1, i1 = lax.top_k(s1, P_TOPK)
        v2, i2 = lax.top_k(s2, P_TOPK)
        cand = (v1[..., :, None] + v2[..., None, :]).reshape(P_BLOCK, P_HEADS, P_TOPK * P_TOPK)
        sc, ci = lax.top_k(cand, P_TOPK)
        expert = (jnp.take_along_axis(i1, ci // P_TOPK, axis=-1) * P_NKEYS
                  + jnp.take_along_axis(i2, ci % P_TOPK, axis=-1))
        gate = jax.nn.softmax(sc.astype(jnp.float32), axis=-1)
        act = jax.nn.gelu(jnp.einsum('td,thkd->thk', hb, u_tab[expert]))
        return jnp.einsum('thk,thkd->td', gate * act, v_tab[expert])

    return lax.map(block, h.reshape(-1, P_BLOCK, D)).reshape(B, T, D)

def trunk_layer(x, mod, lp, S_a0, S_c0, latent):
    sh1, sc1, g1, sh2, sc2, g2 = mod
    h = rms_norm(x, lp['norm1']) * (1 + sc1) + sh1
    mix, S_a, S_c = token_mixers(h, lp, S_a0, S_c0, latent)
    x = x + g1 * mix
    h = rms_norm(x, lp['norm2']) * (1 + sc2) + sh2
    x = x + g2 * peer_ffn(h, lp)
    return x, S_a, S_c

def setup_inputs(seed: int = 0) -> dict:
    key = jax.random.key(seed)
    ks = iter(jax.random.split(key, 64))
    nrm = lambda shape, scale: jax.random.normal(next(ks), shape, jnp.float32) * scale
    unif = lambda shape, lo, hi: jax.random.uniform(next(ks), shape, jnp.float32, lo, hi)
    L, D = DEPTH, D_MODEL
    return {
        'x_prompt': nrm((BATCH, SEQ, D), 1.0),
        'x_sample': nrm((DEC_BATCH, DEC_SEQ, D), 1.0),
        'state_hgrn': nrm((DEC_BATCH, DEPTH, 2, A_HEADS, A_DK, A_DV), 0.3),
        'state_rwkv': nrm((DEC_BATCH, DEPTH, 2, C_HEADS, C_HEAD_DIM, C_HEAD_DIM), 0.1),
        'c': nrm((DEC_BATCH, D), 1.0),
        'c_ctx': nrm((D,), 1.0),
        'w_ada': nrm((L, D, 6 * D), 0.5 * D ** -0.5),
        'b_ada': nrm((L, 6 * D), 0.02),
        'norm1': 1.0 + nrm((L, D), 0.02),
        'norm2': 1.0 + nrm((L, D), 0.02),
        'w_in': nrm((L, D, IN_COLS), D ** -0.5),
        'hgrn_lb_logits': nrm((2, L, A_HEADS * A_DK), 0.5),
        'hgrn_norm': 1.0 + nrm((L, A_DV), 0.02),
        'hy_conv_w': nrm((L, 3, B_COLS), 0.5),
        'hy_conv_b': nrm((L, B_COLS), 0.02),
        'hy_w1': nrm((L, HY_EMB, HY_FFN), HY_EMB ** -0.5),
        'hy_b1': nrm((L, HY_FFN), 0.1),
        'hy_freq1': 1.0 + nrm((L, HY_FFN), 0.05),
        'hy_w2': nrm((L, HY_FFN, HY_FFN), HY_FFN ** -0.5),
        'hy_b2': nrm((L, HY_FFN), 0.1),
        'hy_freq2': 1.0 + nrm((L, HY_FFN), 0.05),
        'hy_w3': nrm((L, HY_FFN, 2 * B_WIDTH), HY_FFN ** -0.5),
        'hy_delta': unif((L, B_WIDTH), 3.07, 15.35),
        'hy_bias': nrm((L, B_WIDTH), 0.5),
        'rw_mu': unif((L, C_COLS), 0.0, 1.0),
        'rw_w0': unif((L, 2, C_WIDTH), -6.5, -1.5),
        'rw_w2': nrm((L, 2, C_DECAY_LORA, C_WIDTH), 0.1),
        'rw_a0': nrm((L, 2, C_WIDTH), 0.1),
        'rw_a2': nrm((L, 2, C_AAA_LORA, C_WIDTH), 0.1),
        'rw_g2': nrm((L, C_GATE_LORA, C_WIDTH), C_GATE_LORA ** -0.5),
        'rw_kk': 0.85 + nrm((L, C_WIDTH), 0.05),
        'rw_ka': 1.0 + nrm((L, C_WIDTH), 0.05),
        'rw_rk': nrm((L, C_HEADS, C_HEAD_DIM), 0.1),
        'rw_ln_g': 1.0 + nrm((L, C_WIDTH), 0.02),
        'rw_ln_b': nrm((L, C_WIDTH), 0.02),
        'w_branch': nrm((L, N_BRANCH, BRANCH_WIDTH, D), BRANCH_WIDTH ** -0.5),
        'w_out': nrm((L, D, D), D ** -0.5),
        'p_wq': nrm((L, D, P_HEADS * P_KEY_DIM), D ** -0.5),
        'p_key1': nrm((L, P_NKEYS, P_KEY_DIM // 2), (P_KEY_DIM // 2) ** -0.5),
        'p_key2': nrm((L, P_NKEYS, P_KEY_DIM // 2), (P_KEY_DIM // 2) ** -0.5),
        'p_u': nrm((L, P_EXPERTS, D), D ** -0.5),
        'p_v': nrm((L, P_EXPERTS, D), 0.5),
        'final_norm': 1.0 + nrm((D,), 0.02),
    }

def reference(x_prompt, x_sample, state_hgrn, state_rwkv, c, c_ctx, w_ada, b_ada, norm1, norm2, w_in,
              hgrn_lb_logits, hgrn_norm, hy_conv_w, hy_conv_b, hy_w1, hy_b1, hy_freq1, hy_w2, hy_b2,
              hy_freq2, hy_w3, hy_delta, hy_bias, rw_mu, rw_w0, rw_w2, rw_a0, rw_a2, rw_g2, rw_kk, rw_ka,
              rw_rk, rw_ln_g, rw_ln_b, w_branch, w_out, p_wq, p_key1, p_key2, p_u, p_v, final_norm):
    lb_p = jax.nn.softmax(hgrn_lb_logits.astype(jnp.float32), axis=1)
    lb = jnp.cumsum(lb_p, axis=1)
    lb = lb - lb[:, :1]
    n_prompt = x_prompt.shape[0]
    zero_a = jnp.zeros((n_prompt, 2, A_HEADS, A_DK, A_DV), jnp.float32)
    zero_c = jnp.zeros((n_prompt, 2, C_HEADS, C_HEAD_DIM, C_HEAD_DIM), jnp.float32)
    y_p, y_s = x_prompt, x_sample
    new_a, new_c = [], []
    for l in range(DEPTH):
        lp = {
            'norm1': norm1[l], 'norm2': norm2[l], 'w_in': w_in[l], 'hgrn_norm': hgrn_norm[l], 'lb': lb[:, l],
            'hy_conv_w': hy_conv_w[l], 'hy_conv_b': hy_conv_b[l], 'hy_w1': hy_w1[l], 'hy_b1': hy_b1[l],
            'hy_freq1': hy_freq1[l], 'hy_w2': hy_w2[l], 'hy_b2': hy_b2[l], 'hy_freq2': hy_freq2[l],
            'hy_w3': hy_w3[l], 'hy_delta': hy_delta[l], 'hy_bias': hy_bias[l],
            'rw_mu': rw_mu[l], 'rw_w0': rw_w0[l], 'rw_w2': rw_w2[l], 'rw_a0': rw_a0[l], 'rw_a2': rw_a2[l],
            'rw_g2': rw_g2[l], 'rw_kk': rw_kk[l], 'rw_ka': rw_ka[l], 'rw_rk': rw_rk[l],
            'rw_ln_g': rw_ln_g[l], 'rw_ln_b': rw_ln_b[l], 'w_branch': w_branch[l], 'w_out': w_out[l],
            'p_wq': p_wq[l], 'p_key1': p_key1[l], 'p_key2': p_key2[l], 'p_u': p_u[l], 'p_v': p_v[l],
        }
        mod_ctx = adaln(c_ctx, w_ada[l], b_ada[l])
        mod_lat = adaln(c, w_ada[l], b_ada[l])
        y_p, s_a, s_c = trunk_layer(y_p, mod_ctx, lp, zero_a, zero_c, False)
        y_s, _, _ = trunk_layer(y_s, mod_lat, lp, state_hgrn[:, l], state_rwkv[:, l], True)
        new_a.append(s_a)
        new_c.append(s_c)
    y_prompt = rms_norm(y_p, final_norm)
    y_sample = rms_norm(y_s, final_norm)
    new_state_hgrn = jnp.stack(new_a, axis=1)
    new_state_rwkv = jnp.stack(new_c, axis=1)
    return (y_prompt, y_sample, new_state_hgrn, new_state_rwkv)


_drawn_inputs = setup_inputs


def setup_inputs(seed=0):
    import zlib

    import numpy as np

    out = dict(_drawn_inputs(seed))
    spreads = {}
    factors = {'state_hgrn': 28.152,
     'state_rwkv': 8.0,
     'norm2': 19.83,
     'hgrn_norm': 96.619,
     'hy_conv_b': 44.566,
     'hy_b1': 7.819,
     'hy_freq1': 8.0,
     'hy_b2': 8.0,
     'hy_freq2': 39.194,
     'hy_delta': 140.293,
     'rw_ln_g': 115.023,
     'rw_ln_b': 98.278,
     'final_norm': 21.043,
     'rw_rk': 5.317}
    for name, (base, spread) in spreads.items():
        noise = np.random.default_rng([zlib.crc32(name.encode()), seed]).standard_normal(out[name].shape)
        drawn = base * np.exp(spread * noise) if base else spread * noise
        out[name] = jnp.asarray(drawn.astype(out[name].dtype))
    for name, factor in factors.items():
        out[name] = (out[name] * factor).astype(out[name].dtype)
    return out
```

```python
import math
from contextlib import ExitStack

import numpy as np
import concourse.bass as bass
from concourse import mybir

F32 = mybir.dt.float32
I32 = mybir.dt.int32
U32 = mybir.dt.uint32
ALU = mybir.AluOpType
ACT = mybir.ActivationFunctionType
AX = mybir.AxisListType.X

P = 128
D = 1024
KD = D // P
LP, LS = 128, 512
T = LP + LS
NCH = T // P
HALF = T // 2
SEG = [(0, LP), (LP, T)]
GRID_W = 64
W = 512
KW = W // P
DK = 128
HEADS_A = 4
HD = 64
BANDS = 16
EMB = 1 + 2 * BANDS
FFN = 64
A_TILES, B_TILES, C_TILES = 20, 12, 15
G_TILE0 = A_TILES + B_TILES + C_TILES
HEADS_P, NKEYS, TOPK = 8, 128, 16
SLOTS = HEADS_P * TOPK
EPS = 1e-6
GN_EPS = 64e-5
LEVELS = [64, 32, 16, 8, 4, 2, 1]
NL = len(LEVELS)

PARAMS = [("b_ada", 48), ("norm1", 8), ("norm2", 8), ("final", 8), ("lb", 8), ("hgrn_norm", 1),
          ("conv_w", 36), ("conv_b", 12), ("hy_bias", 4), ("mu", 15), ("w0", 8), ("a0", 8), ("kk", 4),
          ("ka", 4), ("rk", 4), ("ln_g", 4), ("ln_b", 4), ("b1", 1), ("freq1", 1), ("b2", 1), ("freq2", 1)]
PCOL, _n = {}, 0
for _name, _w in PARAMS:
    PCOL[_name] = _n
    _n += _w
NPAR = _n
CONSTS = [("ident", P), ("ones", P), ("blk64", P), ("tneg", NCH), ("iota", TOPK)]
CCOL, _n = {}, 0
for _name, _w in CONSTS:
    CCOL[_name] = _n
    _n += _w
NCONST = _n
RESET_W = NCH * 129


class Order:

    def __init__(self, sem):
        self.sem, self.n = sem, 0

    def link(self, eng, ins):
        ins.then_inc(self.sem, 1)
        self.n += 1
        eng.wait_ge(self.sem, self.n)


class Kern:

    def sem(self, name):
        self.taken.append(self.nc.alloc_semaphore(name))
        return self.taken[-1]

    def end_stage(self):
        self.nc.clear_and_free_semaphores(self.taken)
        self.nc.all_engine_barrier()
        self.taken = []


def bc(ap, shape):
    return ap.broadcast_to(shape)


def load_stage(nc, K, A):
    CH = 8
    CW = 6 * D // CH
    CP = CW // 2
    with ExitStack() as ctx:
        wt = ctx.enter_context(nc.sbuf_tensor("ada_w", [P, 3, KD * CW], F32))
        cT = ctx.enter_context(nc.sbuf_tensor("ada_c", [P, KD * 2], F32))
        sc = ctx.enter_context(nc.sbuf_tensor("ada_silu", [P, KD * 2], F32))
        rows = ctx.enter_context(nc.sbuf_tensor("ada_rows", [2, 6 * D], F32))
        ps_r = ctx.enter_context(nc.psum_tensor("ada_psr", [2, 4, 512], F32))
        ps = ctx.enter_context(nc.psum_tensor("ada_ps", [P, 512], F32))
        c_in, silu_done, ada_used, row_taken, turned, mod_done = (K.sem(x) for x in (
            "c_in", "silu_done", "ada_used", "row_taken", "turned", "mod_done"))
        w_in = [K.sem(f"ada_in{i}") for i in range(3)]
        params_in = K.sem("params_in")
        with nc.Block() as block:
            @block.sync
            def _(sp):
                sp.dma_start(cT[:], A["c"]).then_inc(c_in, 16)
                for i in range(CH):
                    if i == 3:
                        sp.dma_start(K.par[:], A["params"]).then_inc(params_in, 16)
                        sp.dma_start(K.con[:], A["consts"]).then_inc(params_in, 16)
                    if i >= 3:
                        sp.wait_ge(ada_used, 2 * (i - 2))
                    sp.dma_start(wt[:, i % 3, :], A["w_ada"][i]).then_inc(w_in[i % 3], 16)
                sp.wait_ge(params_in, 32)

            @block.scalar
            def _(act):
                act.wait_ge(c_in, 16)
                nc.scalar.activation(sc[:], cT[:], ACT.Silu).then_inc(silu_done, 1)
                for n in range(2 * CH):
                    act.wait_ge(ada_used, n + 1)
                    nc.scalar.activation(rows[:, n * CP:(n + 1) * CP], ps_r[:, n % 4, 0:CP],
                                         ACT.Copy).then_inc(row_taken, 1)

            @block.tensor
            def _(pe):
                pe.wait_ge(silu_done, 1)
                for n in range(2 * CH):
                    i = n // 2
                    if n % 2 == 0:
                        pe.wait_ge(w_in[i % 3], 16 * (i // 3 + 1))
                    if n >= 4:
                        pe.wait_ge(row_taken, n - 3)
                    for k in range(KD):
                        o = k * CW + (n % 2) * CP
                        last = nc.tensor.matmul(ps_r[:, n % 4, 0:CP], sc[:, 2 * k:2 * k + 2], wt[:, i % 3, o:o + CP],
                                                start=(k == 0), stop=(k == KD - 1))
                    last.then_inc(ada_used, 1)
                pe.wait_ge(params_in, 32)
                pe.wait_ge(row_taken, 2 * CH)
                for m in range(48):
                    last = nc.tensor.transpose(ps[:, 2 * m:2 * m + 2], rows[:, m * P:(m + 1) * P], K.ident[0:2, 0:2])
                last.then_inc(turned, 1)

            @block.vector
            def _(dve):
                dve.wait_ge(turned, 1)
                dve.wait_ge(params_in, 32)
                b = K.par[:, PCOL["b_ada"]:PCOL["b_ada"] + 48]
                K.dve.link(dve, nc.vector.tensor_tensor(K.mod[:], ps[:, 0:96].rearrange("p (m s) -> p m s", s=2),
                                                        bc(b.unsqueeze(2), [P, 48, 2]), ALU.add))
                for n, part, name in ((0, 1, "norm1"), (1, 4, "norm2")):
                    g = K.par[:, PCOL[name]:PCOL[name] + KD]
                    K.dve.link(dve, nc.vector.scalar_tensor_tensor(
                        out=K.gain[:, n], in0=K.mod[:, part * KD:(part + 1) * KD, :], scalar=1.0,
                        in1=bc(g.unsqueeze(2), [P, KD, 2]), op0=ALU.add, op1=ALU.mult))
                lg = K.par[:, PCOL["lb"]:PCOL["lb"] + 8]
                K.dve.link(dve, nc.vector.tensor_tensor(K.lb[:, 0], lg, lg, ALU.subtract))
                nc.vector.memset(K.lb[:, 2], 0.0).then_inc(mod_done, 1)

            @block.gpsimd
            def _(pool):
                pass
        sm = [K.sem(f"lb_step{i}") for i in range(2)]
        with nc.Block() as block:
            @block.scalar
            def _(act):
                nc.scalar.activation(K.lb[:, 1], K.lb[:, 0], ACT.Exp).then_inc(sm[0], 1)

            @block.vector
            def _(dve):
                dve.wait_ge(sm[0], 1)
                K.dve.link(dve, nc.vector.reciprocal(K.lb[:, 0], K.lb[:, 1]))
                K.dve.link(dve, nc.vector.tensor_tensor(K.lb[:, 1], K.lb[:, 1], K.lb[:, 0], ALU.mult))
                K.dve.link(dve, nc.vector.tensor_tensor(K.lb[:, 0], K.lb[:, 1], K.lb[:, 1], ALU.subtract))
                K.dve.link(dve, nc.vector.tensor_scalar(K.lb[:, 1], K.lb[:, 0], -1.0, 1.0, ALU.mult, ALU.add))


def norm_stage(nc, K, A, n, src, dst, name, load=None):
    with ExitStack() as ctx:
        sq = ctx.enter_context(nc.sbuf_tensor(name + "_sq", [P, KD, T], F32))
        rstd = ctx.enter_context(nc.sbuf_tensor(name + "_rstd", [P, T], F32))
        ps = ctx.enter_context(nc.psum_tensor(name + "_ps", [P, 2, 512], F32))
        x_in, sq_done, sum_done, ms_done, root_done = (K.sem(name + x) for x in (
            "_x_in", "_sq_done", "_sum_done", "_ms_done", "_root_done"))
        with nc.Block() as block:
            @block.sync
            def _(sp):
                if load is not None:
                    sp.dma_start(src[:], load).then_inc(x_in, 16)

            @block.scalar
            def _(act):
                if load is not None:
                    act.wait_ge(x_in, 16)
                for k in range(KD):
                    nc.scalar.activation(sq[:, k], src[:, k], ACT.Square).then_inc(sq_done, 1)
                act.wait_ge(ms_done, 1)
                nc.scalar.activation(rstd[:], rstd[:], ACT.Sqrt).then_inc(root_done, 1)

            @block.tensor
            def _(pe):
                for k in range(KD):
                    pe.wait_ge(sq_done, k + 1)
                    for c in range(2):
                        last = nc.tensor.matmul(ps[:, c, 0:HALF], K.ones, sq[:, k, c * HALF:(c + 1) * HALF],
                                                start=(k == 0), stop=(k == KD - 1))
                last.then_inc(sum_done, 1)

            @block.vector
            def _(dve):
                dve.wait_ge(sum_done, 1)
                nc.vector.tensor_scalar(rstd[:].rearrange("p (c n) -> p c n", c=2), ps[:, :, 0:HALF],
                                        1.0 / D, EPS, ALU.mult, ALU.add).then_inc(ms_done, 1)
                dve.wait_ge(root_done, 1)
                K.dve.link(dve, nc.vector.reciprocal(rstd[:], rstd[:]))
                for k in range(KD):
                    ins = nc.vector.tensor_tensor(dst[:, k], src[:, k], rstd[:], ALU.mult)
                K.dve.link(dve, ins)
                for k in range(KD):
                    if n == 2:
                        g = K.par[:, PCOL["final"] + k:PCOL["final"] + k + 1]
                        ins = nc.vector.tensor_scalar(dst[:, k], dst[:, k], g, None, ALU.mult)
                        continue
                    for s, (a, b) in enumerate(SEG):
                        shift = K.mod[:, (0, 3)[n] * KD + k, s:s + 1]
                        ins = nc.vector.tensor_scalar(dst[:, k, a:b], dst[:, k, a:b], K.gain[:, n, k, s:s + 1],
                                                      shift, ALU.mult, ALU.add)
                K.dve.link(dve, ins)


class Projection:
    RING, BANKS = 4, 2

    def __init__(self, nc, ctx, K, A, name, tiles, array="w_in"):
        self.array = array
        self.nc, self.K, self.A, self.tiles = nc, K, A, tiles
        self.w = ctx.enter_context(nc.sbuf_tensor(name + "_w", [P, self.RING, KD, P], F32))
        self.ps = ctx.enter_context(nc.psum_tensor(name + "_ps", [P, self.BANKS, 2, 512], F32))
        self.w_in = [K.sem(f"{name}_w_in{i}") for i in range(self.RING)]
        self.proj_done = K.sem(name + "_proj_done")
        self.proj_taken = K.sem(name + "_proj_taken")

    def load(self, sp, i):
        if i >= self.RING:
            sp.wait_ge(self.proj_done, i - self.RING + 1)
        sp.dma_start(self.w[:, i % self.RING], self.A[self.array][self.tiles[i]]).then_inc(
            self.w_in[i % self.RING], 16)

    def mm(self, pe, i):
        nc = self.nc
        pe.wait_ge(self.w_in[i % self.RING], 16 * (i // self.RING + 1))
        if i >= self.BANKS:
            pe.wait_ge(self.proj_taken, i - self.BANKS + 1)
        for k in range(KD):
            for c in range(2):
                last = nc.tensor.matmul(self.ps[:, i % self.BANKS, c, 0:HALF], self.w[:, i % self.RING, k],
                                        self.K.hT[:, k, c * HALF:(c + 1) * HALF],
                                        start=(k == 0), stop=(k == KD - 1))
        last.then_inc(self.proj_done, 1)

    def out(self, i):
        return self.ps[:, i % self.BANKS, :, 0:HALF]


def halves(ap):
    return ap.rearrange("p (c n) -> p c n", c=2)


def hgrn_stage(nc, K, A):
    with ExitStack() as ctx:
        def sb(name, shape):
            return ctx.enter_context(nc.sbuf_tensor("hg_" + name, shape, F32))

        def sem(name):
            return K.sem("hg_" + name)
        qT = sb("q", [P, 4, T])
        fT = sb("f", [P, 8, T])
        gT = sb("g", [P, 4, T])
        i_tok = sb("i", [P, NCH, W])
        with ExitStack() as pctx:
            pr = Projection(nc, pctx, K, A, "hg", [t for t in range(A_TILES) if not 12 <= t < 16])
            w_i = pctx.enter_context(nc.sbuf_tensor("hg_wi", [P, KD, W], F32))
            ps_i = pctx.enter_context(nc.psum_tensor("hg_psi", [P, 2, W], F32))
            wi_in, i_done, i_taken = sem("wi_in"), sem("i_done"), sem("i_taken")
            NT = len(pr.tiles)
            with nc.Block() as block:
                @block.sync
                def _(sp):
                    for i in range(NT):
                        pr.load(sp, i)
                        if i == 3:
                            sp.dma_start(w_i[:], A["w_i"]).then_inc(wi_in, 16)

                @block.tensor
                def _(pe):
                    for i in range(NT):
                        pr.mm(pe, i)
                    pe.wait_ge(wi_in, 16)
                    for c in range(NCH):
                        if c >= 2:
                            pe.wait_ge(i_taken, c - 1)
                        for k in range(KD):
                            last = nc.tensor.matmul(ps_i[:, c % 2], K.hT[:, k, c * P:(c + 1) * P], w_i[:, k],
                                                    start=(k == 0), stop=(k == KD - 1))
                        last.then_inc(i_done, 1)

                @block.scalar
                def _(act):
                    for i in range(NT):
                        act.wait_ge(pr.proj_done, i + 1)
                        if i < 4:
                            dst, fn = qT[:, i], ACT.Silu
                        elif i < 12:
                            dst, fn = fT[:, i - 4], ACT.Sigmoid
                        else:
                            dst, fn = gT[:, i - 12], ACT.Silu
                        nc.scalar.activation(halves(dst), pr.out(i), fn).then_inc(pr.proj_taken, 1)

                @block.vector
                def _(dve):
                    for c in range(NCH):
                        dve.wait_ge(i_done, c + 1)
                        nc.vector.tensor_copy(i_tok[:, c], ps_i[:, c % 2]).then_inc(i_taken, 1)

        NE = NL + 2
        mask = sb("mask", [P, 2, NL + 1, P])
        reset = sb("reset", [P, RESET_W])
        lf = sb("lf", [P, RESET_W])
        cum = sb("cum", [P, RESET_W])
        kT = sb("k", [P, 2, NCH, P])
        E = sb("E", [P, 2, NE, NCH, P])
        dec = sb("dec", [P, 2, NCH])
        att = sb("att", [P, 2, NL + 1, P])
        khat = sb("khat", [P, 2, NCH, P])
        S = sb("S", [P, 3, DK])
        S_in = sb("S_in", [P, 8, DK])
        ps_s = ctx.enter_context(nc.psum_tensor("hg_pss", [P, 2, NL + 1, P], F32))
        ps_t = ctx.enter_context(nc.psum_tensor("hg_pst", [P, 1024], F32))
        ps_o = ctx.enter_context(nc.psum_tensor("hg_pso", [P, 512], F32))
        ps_d = ctx.enter_context(nc.psum_tensor("hg_psd", [P, 512], F32))
        (const_in, s_in, logs, dec_sub, exp_done, x_ready, s_done, att_ready, tr_done, khat_ready, o_done, o_taken,
         ds_done, st_ready, st_out, f_ready, cum_done) = (sem(x) for x in (
             "const_in", "s_in", "logs", "dec_sub", "exp_done", "x_ready", "s_done", "att_ready", "tr_done",
             "khat_ready", "o_done", "o_taken", "ds_done", "st_ready", "st_out", "f_ready", "cum_done"))
        cumv = cum[:].rearrange("p (c t) -> p c t", t=129)
        lfv = lf[:].rearrange("p (c t) -> p c t", t=129)

        def order(d):
            return [0] + ([1, 2, 3, 4] if d == 0 else [4, 3, 2, 1])

        steps = [(g, g // 4, g % 4, c) for g in range(8) for c in order(g // 4)]
        with nc.Block() as block:
            @block.sync
            def _(sp):
                sp.dma_start(mask[:], A["hg_mask"]).then_inc(const_in, 16)
                sp.dma_start(reset[:], A["reset"]).then_inc(const_in, 16)
                sp.dma_start(S_in[:], A["state_hgrn"]).then_inc(s_in, 16)
                for g in range(8):
                    sp.wait_ge(st_ready, 4 * g + 1)
                    sp.dma_start(A["out_hgrn"][g], S[:, 0]).then_inc(st_out, 16)
                sp.wait_ge(st_out, 16 * 8)

            @block.scalar
            def _(act):
                for g in range(8):
                    act.wait_ge(f_ready, g + 1)
                    if g >= 1:
                        act.wait_ge(cum_done, g)
                    nc.scalar.activation(lfv[:, :, 1:129], fT[:, g].rearrange("p (c t) -> p c t", t=P),
                                         ACT.Ln).then_inc(logs, 1)
                    act.wait_ge(dec_sub, g + 1)
                    nc.scalar.activation(dec[:, g % 2], cumv[:, :, 128], ACT.Exp)
                    nc.scalar.activation(E[:, g % 2], E[:, g % 2], ACT.Exp).then_inc(exp_done, 1)
                    act.wait_ge(tr_done, g + 1)
                    nc.scalar.activation(khat[:, g % 2], ps_t[:, 0:T].rearrange("p (c t) -> p c t", t=P),
                                         ACT.Copy).then_inc(khat_ready, 1)

            @block.tensor
            def _(pe):
                def scores(n):
                    g, d, h, c = steps[n]
                    b = g % 2
                    if n % NCH == 0:
                        pe.wait_ge(x_ready, g + 1)
                        if g >= 1:
                            pe.wait_ge(khat_ready, g)
                        for cc in range(NCH):
                            last = nc.tensor.transpose(ps_t[:, cc * P:(cc + 1) * P], E[:, b, NL + 1, cc], K.ident)
                        last.then_inc(tr_done, 1)
                    if n >= 2:
                        pe.wait_ge(att_ready, n - 1)
                    for v in range(NL):
                        nc.tensor.matmul(ps_s[:, n % 2, v], E[:, b, v, c], E[:, b, v, c], start=True, stop=True)
                    nc.tensor.matmul(ps_s[:, n % 2, NL], kT[:, b, c], qT[:, h, c * P:(c + 1) * P],
                                     start=True, stop=True).then_inc(s_done, 1)

                def outputs(n):
                    g, d, h, c = steps[n]
                    b = g % 2
                    iv = i_tok[:, c, h * P:(h + 1) * P]
                    pe.wait_ge(khat_ready, g + 1)
                    if n % NCH != NCH - 1:
                        if n >= 1:
                            pe.wait_ge(st_ready, 4 * g + n % NCH)
                        nc.tensor.matmul(ps_d[:, 0:P], khat[:, b, c], iv, start=True, stop=True).then_inc(ds_done, 1)
                    pe.wait_ge(att_ready, n + 1)
                    if n >= 1:
                        pe.wait_ge(o_taken, n)
                    first = n % NCH == 0
                    for v in range(NL + 1):
                        last = nc.tensor.matmul(ps_o[:, 0:P], iv, att[:, n % 2, v], start=(v == 0),
                                                stop=(v == NL and first))
                    if not first:
                        k = n % NCH
                        if k == 1:
                            pe.wait_ge(s_in, 16)
                            src = S_in[:, g]
                        else:
                            pe.wait_ge(st_ready, 4 * g + k)
                            src = S[:, 1 + k % 2]
                        last = nc.tensor.matmul(ps_o[:, 0:P], src, E[:, b, NL, c], start=False, stop=True)
                    last.then_inc(o_done, 1)

                scores(0)
                for n in range(len(steps)):
                    if n + 1 < len(steps) and (n + 1) % NCH:
                        scores(n + 1)
                    outputs(n)
                    if n + 1 < len(steps) and (n + 1) % NCH == 0:
                        scores(n + 1)

            @block.vector
            def _(dve):
                link = lambda ins: K.dve.link(dve, ins)
                nc.vector.memset(lfv[:, :, 0:1], 0.0)
                dve.wait_ge(const_in, 32)

                def prepare(g):
                    d, h, b = g // 4, g % 4, g % 2
                    inc, exc = cumv[:, :, 1:129], cumv[:, :, 0:128]
                    q = qT[:, h].rearrange("p (c t) -> p c t", t=P)
                    lo, hi = (kT[:, b], q) if d == 0 else (q, kT[:, b])

                    def gates():
                        link(nc.vector.tensor_scalar(fT[:, g], fT[:, g], K.lb[:, 1, g:g + 1], K.lb[:, 0, g:g + 1],
                                                     ALU.mult, ALU.add))
                        if g >= 2:
                            dve.wait_ge(o_done, NCH * (g - 1))
                        link(nc.vector.tensor_scalar(kT[:, b], fT[:, g].rearrange("p (c t) -> p c t", t=P), -1.0,
                                                     1.0, ALU.mult, ALU.add))
                        nc.vector.tensor_scalar(fT[:, g], fT[:, g], 2.0 ** -63, None, ALU.max).then_inc(f_ready, 1)

                    def sums():
                        dve.wait_ge(logs, g + 1)
                        if g >= 1:
                            dve.wait_ge(exp_done, g)
                        nc.vector.tensor_tensor_scan(cum[:], reset[:], lf[:], 0.0, ALU.mult, ALU.add).then_inc(
                            cum_done, 1)
                        dve.wait_ge(cum_done, g + 1)

                    def level(v):
                        w = LEVELS[v]
                        out = E[:, b, v].rearrange("p c (n t) -> p c n t", t=2 * w)
                        at = (inc if d == 0 else exc).rearrange("p c (n t) -> p c n t", t=2 * w)
                        mid = exc.rearrange("p c (n t) -> p c n t", t=2 * w)[:, :, :, w:w + 1]
                        mid = bc(mid, [P, NCH, 64 // w, w])
                        L, R = slice(0, w), slice(w, 2 * w)
                        nc.vector.tensor_tensor(out[:, :, :, L], mid, at[:, :, :, L], ALU.subtract)
                        nc.vector.tensor_tensor(out[:, :, :, R], at[:, :, :, R], mid, ALU.subtract)

                    def to_ends():
                        zero = bc(cumv[:, :, 0:1], [P, NCH, P])
                        end = bc(cumv[:, :, 128:129], [P, NCH, P])
                        if d == 0:
                            nc.vector.tensor_tensor(E[:, b, NL], inc, zero, ALU.subtract)
                            nc.vector.tensor_tensor(E[:, b, NL + 1], end, inc, ALU.subtract).then_inc(dec_sub, 1)
                        else:
                            nc.vector.tensor_tensor(E[:, b, NL], end, exc, ALU.subtract)
                            nc.vector.tensor_tensor(E[:, b, NL + 1], exc, zero, ALU.subtract).then_inc(dec_sub, 1)

                    def scale(v):
                        w = LEVELS[v]
                        dve.wait_ge(exp_done, g + 1)
                        x = E[:, b, v].rearrange("p c (n t) -> p c n t", t=2 * w)
                        for src, s in ((lo, slice(0, w)), (hi, slice(w, 2 * w))):
                            y = src.rearrange("p c (n t) -> p c n t", t=2 * w)[:, :, :, s]
                            nc.vector.tensor_tensor(x[:, :, :, s], x[:, :, :, s], y, ALU.mult)

                    def scale_ends():
                        nc.vector.tensor_tensor(E[:, b, NL], E[:, b, NL], q, ALU.mult)
                        nc.vector.tensor_tensor(E[:, b, NL + 1], E[:, b, NL + 1], kT[:, b], ALU.mult).then_inc(
                            x_ready, 1)
                    return [[gates], [sums] + [lambda v=v: level(v) for v in range(4)],
                            [lambda v=v: level(v) for v in range(4, NL)] + [to_ends],
                            [lambda v=v: scale(v) for v in range(4)],
                            [lambda v=v: scale(v) for v in range(4, NL)] + [scale_ends]]

                def chunk(n, meanwhile):
                    g, d, h, c = steps[n]
                    dve.wait_ge(s_done, n + 1)
                    if n >= 2:
                        dve.wait_ge(o_done, n - 1)
                    nc.vector.tensor_tensor(att[:, n % 2], ps_s[:, n % 2], mask[:, d], ALU.mult).then_inc(att_ready, 1)
                    k = n % NCH
                    if k != NCH - 1:
                        dve.wait_ge(ds_done, 4 * g + k + 1)
                        if k == 0:
                            if g >= 1:
                                dve.wait_ge(st_out, 16 * g)
                            nc.vector.tensor_copy(S[:, 0], ps_d[:, 0:P]).then_inc(st_ready, 1)
                        else:
                            src = S_in[:, g] if k == 1 else S[:, 1 + k % 2]
                            if k == 1:
                                dve.wait_ge(s_in, 16)
                            else:
                                dve.wait_ge(st_ready, 4 * g + k)
                            if k == 3:
                                dve.wait_ge(o_done, n - 1)
                            nc.vector.scalar_tensor_tensor(
                                out=S[:, 1 + (k + 1) % 2], in0=src, scalar=dec[:, g % 2, c:c + 1], in1=ps_d[:, 0:P],
                                op0=ALU.mult, op1=ALU.add).then_inc(st_ready, 1)
                    for step in meanwhile:
                        step()
                    dve.wait_ge(o_done, n + 1)
                    o = K.yT[0][:, h, c * P:(c + 1) * P]
                    if d == 0:
                        nc.vector.tensor_copy(o, ps_o[:, 0:P]).then_inc(o_taken, 1)
                    else:
                        nc.vector.tensor_tensor(o, o, ps_o[:, 0:P], ALU.add).then_inc(o_taken, 1)

                for steps_of in prepare(0):
                    for step in steps_of:
                        step()
                for g in range(8):
                    ahead = prepare(g + 1) if g < 7 else [[]] * NCH
                    for k in range(NCH):
                        chunk(NCH * g + k, ahead[k])

        head_norm_stage(nc, K, K.yT[0], K.ones, 1.0 / DK, "hgn", gT, E[:, 0].rearrange("p e c t -> p (e c t)"),
                        ps_t[:].rearrange("p (c n) -> p c n", c=2))


def head_norm_stage(nc, K, y, sums, scale, name, gate, tmp, ps):
    sq = tmp[:, 0:4 * T].rearrange("p (h t) -> p h t", h=4)
    sq_done, sum_done, ms_done, root_done = (K.sem(name + x) for x in (
        "_sq_done", "_sum_done", "_ms_done", "_root_done"))
    rstd = sq
    if True:
        with nc.Block() as block:
            @block.scalar
            def _(act):
                for h in range(4):
                    nc.scalar.activation(sq[:, h], y[:, h], ACT.Square).then_inc(sq_done, 1)
                for h in range(4):
                    act.wait_ge(ms_done, h + 1)
                    nc.scalar.activation(rstd[:, h], rstd[:, h], ACT.Sqrt).then_inc(root_done, 1)

            @block.tensor
            def _(pe):
                for h in range(4):
                    pe.wait_ge(sq_done, h + 1)
                    if h >= 1:
                        pe.wait_ge(ms_done, h)
                    for c in range(2):
                        last = nc.tensor.matmul(ps[:, c, 0:HALF], sums, sq[:, h, c * HALF:(c + 1) * HALF],
                                                start=True, stop=True)
                    last.then_inc(sum_done, 1)

            @block.vector
            def _(dve):
                for h in range(4):
                    dve.wait_ge(sum_done, h + 1)
                    nc.vector.tensor_scalar(halves(rstd[:, h]), ps[:, :, 0:HALF], scale, EPS, ALU.mult,
                                            ALU.add).then_inc(ms_done, 1)
                for h in range(4):
                    dve.wait_ge(root_done, h + 1)
                    K.dve.link(dve, nc.vector.reciprocal(rstd[:, h], rstd[:, h]))
                    K.dve.link(dve, nc.vector.scalar_tensor_tensor(
                        out=y[:, h], in0=y[:, h], scalar=K.par[:, PCOL["hgrn_norm"]:PCOL["hgrn_norm"] + 1],
                        in1=rstd[:, h], op0=ALU.mult, op1=ALU.mult))
                    K.dve.link(dve, nc.vector.tensor_tensor(y[:, h], y[:, h], gate[:, h], ALU.mult))


def tok0(c):
    return 1 if c == 0 else 2 + P * c


PADW = T + 3
SEQ_OF = [[0], [1, 2, 3, 4]]


def sin_steps(nc, K, dve, x, n, bias, freq):
    magic, c1 = 1.5 * 2.0 ** 23, 6.28125
    c2 = 2.0 * math.pi - c1
    pi = 3.1415925
    link = lambda ins: K.dve.link(dve, ins)
    link(nc.vector.tensor_scalar(x, x, bias, freq, ALU.add, ALU.mult))
    link(nc.vector.tensor_scalar(n, x, 1.0 / (2.0 * math.pi), magic, ALU.mult, ALU.add))
    link(nc.vector.tensor_scalar(n, n, -magic, None, ALU.add))
    link(nc.vector.scalar_tensor_tensor(out=x, in0=n, scalar=-c1, in1=x, op0=ALU.mult, op1=ALU.add))
    link(nc.vector.scalar_tensor_tensor(out=x, in0=n, scalar=-c2, in1=x, op0=ALU.mult, op1=ALU.add))
    return nc.vector.tensor_scalar(x, x, pi, -pi, ALU.min, ALU.max)


def hyena_stage(nc, K, A):
    with ExitStack() as ctx:
        def sb(name, shape):
            return ctx.enter_context(nc.sbuf_tensor("hy_" + name, shape, F32))

        def sem(name):
            return K.sem("hy_" + name)
        par = lambda name, i=0, rows=P: K.par[0:rows, PCOL[name] + i:PCOL[name] + i + 1]
        u = sb("u", [P, 12, PADW])
        z_tok = sb("z_tok", [P, NCH, W])
        with ExitStack() as c1:
            pr = Projection(nc, c1, K, A, "hy", list(range(A_TILES, A_TILES + 12)))
            R = c1.enter_context(nc.sbuf_tensor("hy_raw", [P, 2, PADW], F32))
            ps_t = c1.enter_context(nc.psum_tensor("hy_pst", [P, 2, 512], F32))
            zeroed, raw, conv, z_done, zt_done, zt_taken = (sem(x) for x in (
                "zeroed", "raw", "conv", "z_done", "zt_done", "zt_taken"))
            with nc.Block() as block:
                @block.sync
                def _(sp):
                    for i in range(12):
                        pr.load(sp, i)

                @block.tensor
                def _(pe):
                    for i in range(12):
                        pr.mm(pe, i)
                    pe.wait_ge(z_done, 1)
                    for c in range(NCH):
                        if c >= 2:
                            pe.wait_ge(zt_taken, c - 1)
                        for j in range(KW):
                            last = nc.tensor.transpose(ps_t[:, c % 2, j * P:(j + 1) * P],
                                                       u[:, 8 + j, tok0(c):tok0(c) + P], K.ident)
                        last.then_inc(zt_done, 1)

                @block.scalar
                def _(act):
                    act.wait_ge(zeroed, 1)
                    for i in range(12):
                        act.wait_ge(pr.proj_done, i + 1)
                        if i >= 2:
                            act.wait_ge(conv, i - 1)
                        b, o = i % 2, pr.out(i)
                        nc.scalar.activation(R[:, b, 1:1 + LP], o[:, 0, 0:LP], ACT.Copy)
                        nc.scalar.activation(R[:, b, 2 + LP:2 + HALF], o[:, 0, LP:HALF], ACT.Copy)
                        nc.scalar.activation(R[:, b, 2 + HALF:2 + T], o[:, 1], ACT.Copy).then_inc(pr.proj_taken, 1)
                    for c in range(NCH):
                        act.wait_ge(zt_done, c + 1)
                        nc.scalar.activation(z_tok[:, c], ps_t[:, c % 2], ACT.Copy).then_inc(zt_taken, 1)

                @block.vector
                def _(dve):
                    link = lambda ins: K.dve.link(dve, ins)
                    nc.vector.memset(R[:], 0.0).then_inc(zeroed, 1)
                    for i in range(12):
                        dve.wait_ge(pr.proj_taken, i + 1)
                        b, uo = i % 2, u[:, i, 1:PADW - 1]
                        link(nc.vector.tensor_scalar(uo, R[:, b, 1:PADW - 1], par("conv_w", 12 + i), par("conv_b", i),
                                                     ALU.mult, ALU.add))
                        link(nc.vector.scalar_tensor_tensor(out=uo, in0=R[:, b, 0:PADW - 2], scalar=par("conv_w", i),
                                                            in1=uo, op0=ALU.mult, op1=ALU.add))
                        nc.vector.scalar_tensor_tensor(out=uo, in0=R[:, b, 2:PADW], scalar=par("conv_w", 24 + i),
                                                       in1=uo, op0=ALU.mult, op1=ALU.add).then_inc(conv, 1)
                    dve.wait_ge(conv, 12)
                    nc.vector.tensor_tensor(u[:, 8:12, 1:PADW - 1], u[:, 8:12, 1:PADW - 1], u[:, 4:8, 1:PADW - 1],
                                            ALU.mult).then_inc(z_done, 1)
        fwd = sb("fwd", [P, 4, 2, LS])
        inv = sb("inv", [P, 4, 2, LS])
        fwd_p = sb("fwd_p", [P, 2, LP])
        inv_p = sb("inv_p", [P, 2, LP])
        H = sb("H", [P, NCH, 2, W])
        G = sb("G", [P, NCH, 2, W])
        inorm = sb("inorm", [P, 2, W])
        tables_in = sem("tables_in")
        with ExitStack() as c1:
            def tb(name, shape):
                return c1.enter_context(nc.sbuf_tensor("hy_" + name, shape, F32))
            zf, w1, w2 = tb("zf", [EMB, T]), tb("w1", [EMB, FFN]), tb("w2", [FFN, FFN])
            w3, dl = tb("w3", [FFN, 2 * W]), tb("dl", [P, W])
            f1, f2, turns = tb("f1", [FFN, T]), tb("f2", [FFN, T]), tb("turns", [FFN, T])
            Et = tb("Et", [P, 2, W])
            ps_f = c1.enter_context(nc.psum_tensor("hy_psf", [P, 2, 512], F32))
            ps_h = c1.enter_context(nc.psum_tensor("hy_psh", [P, 2, 2, 512], F32))
            ps_n = c1.enter_context(nc.psum_tensor("hy_psn", [P, 2, 512], F32))
            f_in, ffn_mm, ffn_arg, ffn_act, dabs, env, hf_mm, hf_taken, abs_done, sums, h_done, zrow = (
                sem(x) for x in ("f_in", "ffn_mm", "ffn_arg", "ffn_act", "dabs", "env", "hf_mm", "hf_taken",
                                 "abs_done", "sums", "h_done", "zrow"))
            with nc.Block() as block:
                @block.sync
                def _(sp):
                    for t, n in ((zf, "zf"), (w1, "hy_w1"), (w2, "hy_w2"), (w3, "hy_w3"), (dl, "delta")):
                        sp.dma_start(t[:], A[n]).then_inc(f_in, 16)
                    for t, n in ((fwd, "fwd"), (inv, "inv"), (fwd_p, "fwd_p"), (inv_p, "inv_p")):
                        sp.dma_start(t[:], A[n]).then_inc(tables_in, 16)
                    sp.wait_ge(tables_in, 64)

                @block.tensor
                def _(pe):
                    pe.wait_ge(f_in, 80)
                    for layer, (w, x) in enumerate(((w1, zf), (w2, f1))):
                        if layer:
                            pe.wait_ge(ffn_act, 1)
                        for c in range(2):
                            last = nc.tensor.matmul(ps_f[0:FFN, c, 0:HALF], w[:], x[:, c * HALF:(c + 1) * HALF],
                                                    start=True, stop=True)
                        last.then_inc(ffn_mm, 1)
                    pe.wait_ge(ffn_act, 2)
                    for c in range(NCH):
                        if c >= 2:
                            pe.wait_ge(hf_taken, c - 1)
                        for s in range(2):
                            last = nc.tensor.matmul(ps_h[:, c % 2, s], f2[:, c * P:(c + 1) * P],
                                                    w3[:, s * W:(s + 1) * W], start=True, stop=True)
                        last.then_inc(hf_mm, 1)
                    for q, chunks in enumerate(SEQ_OF):
                        for c in chunks:
                            pe.wait_ge(abs_done, c + 1)
                            for s in range(2):
                                last = nc.tensor.matmul(ps_n[:, q], K.ones, G[:, c, s],
                                                        start=(c == chunks[0] and s == 0),
                                                        stop=(c == chunks[-1] and s == 1))
                        last.then_inc(sums, 1)

                @block.scalar
                def _(act):
                    act.wait_ge(f_in, 80)
                    nc.scalar.activation(dl[:], dl[:], ACT.Abs).then_inc(dabs, 1)
                    for layer, f in enumerate((f1, f2)):
                        act.wait_ge(ffn_arg, layer + 1)
                        nc.scalar.activation(f[:], f[:], ACT.Sin).then_inc(ffn_act, 1)
                    act.wait_ge(dabs, 1)
                    for c in range(NCH):
                        if c >= 2:
                            act.wait_ge(hf_taken, c - 1)
                        tn = K.con[:, CCOL["tneg"] + c:CCOL["tneg"] + c + 1]
                        nc.scalar.activation(Et[:, c % 2], dl[:], ACT.Exp, scale=tn).then_inc(env, 1)
                    for c in range(NCH):
                        act.wait_ge(zrow, c + 1)
                        nc.scalar.activation(G[:, c], H[:, c], ACT.Abs).then_inc(abs_done, 1)

                @block.vector
                def _(dve):
                    link = lambda ins: K.dve.link(dve, ins)
                    for layer, f in enumerate((f1, f2)):
                        dve.wait_ge(ffn_mm, layer + 1)
                        link(nc.vector.tensor_copy(halves(f[:]), ps_f[0:FFN, :, 0:HALF]))
                        sin_steps(nc, K, dve, f[:], turns[:], par("b1" if layer == 0 else "b2", 0, FFN),
                                  par("freq1" if layer == 0 else "freq2", 0, FFN)).then_inc(ffn_arg, 1)
                    for c in range(NCH):
                        dve.wait_ge(hf_mm, c + 1)
                        dve.wait_ge(env, c + 1)
                        ins = nc.vector.tensor_tensor(H[:, c], ps_h[:, c % 2],
                                                      bc(Et[:, c % 2].unsqueeze(1), [P, 2, W]), ALU.mult)
                        ins.then_inc(hf_taken, 1)
                        dve.wait_ge(hf_taken, c + 1)
                        if c < 2:
                            nc.vector.memset(H[0:1, c, 1, :], 0.0).then_inc(zrow, 1)
                        else:
                            dve.sem_inc(zrow, 1)
                    dve.wait_ge(abs_done, NCH)
                    link(nc.vector.tensor_tensor(H[:, :, 0], H[:, :, 0], H[:, :, 1], ALU.add))
                    link(nc.vector.scalar_tensor_tensor(out=H[:, :, 1], in0=H[:, :, 1], scalar=2.0, in1=H[:, :, 0],
                                                        op0=ALU.mult, op1=ALU.subtract))
                    dve.wait_ge(sums, 2)
                    for q, L in enumerate((LP, LS)):
                        link(nc.vector.tensor_scalar(inorm[:, q], ps_n[:, q], float(L), None, ALU.mult))
                    link(nc.vector.reciprocal(inorm[:], inorm[:]))
        Z = sb("Z", [P, NCH, 2, W])
        t1 = H
        with ExitStack() as c1:
            ps_k = c1.enter_context(nc.psum_tensor("hy_psk", [P, 2, 2, 512], F32))
            ps_z = c1.enter_context(nc.psum_tensor("hy_psz", [P, 2, 2, 512], F32))
            k_mm, k_taken, z_mm, z_taken, y_done, inv_mm, inv_taken, z_neg = (sem(x) for x in (
                "k_mm", "k_taken", "z_mm", "z_taken", "y_done", "inv_mm", "inv_taken", "z_neg"))
            tiles = [(q, f) for q in range(2) for f in SEQ_OF[q]]
            with nc.Block() as block:
                @block.tensor
                def _(pe):
                    for n, (q, f) in enumerate(tiles):
                        for ps, src, mm, taken in ((ps_k, None, k_mm, k_taken), (ps_z, z_tok, z_mm, z_taken)):
                            if n >= 2:
                                pe.wait_ge(taken, n - 1)
                            for s in range(2):
                                chunks = SEQ_OF[q]
                                for c in chunks:
                                    tab = (fwd_p[:, s, :] if q == 0 else
                                           fwd[:, c - 1, s, (f - 1) * P:f * P])
                                    rhs = H[:, c, s] if src is None else src[:, c]
                                    last = nc.tensor.matmul(ps[:, n % 2, s], tab, rhs, start=(c == chunks[0]),
                                                            stop=(c == chunks[-1]))
                            last.then_inc(mm, 1)
                    pe.wait_ge(y_done, 1)
                    n = 0
                    for j in range(KW):
                        for q in range(2):
                            if n >= 4:
                                pe.wait_ge(inv_taken, n - 3)
                            chunks = SEQ_OF[q]
                            L = LS if q else LP
                            for f in chunks:
                                for s in range(2):
                                    tab = inv_p[:, s] if q == 0 else inv[:, f - 1, s]
                                    last = nc.tensor.matmul(ps_k[:, (n // 2) % 2, n % 2, 0:L],
                                                            Z[:, f, s, j * P:(j + 1) * P], tab,
                                                            start=(f == chunks[0] and s == 0),
                                                            stop=(f == chunks[-1] and s == 1))
                            last.then_inc(inv_mm, 1)
                            n += 1

                @block.scalar
                def _(act):
                    for n, (q, f) in enumerate(tiles):
                        act.wait_ge(z_mm, n + 1)
                        nc.scalar.activation(Z[:, f], ps_z[:, n % 2], ACT.Copy).then_inc(z_taken, 1)

                @block.vector
                def _(dve):
                    link = lambda ins: K.dve.link(dve, ins)
                    for n, (q, f) in enumerate(tiles):
                        dve.wait_ge(k_mm, n + 1)
                        nc.vector.tensor_tensor(G[:, f], ps_k[:, n % 2],
                                                bc(inorm[:, q].unsqueeze(1), [P, 2, W]), ALU.mult).then_inc(k_taken, 1)
                    dve.wait_ge(z_taken, NCH)
                    dve.wait_ge(k_taken, NCH)
                    nc.vector.tensor_tensor(t1[:, :, 0], Z[:, :, 1], G[:, :, 1], ALU.mult)
                    link(nc.vector.tensor_tensor(t1[:, :, 1], Z[:, :, 0], G[:, :, 1], ALU.mult))
                    link(nc.vector.tensor_tensor(Z[:, :, 0], Z[:, :, 0], G[:, :, 0], ALU.mult))
                    link(nc.vector.tensor_tensor(Z[:, :, 1], Z[:, :, 1], G[:, :, 0], ALU.mult))
                    nc.vector.tensor_tensor(Z[:, :, 0], Z[:, :, 0], t1[:, :, 0], ALU.add)
                    nc.vector.tensor_tensor(Z[:, :, 1], Z[:, :, 1], t1[:, :, 1], ALU.subtract).then_inc(y_done, 1)
                    n = 0
                    for j in range(KW):
                        for q in range(2):
                            dve.wait_ge(inv_mm, n + 1)
                            a, b = SEG[q]
                            cols = slice(a + 1 + q, b + 1 + q)
                            y = K.yT[1][:, j, a:b]
                            nc.vector.scalar_tensor_tensor(
                                out=y, in0=u[:, 8 + j, cols], scalar=par("hy_bias", j),
                                in1=ps_k[:, (n // 2) % 2, n % 2, 0:b - a], op0=ALU.mult, op1=ALU.add).then_inc(inv_taken, 1)
                            dve.wait_ge(inv_taken, n + 1)
                            link(nc.vector.tensor_tensor(y, y, u[:, j, cols], ALU.mult))
                            n += 1


KINDS = 5
LBT, MBR, LKT, MKR, LB = range(KINDS)
KAPPA = -math.exp(-0.5)


MERGE_ORDER = [(m, b) for m in range(KD) for b in range(3)]
GATES = [G_TILE0 + KD * b + m for m, b in MERGE_ORDER]


class Uses:
    SLOTS = 3

    def __init__(self, K):
        self.sems = {"v": K.sem("rw_read_by_vector"), "s": K.sem("rw_read_by_scalar")}
        self.mm_done = K.sem("rw_mm_done")
        self.owner, self.value, self.index = [], [], {}
        self.count = {"v": 0, "s": 0}

    def add(self, key, owner):
        self.index[key] = len(self.owner)
        self.owner.append(owner)
        self.count[owner] += 1
        self.value.append(self.count[owner])

    def slot(self, key):
        return self.index[key] % self.SLOTS

    def wait_read(self, eng, key):
        n = self.index[key]
        eng.wait_ge(self.sems[self.owner[n]], self.value[n])

    def wait_free(self, pe, key):
        n = self.index[key] - self.SLOTS
        if n >= 0:
            pe.wait_ge(self.sems[self.owner[n]], self.value[n])

    def wait_mm(self, eng, key):
        eng.wait_ge(self.mm_done, self.index[key] + 1)

    def read(self, ins, key):
        ins.then_inc(self.sems[self.owner[self.index[key]]], 1)


def rwkv_stage(nc, K, A):
    with ExitStack() as ctx:
        def sb(name, shape):
            return ctx.enter_context(nc.sbuf_tensor("rw_" + name, shape, F32))

        def sem(name):
            return K.sem("rw_" + name)
        par = lambda name, i=0: K.par[:, PCOL[name] + i:PCOL[name] + i + 1]
        rT, kT, vT, kk = (sb(x, [P, 4, T]) for x in ("r", "k", "v", "kk"))
        v_tok = sb("v_tok", [P, NCH, W])
        lo = sb("lo", [P, 3, T])
        w2, a2 = (sb(x, [P, W]) for x in ("w2", "a2"))
        omka = sb("omka", [P, 4])
        ld_in = sem("ld_in")
        with ExitStack() as c1:
            pr = Projection(nc, c1, K, A, "rw", list(range(A_TILES + B_TILES, G_TILE0)))
            pp = c1.enter_context(nc.sbuf_tensor("rw_pp", [P, 2, LP + 2], F32))
            gp = c1.enter_context(nc.sbuf_tensor("rw_gp", [P, 2, 10, GRID_W + 2], F32))
            side = c1.enter_context(nc.sbuf_tensor("rw_side", [P, 2, LS], F32))
            zeroed, mixed, lo_act, y_out = sem("zeroed"), sem("mixed"), sem("lo_act"), sem("y_out")
            with nc.Block() as block:
                @block.sync
                def _(sp):
                    for b in range(2):
                        sp.dma_start(A["y_scratch"][b], K.yT[b][:]).then_inc(y_out, 16)
                    for i in range(C_TILES):
                        pr.load(sp, i)
                        if i == 3:
                            for t, n in ((w2, "rw_w2"), (a2, "rw_a2")):
                                sp.dma_start(t[:], A[n]).then_inc(ld_in, 16)
                    sp.wait_ge(y_out, 32)

                @block.tensor
                def _(pe):
                    for i in range(C_TILES):
                        pr.mm(pe, i)

                @block.scalar
                def _(act):
                    act.wait_ge(zeroed, 1)
                    for i in range(C_TILES):
                        act.wait_ge(pr.proj_done, i + 1)
                        if i >= 2:
                            act.wait_ge(mixed, i - 1)
                        b, o = i % 2, pr.out(i)
                        r0 = (HALF - LP) // GRID_W
                        nc.scalar.activation(pp[:, b, 1:1 + LP], o[:, 0, 0:LP], ACT.Copy)
                        nc.scalar.activation(gp[:, b, 1:1 + r0, 1:1 + GRID_W],
                                             o[:, 0, LP:HALF].rearrange("p (r c) -> p r c", c=GRID_W), ACT.Copy)
                        nc.scalar.activation(gp[:, b, 1 + r0:9, 1:1 + GRID_W],
                                             o[:, 1].rearrange("p (r c) -> p r c", c=GRID_W),
                                             ACT.Copy).then_inc(pr.proj_taken, 1)
                    act.wait_ge(mixed, C_TILES)
                    nc.scalar.activation(lo[:, 0], lo[:, 0], ACT.Tanh)
                    nc.scalar.activation(lo[:, 2], lo[:, 2], ACT.Sigmoid).then_inc(lo_act, 1)

                @block.vector
                def _(dve):
                    link = lambda ins: K.dve.link(dve, ins)
                    nc.vector.memset(pp[:], 0.0)
                    nc.vector.memset(gp[:], 0.0).then_inc(zeroed, 1)
                    for i in range(C_TILES):
                        dve.wait_ge(pr.proj_taken, i + 1)
                        b = i % 2
                        dst = (rT, kT, vT)[i // 4][:, i % 4] if i < 12 else lo[:, i - 12]
                        own_p, own_s = pp[:, b, 1:1 + LP], gp[:, b, 1:9, 1:1 + GRID_W]
                        dp, ds = dst[:, 0:LP], dst[:, LP:T].rearrange("p (r c) -> p r c", c=GRID_W)
                        sd = side[:, b].rearrange("p (r c) -> p r c", c=GRID_W)
                        nc.vector.tensor_tensor(dp, pp[:, b, 0:LP], pp[:, b, 2:LP + 2], ALU.add)
                        nc.vector.tensor_tensor(ds, gp[:, b, 0:8, 1:1 + GRID_W], gp[:, b, 2:10, 1:1 + GRID_W], ALU.add)
                        link(nc.vector.tensor_tensor(sd, gp[:, b, 1:9, 0:GRID_W], gp[:, b, 1:9, 2:2 + GRID_W], ALU.add))
                        nc.vector.scalar_tensor_tensor(out=dp, in0=dp, scalar=0.5, in1=own_p, op0=ALU.mult,
                                                       op1=ALU.subtract)
                        link(nc.vector.tensor_tensor(ds, ds, sd, ALU.add))
                        link(nc.vector.scalar_tensor_tensor(out=ds, in0=ds, scalar=0.25, in1=own_s, op0=ALU.mult,
                                                            op1=ALU.subtract))
                        nc.vector.scalar_tensor_tensor(out=dp, in0=dp, scalar=par("mu", i), in1=own_p,
                                                       op0=ALU.mult, op1=ALU.add)
                        nc.vector.scalar_tensor_tensor(out=ds, in0=ds, scalar=par("mu", i), in1=own_s,
                                                       op0=ALU.mult, op1=ALU.add).then_inc(mixed, 1)
        with ExitStack() as c1:
            sq = c1.enter_context(nc.sbuf_tensor("rw_sq", [P, 4, T], F32))
            ps = c1.enter_context(nc.psum_tensor("rw_ps0", [P, 2, 2, 512], F32))
            ps_t = c1.enter_context(nc.psum_tensor("rw_pst", [P, 2, 512], F32))
            kk_done, sq_done, sum_done, ms_done, root, v_done, v_taken = (sem(x) for x in (
                "kk_done", "sq_done", "sum_done", "ms_done", "root", "v_done", "v_taken"))
            with nc.Block() as block:
                @block.tensor
                def _(pe):
                    for j in range(4):
                        pe.wait_ge(sq_done, j + 1)
                        if j >= 2:
                            pe.wait_ge(ms_done, j - 1)
                        for c in range(2):
                            last = nc.tensor.matmul(ps[:, j % 2, c, 0:HALF], K.blk64,
                                                    sq[:, j, c * HALF:(c + 1) * HALF], start=True, stop=True)
                        last.then_inc(sum_done, 1)
                    for c in range(NCH):
                        if c >= 2:
                            pe.wait_ge(v_taken, c - 1)
                        for j in range(4):
                            last = nc.tensor.transpose(ps_t[:, c % 2, j * P:(j + 1) * P],
                                                       vT[:, j, c * P:(c + 1) * P], K.ident)
                        last.then_inc(v_done, 1)

                @block.scalar
                def _(act):
                    for j in range(4):
                        act.wait_ge(kk_done, j + 1)
                        nc.scalar.activation(sq[:, j], kk[:, j], ACT.Square).then_inc(sq_done, 1)
                    for j in range(4):
                        act.wait_ge(ms_done, j + 1)
                        nc.scalar.activation(sq[:, j], sq[:, j], ACT.Sqrt).then_inc(root, 1)
                    for c in range(NCH):
                        act.wait_ge(v_done, c + 1)
                        nc.scalar.activation(v_tok[:, c], ps_t[:, c % 2], ACT.Copy).then_inc(v_taken, 1)

                @block.vector
                def _(dve):
                    link = lambda ins: K.dve.link(dve, ins)
                    for j in range(4):
                        nc.vector.tensor_scalar(kk[:, j], kT[:, j], par("kk", j), None, ALU.mult).then_inc(kk_done, 1)
                    nc.vector.tensor_scalar(omka[:], K.par[:, PCOL["ka"]:PCOL["ka"] + 4], -1.0, 1.0, ALU.mult, ALU.add)
                    for j in range(4):
                        dve.wait_ge(sum_done, j + 1)
                        nc.vector.tensor_scalar(halves(sq[:, j]), ps[:, j % 2, :, 0:HALF], 1e-12, None,
                                                ALU.add).then_inc(ms_done, 1)
                    for j in range(4):
                        dve.wait_ge(root, j + 1)
                        link(nc.vector.reciprocal(sq[:, j], sq[:, j]))
                        link(nc.vector.tensor_tensor(kk[:, j], kk[:, j], sq[:, j], ALU.mult))
        with ExitStack() as c1:
            def wb(name, shape):
                return c1.enter_context(nc.sbuf_tensor("rw_" + name, shape, F32))
            mask = wb("mask", [P, 2, KINDS, P])
            bmask = wb("bmask", [P, 4, P])
            reset, lf, cum = (wb(x, [P, RESET_W]) for x in ("reset", "lf", "cum"))
            rate = wb("rate", [P, NCH, P])
            AR = wb("AR", [P, NCH, 2, P])
            bT, kd, b_tok, kd_tok = (wb(x, [P, NCH, P]) for x in ("bT", "kd", "b_tok", "kd_tok"))
            ends = wb("ends", [P, 2, NCH])
            sys_ = wb("sys", [P, 2, NCH, KINDS, P])
            own = [K.yT[b][:].rearrange("p k t -> p (k t)").rearrange("p (n h c t) -> p n h c t", n=2, h=2, c=NCH)
                   for b in range(2)]
            D_, U_, D2, U2 = (own[n // 2][:, n % 2] for n in range(4))
            gate_w = wb("gate_w", [P, 2, KD, P])
            gate = wb("gate", [P, T])
            D4, U4, X_, C_ = (wb(x, [P, 2, NCH, P]) for x in ("D4", "U4", "X", "C"))
            R1, SA = wb("R1", [P, P]), wb("SA", [P, P])
            S0 = wb("S0", [P, 8, HD])
            STp, tS, Sout = wb("STp", [P, HD]), wb("tS", [P, HD]), wb("Sout", [P, HD])
            ring = c1.enter_context(nc.psum_tensor("rw_ring", [P, Uses.SLOTS, 1024], F32))
            gate_ps = c1.enter_context(nc.psum_tensor("rw_gate_ps", [P, 2, 512], F32))
            use = Uses(K)
            gate_w_in = [sem(f"gate_w_in{i}") for i in range(2)]
            gate_mm, gate_taken, gate_out = sem("gate_mm"), sem("gate_taken"), sem("gate_out")
            c_in, s0_in, logs, cum_done, exps, exp_done, ops_ready, sys_masked, s_out, s_ready, pool_done, ends_used = (
                sem(x) for x in ("c_in", "s0_in", "logs", "cum_done", "exps", "exp_done", "ops_ready", "sys_masked",
                                 "s_out", "s_ready", "pool_done", "ends_used"))

            def order(d):
                return [0] + ([1, 2, 3, 4] if d == 0 else [4, 3, 2, 1])
            STEPS = [("U2", "s"), ("D2", "v"), ("X1", "v"), ("U4", "s"), ("D4", "s"), ("X2", "v"), ("D8", "s"),
                     ("X3", "v")]
            for lv in range(3):
                STEPS += [(f"Y{lv}", "s"), (f"W{lv}", "s"), (f"J{lv}", "v")]
            for w in range(8):
                for x in ("w", "a", "bt", "kt"):
                    use.add((w, x), "s")
                for hh in range(2):
                    for c in range(NCH):
                        use.add((w, "sys", hh, c), "v")
                for x, owner in STEPS:
                    for hh in range(2):
                        use.add((w, x, hh), owner)
                for k in range(NCH):
                    for x in ("R1", "SA", "Y", "S"):
                        if x == "S" and k == NCH - 1:
                            continue
                        use.add((w, x, k), "v")

            def flat(key, n=T):
                return ring[:, use.slot(key), 0:n]

            def chunks(key):
                return flat(key).rearrange("p (c t) -> p c t", t=P)
            POOL = ["D", "U", "X0", "C0", "C1", "C2"]

            def pool_count(w, name, hh):
                return 12 * w + 2 * POOL.index(name) + hh + 1

            with nc.Block() as block:
                @block.sync
                def _(sp):
                    for t, n in ((mask, "rw_mask"), (bmask, "rw_bmask"), (reset, "reset")):
                        sp.dma_start(t[:], A[n]).then_inc(c_in, 16)
                    sp.dma_start(S0[:], A["state_rwkv"]).then_inc(s0_in, 16)

                    def gate_load(i):
                        if i >= 2:
                            sp.wait_ge(gate_mm, i - 1)
                        sp.dma_start(gate_w[:, i % 2], A["w_in"][GATES[i]]).then_inc(gate_w_in[i % 2], 16)

                    for i in range(2):
                        gate_load(i)
                    for w in range(8):
                        for i in range(3 * w, 3 * w + 3):
                            if i == 3 * w + 1:
                                sp.wait_ge(s_ready, w + 1)
                                sp.dma_start(A["out_rwkv"][w], Sout[:]).then_inc(s_out, 16)
                            if i + 2 < len(GATES):
                                gate_load(i + 2)
                            sp.wait_ge(gate_taken, i + 1)
                            sp.dma_start(A["gate_scratch"][i], gate[:]).then_inc(gate_out, 16)
                    sp.wait_ge(s_out, 16 * 8)
                    sp.wait_ge(gate_out, 16 * len(GATES))

                @block.tensor
                def _(pe):
                    pe.wait_ge(ld_in, 32)
                    pe.wait_ge(c_in, 48)

                    def product(key, pairs, n=NCH):
                        use.wait_free(pe, key)
                        out = chunks(key)
                        for c in range(n):
                            last = pairs(out[:, c], c)
                        last.then_inc(use.mm_done, 1)

                    def gates(i, first, end):
                        for n in range(first, end):
                            k, c = n // 2, n % 2
                            if n == 0:
                                pe.wait_ge(gate_w_in[i % 2], 16 * (i // 2 + 1))
                                if i:
                                    pe.wait_ge(gate_taken, i)
                            last = nc.tensor.matmul(gate_ps[:, c, 0:HALF], gate_w[:, i % 2, k],
                                                    K.hT[:, k, c * HALF:(c + 1) * HALF],
                                                    start=(k == 0), stop=(k == KD - 1))
                            if n == 2 * KD - 1:
                                last.then_inc(gate_mm, 1)

                    def gates_in_scan(w, point):
                        i, q = 3 * w + 1 + point // 8, point % 8
                        if q < 7:
                            gates(i, 2 * KD * q // 7, 2 * KD * (q + 1) // 7)

                    for w in range(8):
                        d, j = w // 4, w % 4
                        rows = slice(64 * d, 64 * d + 64)
                        for key, wt, x in (((w, "w"), w2, lo[rows, 0]), ((w, "a"), a2, lo[rows, 1])):
                            use.wait_free(pe, key)
                            o = ring[:, use.slot(key)].rearrange("p (c n) -> p c n", c=2)
                            for c in range(2):
                                last = nc.tensor.matmul(o[:, c, 0:HALF], wt[rows, j * P:(j + 1) * P],
                                                        x[:, c * HALF:(c + 1) * HALF], start=True, stop=True)
                            last.then_inc(use.mm_done, 1)
                        gates(3 * w, 0, 2 * KD)
                        pe.wait_ge(ops_ready, w + 1)
                        for key, src in (((w, "bt"), bT), ((w, "kt"), kd)):
                            product(key, lambda o, c: nc.tensor.transpose(o, src[:, c], K.ident))
                        for hh in range(2):
                            hp = slice(64 * hh, 64 * hh + 64)
                            for c in range(NCH):
                                key = (w, "sys", hh, c)
                                use.wait_free(pe, key)
                                o = flat(key)
                                ar = AR[hp, c].rearrange("p a t -> p (a t)")
                                nc.tensor.matmul(o[:, 0:2 * P], bT[hp, c], ar, start=True, stop=True)
                                nc.tensor.matmul(o[:, 2 * P:4 * P], kd[hp, c], ar, start=True, stop=True)
                                nc.tensor.matmul(o[:, 4 * P:5 * P], AR[hp, c, 0], bT[hp, c], start=True,
                                                 stop=True).then_inc(use.mm_done, 1)

                        mm = lambda l, r: (lambda o, c: nc.tensor.matmul(o, l[:, c], r[:, c], start=True, stop=True))
                        for name, _owner in STEPS:
                            for hh in range(2):
                                key = (w, name, hh)
                                D, U, DD, UU, D4h, U4h, X, C = (x[:, hh] for x in (D_, U_, D2, U2, D4, U4, X_, C_))
                                if name == "U2":
                                    pe.wait_ge(pool_done, pool_count(w, "U", hh))
                                    product(key, mm(D, U))
                                elif name == "D2":
                                    product(key, mm(U, D))
                                elif name == "X1":
                                    pe.wait_ge(pool_done, pool_count(w, "X0", hh))
                                    use.wait_read(pe, (w, "D2", hh))
                                    product(key, mm(DD, X))
                                elif name == "U4":
                                    use.wait_read(pe, (w, "U2", hh))
                                    product(key, mm(DD, UU))
                                elif name == "D4":
                                    product(key, mm(UU, DD))
                                elif name == "X2":
                                    use.wait_read(pe, (w, "D4", hh))
                                    use.wait_read(pe, (w, "X1", hh))
                                    product(key, mm(D4h, X))
                                elif name == "D8":
                                    use.wait_read(pe, (w, "U4", hh))
                                    product(key, mm(U4h, D4h))
                                elif name == "X3":
                                    use.wait_read(pe, (w, "D8", hh))
                                    use.wait_read(pe, (w, "X2", hh))
                                    product(key, mm(D, X))
                                else:
                                    lv = int(name[1])
                                    Cl = (C, D4h, U4h)[lv]
                                    if name[0] == "Y":
                                        use.wait_read(pe, (w, "X3" if lv == 0 else f"J{lv - 1}", hh))
                                        product(key, lambda o, c: nc.tensor.transpose(o, X[:, c], K.ident))
                                    elif name[0] == "W":
                                        pe.wait_ge(pool_done, pool_count(w, f"C{lv}", hh))
                                        product(key, mm(Cl, X))
                                    else:
                                        use.wait_read(pe, (w, f"W{lv}", hh))
                                        product(key, mm(UU, DD))
                        for k, c in enumerate(order(d)):
                            hps = [slice(64 * hh, 64 * hh + 64) for hh in range(2)]
                            v_of = lambda hh: v_tok[:, c, (2 * j + hh) * HD:(2 * j + hh + 1) * HD]
                            with_state = k > 0
                            key = (w, "R1", k)
                            use.wait_free(pe, key)
                            gates_in_scan(w, 3 * k)
                            if k == 0:
                                use.wait_read(pe, (w, "J2", 1))
                            else:
                                pe.wait_ge(ends_used, 4 * w + k)
                            for hh, hp in enumerate(hps):
                                o = ring[:, use.slot(key), hh * 512:hh * 512 + HD]
                                if with_state:
                                    nc.tensor.matmul(o, AR[hp, c, 0], STp[hp, :], start=True, stop=False)
                                last = nc.tensor.matmul(o, sys_[:, hh, c, LKT], v_of(hh), start=not with_state,
                                                        stop=True)
                            last.then_inc(use.mm_done, 1)
                            gates_in_scan(w, 3 * k + 1)
                            use.wait_read(pe, key)
                            key = (w, "SA", k)
                            use.wait_free(pe, key)
                            for hh in range(2):
                                last = nc.tensor.matmul(ring[:, use.slot(key), hh * 512:hh * 512 + HD], X_[:, hh, c],
                                                        R1[:, hh * HD:(hh + 1) * HD], start=True, stop=True)
                            last.then_inc(use.mm_done, 1)
                            gates_in_scan(w, 3 * k + 2)
                            use.wait_read(pe, key)
                            key = (w, "Y", k)
                            use.wait_free(pe, key)
                            for hh, hp in enumerate(hps):
                                o = flat(key)[hp, 0:P]
                                sa = SA[:, hh * HD:(hh + 1) * HD]
                                if with_state:
                                    nc.tensor.matmul(o, STp[hp, :], AR[hp, c, 1], start=True, stop=False)
                                nc.tensor.matmul(o, sa, sys_[:, hh, c, MBR], start=not with_state, stop=False)
                                last = nc.tensor.matmul(o, v_of(hh), sys_[:, hh, c, MKR], start=False, stop=True)
                            last.then_inc(use.mm_done, 1)
                            if k == NCH - 1:
                                continue
                            key = (w, "S", k)
                            use.wait_free(pe, key)
                            for hh, hp in enumerate(hps):
                                o = flat(key)[hp, 0:HD]
                                sa = SA[:, hh * HD:(hh + 1) * HD]
                                nc.tensor.matmul(o, b_tok[:, c, hp], sa, start=True, stop=False)
                                last = nc.tensor.matmul(o, kd_tok[:, c, hp], v_of(hh), start=False, stop=True)
                            last.then_inc(use.mm_done, 1)

                @block.scalar
                def _(act):
                    lfv = lf[:].rearrange("p (c t) -> p c t", t=129)
                    cumv = cum[:].rearrange("p (c t) -> p c t", t=129)

                    def take(key, dst):
                        use.wait_mm(act, key)
                        use.read(nc.scalar.activation(dst, chunks(key), ACT.Copy), key)

                    def take_gate(i):
                        act.wait_ge(gate_mm, i + 1)
                        if i:
                            act.wait_ge(gate_out, 16 * i)
                        nc.scalar.activation(halves(gate[:]), gate_ps[:, :, 0:HALF],
                                             ACT.Copy).then_inc(gate_taken, 1)

                    for w in range(8):
                        d, j = w // 4, w % 4
                        if w:
                            act.wait_ge(ops_ready, w)
                        for key, dst, bias in (((w, "w"), lf, par("w0", 4 * d + j)), ((w, "a"), rate, par("a0", 4 * d + j))):
                            use.wait_mm(act, key)
                            pieces = ring[:, use.slot(key)].rearrange("p (c n) -> p c n", c=2)
                            if key[1] == "w":
                                nc.scalar.activation(lfv[:, 0:2, 1:129],
                                                     pieces[:, 0, 0:2 * P].rearrange("p (c t) -> p c t", t=P),
                                                     ACT.Sigmoid, bias=bias)
                                nc.scalar.activation(lfv[:, 2, 1:65], pieces[:, 0, 2 * P:HALF], ACT.Sigmoid, bias=bias)
                                nc.scalar.activation(lfv[:, 2, 65:129], pieces[:, 1, 0:64], ACT.Sigmoid, bias=bias)
                                ins = nc.scalar.activation(lfv[:, 3:5, 1:129],
                                                           pieces[:, 1, 64:HALF].rearrange("p (c t) -> p c t", t=P),
                                                           ACT.Sigmoid, bias=bias)
                            else:
                                ins = nc.scalar.activation(rate[:].rearrange("p c t -> p (c t)").rearrange(
                                    "p (c n) -> p c n", c=2), pieces[:, :, 0:HALF], ACT.Sigmoid, bias=bias)
                            use.read(ins, key)
                        act.wait_ge(exps, w + 1)
                        nc.scalar.activation(AR[:], AR[:], ACT.Exp, scale=KAPPA)
                        nc.scalar.activation(ends[:], ends[:], ACT.Exp, scale=KAPPA)
                        nc.scalar.activation(bT[:], bT[:], ACT.Exp, scale=KAPPA).then_inc(exp_done, 1)
                        take_gate(3 * w)
                        take((w, "bt"), b_tok[:])
                        take((w, "kt"), kd_tok[:])
                        for name, owner in STEPS:
                            if owner != "s":
                                continue
                            for hh in range(2):
                                dst = {"U2": U2, "U4": U4, "D4": D4, "D8": D_}.get(name)
                                if dst is None:
                                    dst = U2 if name[0] == "Y" else D2
                                take((w, name, hh), dst[:, hh])
                        take_gate(3 * w + 1)
                        take_gate(3 * w + 2)

                @block.gpsimd
                def _(pool):
                    pool.wait_ge(c_in, 48)
                    for w in range(8):
                        for name in POOL:
                            for hh in range(2):
                                def msk(i):
                                    return bc(bmask[:, i].unsqueeze(1), [P, NCH, P])
                                if name in "DU":
                                    use.wait_read(pool, (w, "sys", hh, NCH - 1))
                                    src, dst = (LB, D_) if name == "D" else (LBT, U_)
                                    ins = nc.gpsimd.tensor_tensor(dst[:, hh], sys_[:, hh, :, src], msk(0), ALU.mult)
                                elif name == "X0":
                                    pool.wait_ge(pool_done, pool_count(w, "U", hh))
                                    ins = nc.gpsimd.tensor_tensor(
                                        X_[:, hh], U_[:, hh], bc(K.ident.unsqueeze(1), [P, NCH, P]), ALU.add)
                                else:
                                    lv = int(name[1])
                                    if lv == 1:
                                        use.wait_mm(pool, (w, "D8", hh))
                                    if lv == 2:
                                        use.wait_mm(pool, (w, "D8", hh))
                                    ins = nc.gpsimd.tensor_tensor((C_, D4, U4)[lv][:, hh], sys_[:, hh, :, LB],
                                                                  msk(1 + lv), ALU.mult)
                                ins.then_inc(pool_done, 1)

                @block.vector
                def _(dve):
                    link = lambda ins: K.dve.link(dve, ins)
                    lfv = lf[:].rearrange("p (c t) -> p c t", t=129)
                    cumv = cum[:].rearrange("p (c t) -> p c t", t=129)
                    link(nc.vector.memset(lfv[:, :, 0:1], 0.0))
                    dve.wait_ge(c_in, 48)
                    inc, exc = cumv[:, :, 1:129], cumv[:, :, 0:128]
                    mid, end = cumv[:, :, 64:65], cumv[:, :, 128:129]
                    for w in range(8):
                        d, j = w // 4, w % 4
                        use.wait_read(dve, (w, "w"))
                        link(nc.vector.tensor_tensor_scan(cum[:], reset[:], lf[:], 0.0, ALU.mult, ALU.add))
                        m = bc(mid, [P, NCH, P])
                        if d == 0:
                            nc.vector.tensor_tensor(AR[:, :, 0], exc, m, ALU.subtract)
                            nc.vector.tensor_tensor(AR[:, :, 1], inc, m, ALU.subtract)
                            nc.vector.tensor_tensor(bT[:], m, inc, ALU.subtract)
                            pre, post = 0, 1
                        else:
                            nc.vector.tensor_tensor(AR[:, :, 0], m, inc, ALU.subtract)
                            nc.vector.tensor_tensor(AR[:, :, 1], m, exc, ALU.subtract)
                            nc.vector.tensor_tensor(bT[:], exc, m, ALU.subtract)
                            pre, post = 1, 0
                        nc.vector.tensor_copy(ends[:, pre].unsqueeze(2), mid)
                        nc.vector.tensor_tensor(ends[:, post].unsqueeze(2), end, mid, ALU.subtract).then_inc(exps, 1)
                        if d == 1:
                            pass
                        dve.wait_ge(exp_done, w + 1)
                        use.wait_read(dve, (w, "a"))
                        of = lambda x: x[:, j].rearrange("p (c t) -> p c t", t=P)
                        link(nc.vector.scalar_tensor_tensor(out=AR[:, :, 0], in0=AR[:, :, 0], scalar=-1.0, in1=of(kk),
                                                            op0=ALU.mult, op1=ALU.mult))
                        nc.vector.tensor_tensor(AR[:, :, 1], AR[:, :, 1], of(rT), ALU.mult)
                        link(nc.vector.tensor_scalar(kd[:], rate[:], par("ka", j), omka[:, j:j + 1], ALU.mult, ALU.add))
                        link(nc.vector.tensor_tensor(kd[:], kd[:], of(kT), ALU.mult))
                        link(nc.vector.tensor_tensor(kd[:], kd[:], bT[:], ALU.mult))
                        link(nc.vector.tensor_tensor(bT[:], bT[:], rate[:], ALU.mult))
                        nc.vector.tensor_tensor(bT[:], bT[:], of(kk), ALU.mult).then_inc(ops_ready, 1)
                        for hh in range(2):
                            for c in range(NCH):
                                key = (w, "sys", hh, c)
                                use.wait_mm(dve, key)
                                if w and hh == 0 and c == 0:
                                    dve.wait_ge(pool_done, 12 * w)
                                use.read(nc.vector.tensor_tensor(
                                    sys_[:, hh, c], flat(key).rearrange("p (k t) -> p k t", t=P), mask[:, d],
                                    ALU.mult), key)
                        for name, owner in STEPS:
                            if owner != "v":
                                continue
                            for hh in range(2):
                                key = (w, name, hh)
                                use.wait_mm(dve, key)
                                if name == "D2":
                                    use.read(nc.vector.tensor_copy(D2[:, hh], chunks(key)), key)
                                else:
                                    if name == "X1":
                                        dve.wait_ge(pool_done, pool_count(w, "X0", hh))
                                    use.read(nc.vector.tensor_tensor(X_[:, hh], X_[:, hh], chunks(key), ALU.add), key)
                        seq = order(d)
                        if w == 0:
                            dve.wait_ge(s0_in, 16)
                        for k, c in enumerate(seq):
                            for x, dst in (("R1", R1), ("SA", SA)):
                                key = (w, x, k)
                                use.wait_mm(dve, key)
                                both = ring[:, use.slot(key)].rearrange("p (h n) -> p h n", h=2)[:, :, 0:HD]
                                use.read(nc.vector.tensor_copy(dst[:].rearrange("p (h n) -> p h n", h=2), both), key)
                            key = (w, "Y", k)
                            use.wait_mm(dve, key)
                            y = K.yT[2][:, j, c * P:(c + 1) * P]
                            if d == 0:
                                use.read(nc.vector.tensor_copy(y, flat(key, P)), key)
                            else:
                                use.read(nc.vector.tensor_tensor(y, y, flat(key, P), ALU.add), key)
                            if k == NCH - 1:
                                continue
                            key = (w, "S", k)
                            use.wait_mm(dve, key)
                            ps = flat(key, HD)
                            cn = seq[k + 1]
                            if k == 0:
                                if w:
                                    dve.wait_ge(s_out, 16 * w)
                                use.read(nc.vector.tensor_scalar(Sout[:], ps, ends[:, 1, c:c + 1], None, ALU.mult), key)
                                use.wait_read(dve, key)
                                dve.sem_inc(s_ready, 1)
                                nc.vector.tensor_scalar(STp[:], S0[:, w], ends[:, 0, cn:cn + 1], None,
                                                        ALU.mult).then_inc(ends_used, 1)
                            else:
                                ins = nc.vector.tensor_tensor(tS[:], ps, STp[:], ALU.add)
                                use.read(ins, key)
                                use.wait_read(dve, key)
                                nc.vector.tensor_scalar(STp[:], tS[:], ends[:, 1, c:c + 1], ends[:, 0, cn:cn + 1],
                                                        ALU.mult, ALU.mult).then_inc(ends_used, 1)
        with ExitStack() as c1:
            t1 = c1.enter_context(nc.sbuf_tensor("rw_t1", [P, 4, T], F32))
            ps = c1.enter_context(nc.psum_tensor("rw_ps1", [P, 4, 2, 512], F32))
            y = K.yT[2]
            y_in = sem("y_in")
            g2 = c1.enter_context(nc.sbuf_tensor("rw_g2", [P, W], F32))
            gn = {x: sem("gn_" + x) for x in ("mean", "cent", "sq", "var", "varr", "root", "rk", "bon", "bond", "gmm", "norm")}
            with nc.Block() as block:
                @block.sync
                def _(sp):
                    sp.dma_start(g2[:], A["rw_g2"]).then_inc(ld_in, 16)
                    for b in range(2):
                        sp.dma_start(K.yT[b][:], A["y_scratch"][b]).then_inc(y_in, 16)
                    sp.wait_ge(y_in, 32)

                @block.tensor
                def _(pe):
                    def sums(w_, src, j, s, done):
                        for c in range(2):
                            last = nc.tensor.matmul(ps[:, s, c, 0:HALF], w_, src[:, c * HALF:(c + 1) * HALF],
                                                    start=True, stop=True)
                        last.then_inc(done, 1)
                    for j in range(4):
                        if j:
                            pe.wait_ge(gn["cent"], j)
                        sums(K.blk64, y[:, j], j, 0, gn["mean"])
                        pe.wait_ge(gn["sq"], j + 1)
                        if j:
                            pe.wait_ge(gn["varr"], j)
                        sums(K.blk64, t1[:, j], j, 1, gn["var"])
                        pe.wait_ge(gn["rk"], j + 1)
                        if j:
                            pe.wait_ge(gn["bond"], j)
                        sums(K.blk64, kk[:, j], j, 2, gn["bon"])
                        if j:
                            pe.wait_ge(gn["norm"], j)
                        pe.wait_ge(ld_in, 48)
                        sums(g2[:, j * P:(j + 1) * P], lo[:, 2], j, 3, gn["gmm"])

                @block.scalar
                def _(act):
                    for j in range(4):
                        act.wait_ge(gn["cent"], j + 1)
                        nc.scalar.activation(t1[:, j], y[:, j], ACT.Square).then_inc(gn["sq"], 1)
                        act.wait_ge(gn["varr"], j + 1)
                        nc.scalar.activation(t1[:, j], t1[:, j], ACT.Sqrt).then_inc(gn["root"], 1)

                @block.vector
                def _(dve):
                    link = lambda ins: K.dve.link(dve, ins)
                    for j in range(4):
                        link(nc.vector.scalar_tensor_tensor(out=kk[:, j], in0=rT[:, j], scalar=par("rk", j),
                                                            in1=kT[:, j], op0=ALU.mult, op1=ALU.mult))
                        dve.sem_inc(gn["rk"], 1)
                        dve.wait_ge(gn["mean"], j + 1)
                        nc.vector.scalar_tensor_tensor(out=halves(y[:, j]), in0=ps[:, 0, :, 0:HALF], scalar=-1.0 / HD,
                                                       in1=halves(y[:, j]), op0=ALU.mult, op1=ALU.add).then_inc(gn["cent"], 1)
                        dve.wait_ge(gn["var"], j + 1)
                        nc.vector.tensor_scalar(halves(t1[:, j]), ps[:, 1, :, 0:HALF], 1.0 / HD, GN_EPS, ALU.mult,
                                                ALU.add).then_inc(gn["varr"], 1)
                        dve.wait_ge(gn["bon"], j + 1)
                        ins = nc.vector.tensor_tensor(halves(vT[:, j]), halves(vT[:, j]), ps[:, 2, :, 0:HALF], ALU.mult)
                        ins.then_inc(gn["bond"], 1)
                        dve.wait_ge(gn["root"], j + 1)
                        link(nc.vector.reciprocal(t1[:, j], t1[:, j]))
                        link(nc.vector.tensor_tensor(y[:, j], y[:, j], t1[:, j], ALU.mult))
                        link(nc.vector.tensor_scalar(y[:, j], y[:, j], par("ln_g", j), par("ln_b", j), ALU.mult, ALU.add))
                        link(nc.vector.tensor_tensor(y[:, j], y[:, j], vT[:, j], ALU.add))
                        dve.wait_ge(gn["gmm"], j + 1)
                        nc.vector.tensor_tensor(halves(y[:, j]), halves(y[:, j]), ps[:, 3, :, 0:HALF],
                                                ALU.mult).then_inc(gn["norm"], 1)


def merge_stage(nc, K, A):
    with ExitStack() as ctx:
        def sb(name, shape):
            return ctx.enter_context(nc.sbuf_tensor("mg_" + name, shape, F32))

        def sem(name):
            return K.sem("mg_" + name)
        x2 = sb("x2", [P, KD, T])
        x_in, x2_out = sem("x_in"), sem("x2_out")
        with ExitStack() as c1:
            merged = c1.enter_context(nc.sbuf_tensor("mg_merged", [P, KD, T], F32))
            gate = c1.enter_context(nc.sbuf_tensor("mg_gate", [P, 4, T], F32))
            part = c1.enter_context(nc.sbuf_tensor("mg_part", [P, 2, T], F32))
            wb = c1.enter_context(nc.sbuf_tensor("mg_wb", [P, 4, KW, P], F32))
            wo = c1.enter_context(nc.sbuf_tensor("mg_wo", [P, 4, KD, P], F32))
            ps = c1.enter_context(nc.psum_tensor("mg_psb", [P, 4, 2, 512], F32))
            g_in, wb_in, wo_in = ([sem(f"{x}{i}") for i in range(4)] for x in ("g_in", "wb_in", "wo_in"))
            br_mm, br_taken, gated, summed, out_mm, out_taken = (sem(x) for x in (
                "br_mm", "br_taken", "gated", "summed", "out_mm", "out_taken"))
            with nc.Block() as block:
                @block.sync
                def _(sp):
                    for i in range(24):
                        if i >= 4:
                            sp.wait_ge(br_mm, i - 3)
                        sp.dma_start(wb[:, i % 4], A["w_branch"][i]).then_inc(wb_in[i % 4], 16)
                        if i >= 4:
                            sp.wait_ge(br_taken, i - 3)
                        sp.dma_start(gate[:, i % 4], A["gate_scratch"][i]).then_inc(g_in[i % 4], 16)
                        if i == 12:
                            for m in range(4):
                                sp.dma_start(wo[:, m], A["w_out"][m]).then_inc(wo_in[m], 16)
                            sp.dma_start(x2[:], A["x"]).then_inc(x_in, 16)
                    for m in range(4, KD):
                        sp.wait_ge(out_mm, m - 3)
                        sp.dma_start(wo[:, m % 4], A["w_out"][m]).then_inc(wo_in[m % 4], 16)

                @block.tensor
                def _(pe):
                    for i, (m, b) in enumerate(MERGE_ORDER):
                        pe.wait_ge(wb_in[i % 4], 16 * (i // 4 + 1))
                        if i >= 4:
                            pe.wait_ge(br_taken, i - 3)
                        for k in range(KW):
                            for c in range(2):
                                last = nc.tensor.matmul(ps[:, i % 4, c, 0:HALF], wb[:, i % 4, k],
                                                        K.yT[b][:, k, c * HALF:(c + 1) * HALF],
                                                        start=(k == 0), stop=(k == KW - 1))
                        last.then_inc(br_mm, 1)
                    pe.wait_ge(summed, 24)
                    for m in range(KD):
                        pe.wait_ge(wo_in[m % 4], 16 * (m // 4 + 1))
                        if m >= 4:
                            pe.wait_ge(out_taken, m - 3)
                        for k in range(KD):
                            for s, (a, b) in enumerate(SEG):
                                last = nc.tensor.matmul(ps[:, m % 4, s, 0:b - a], wo[:, m % 4, k], merged[:, k, a:b],
                                                        start=(k == 0), stop=(k == KD - 1))
                        last.then_inc(out_mm, 1)

                @block.scalar
                def _(act):
                    for i in range(24):
                        act.wait_ge(g_in[i % 4], 16 * (i // 4 + 1))
                        nc.scalar.activation(gate[:, i % 4], gate[:, i % 4], ACT.Sigmoid).then_inc(gated, 1)

                @block.vector
                def _(dve):
                    for i, (m, b) in enumerate(MERGE_ORDER):
                        dve.wait_ge(br_mm, i + 1)
                        dve.wait_ge(gated, i + 1)
                        dst = merged[:, m] if b == 0 else part[:, b - 1]
                        nc.vector.tensor_tensor(halves(dst), ps[:, i % 4, :, 0:HALF], halves(gate[:, i % 4]),
                                                ALU.mult).then_inc(br_taken, 1)
                        if b:
                            dve.wait_ge(br_taken, i + 1)
                            dve.wait_ge(summed, i)
                            nc.vector.tensor_tensor(merged[:, m], merged[:, m], dst, ALU.add).then_inc(summed, 1)
                        else:
                            dve.sem_inc(summed, 1)
                    dve.wait_ge(x_in, 16)
                    for m in range(KD):
                        dve.wait_ge(out_mm, m + 1)
                        for s, (a, b) in enumerate(SEG):
                            ins = nc.vector.scalar_tensor_tensor(
                                out=x2[:, m, a:b], in0=ps[:, m % 4, s, 0:b - a], scalar=K.mod[:, 2 * KD + m, s:s + 1],
                                in1=x2[:, m, a:b], op0=ALU.mult, op1=ALU.add)
                        ins.then_inc(out_taken, 1)
        with nc.Block() as block:
            @block.sync
            def _(sp):
                sp.dma_start(A["x_scratch"], x2[:]).then_inc(x2_out, 16)
                sp.wait_ge(x2_out, 16)
        norm_stage(nc, K, A, 1, x2, K.hT, "n2")


RING = 8
TURNS = SLOTS // RING


def peer_stage(nc, K, A):
    with ExitStack() as ctx:
        def sb(name, shape, dt=F32):
            return ctx.enter_context(nc.sbuf_tensor("pr_" + name, shape, dt))

        def sem(name):
            return K.sem("pr_" + name)
        h_tok = sb("h_tok", [P, NCH, D])
        qT = sb("q", [P, HEADS_P, T])
        keys = sb("keys", [P, NKEYS])
        keys_in = sem("keys_in")
        with ExitStack() as c1:
            pr = Projection(nc, c1, K, A, "pq", list(range(HEADS_P)), "p_wq")
            ps_t = c1.enter_context(nc.psum_tensor("pr_pst", [P, 2, 2, 512], F32))
            t_done, t_taken = sem("t_done"), sem("t_taken")
            with nc.Block() as block:
                @block.sync
                def _(sp):
                    sp.dma_start(keys[:], A["p_keys"]).then_inc(keys_in, 16)
                    for i in range(HEADS_P):
                        pr.load(sp, i)
                    sp.wait_ge(keys_in, 16)

                @block.tensor
                def _(pe):
                    for c in range(NCH):
                        if c >= 2:
                            pe.wait_ge(t_taken, c - 1)
                        for k in range(KD):
                            last = nc.tensor.transpose(ps_t[:, c % 2, k // 4, (k % 4) * P:(k % 4 + 1) * P],
                                                       K.hT[:, k, c * P:(c + 1) * P], K.ident)
                        last.then_inc(t_done, 1)
                    for i in range(HEADS_P):
                        pr.mm(pe, i)

                @block.scalar
                def _(act):
                    for i in range(HEADS_P):
                        act.wait_ge(pr.proj_done, i + 1)
                        nc.scalar.activation(halves(qT[:, i]), pr.out(i), ACT.Copy).then_inc(pr.proj_taken, 1)

                @block.vector
                def _(dve):
                    for c in range(NCH):
                        dve.wait_ge(t_done, c + 1)
                        nc.vector.tensor_copy(h_tok[:, c].rearrange("p (a n) -> p a n", a=2),
                                              ps_t[:, c % 2]).then_inc(t_taken, 1)
        y_tok = K.hT[:].rearrange("p k t -> p (k t)").rearrange("p (c d) -> p c d", c=NCH)
        s = sb("s", [P, 2 * HEADS_P, NKEYS])
        cand = sb("cand", [P, HEADS_P, TOPK, TOPK])
        hot = sb("hot", [P, HEADS_P, TOPK, TOPK])
        top = sb("top", [P, 2 * HEADS_P, TOPK])
        top_i = sb("top_i", [P, 2 * HEADS_P, TOPK], U32)
        top_f = sb("top_f", [P, 2 * HEADS_P, TOPK])
        best = sb("best", [P, HEADS_P, TOPK])
        best_i = sb("best_i", [P, HEADS_P, TOPK], U32)
        row_i = sb("row_i", [P, 2, HEADS_P, TOPK], U32)
        row_f = sb("row_f", [P, 2, HEADS_P, TOPK])
        pick = sb("pick", [P, 2, HEADS_P, TOPK])
        zsum = sb("zsum", [P, HEADS_P])
        gate = sb("gate", [P, 3, HEADS_P, TOPK])
        experts = sb("experts", [P, 3, SLOTS], I32)
        now_u, now_v = sb("now_u", [P, 2, RING], I32), sb("now_v", [P, 2, RING], I32)
        u_rows, v_rows = sb("u_rows", [P, RING, D]), sb("v_rows", [P, RING, D])
        dot8 = sb("dot8", [P, 2, RING])
        dots = sb("dots", [P, 2, SLOTS])
        weight = sb("weight", [P, 2, SLOTS])
        diag = sb("diag", [P, RING, P])
        ps_s = ctx.enter_context(nc.psum_tensor("pr_pss", [P, 2, HEADS_P, NKEYS], F32))
        ps_y = ctx.enter_context(nc.psum_tensor("pr_psy", [P, 2, 2, 512], F32))
        u_in = [sem(f"u_in{i}") for i in range(RING)]
        v_in = [sem(f"v_in{i}") for i in range(RING)]
        (s_mm, s_taken, arg_done, exp_done, routed, u_used, dots_done, gelu_done, w_done, diag_done, v_used, y_done,
         y_taken, now_done, slot_free, dot_moved) = (sem(x) for x in (
             "s_mm", "s_taken", "arg_done", "exp_done", "routed", "u_used", "dots_done", "gelu_done", "w_done",
             "diag_done", "v_used", "y_done", "y_taken", "now_done", "slot_free", "dot_moved"))
        iota = K.con[:, CCOL["iota"]:CCOL["iota"] + TOPK]
        with nc.Block() as block:
            @block.gpsimd
            def _(pool):
                def turn(c, i, half, order, table, now, rows, arrived, used, first):
                    g = i + c * TURNS
                    nc.gpsimd.tensor_copy(now[:, half], experts[:, c % 3, bass.ds(i * RING, RING)]).then_inc(
                        now_done, 1)
                    pool.wait_ge(now_done, order + (moved[0] + 1))
                    for r in range(RING):
                        if not first:
                            pool.wait_ge(used, (g - 1) * RING + r + 1)
                            pool.sem_inc(slot_free, 1)
                        nc.gpsimd.indirect_dma_start(
                            out=rows[:, r], out_offset=None, in_=table,
                            in_offset=bass.IndirectOffsetOnAxis(ap=now[:, half, r:r + 1], axis=0)).then_inc(
                                arrived[r], 16)

                u = (A["p_u"], now_u, u_rows, u_in, u_used)
                v = (A["p_v"], now_v, v_rows, v_in, v_used)
                moved = [0]

                def gather(*what):
                    first = any(c == 0 for c, _ in what)
                    n = len(what)
                    if first:
                        for half in range(2):
                            for o, (c, t) in enumerate(what):
                                turn(c, half, half, n * half + o, *t, c == 0 and half == 0)
                    with pool.Fori(1 if first else 0, TURNS // 2) as i:
                        for half in range(2):
                            for o, (c, t) in enumerate(what):
                                turn(c, i * 2 + half, half, i * (2 * n) + (n * half + o), *t, False)
                    moved[0] += n * TURNS

                pool.wait_ge(routed, 1)
                gather((0, u))
                for c in range(1, NCH):
                    pool.wait_ge(routed, c + 1)
                    gather((c, u), (c - 1, v))
                gather((NCH - 1, v))

            @block.tensor
            def _(pe):
                def scores(c):
                    if c:
                        pe.wait_ge(s_taken, c)
                    for h in range(HEADS_P):
                        for a in range(2):
                            hp = slice(64 * a, 64 * a + 64)
                            last = nc.tensor.matmul(ps_s[:, a, h], qT[hp, h, c * P:(c + 1) * P], keys[hp, :],
                                                    start=True, stop=True)
                            last.then_inc(s_mm, 1)

                def turn(c, i, first):
                    g = i + c * TURNS
                    for r in range(RING):
                        pe.wait_ge(v_in[r], 16 * (g + 1))
                        pe.wait_ge(diag_done, g * RING + r + 1)
                        for a in range(2):
                            last = nc.tensor.matmul(ps_y[:, c % 2, a], diag[:, r], v_rows[:, r, a * 512:(a + 1) * 512],
                                                    start=(first and r == 0), stop=False, skip_group_check=True)
                        last.then_inc(v_used, 1)

                def combine(c):
                    if c >= 2:
                        pe.wait_ge(y_taken, c - 1)
                    turn(c, 0, True)
                    with pe.Fori(1, TURNS) as i:
                        turn(c, i, False)
                    pe.wait_ge(v_used, (c + 1) * SLOTS)
                    pe.sem_inc(y_done, 1)

                scores(0)
                scores(1)
                for c in range(NCH):
                    if c + 2 < NCH:
                        scores(c + 2)
                    combine(c)

            @block.scalar
            def _(act):
                def take(c):
                    act.wait_ge(s_mm, 16 * (c + 1))
                    if c:
                        act.wait_ge(routed, c)
                    nc.scalar.activation(s[:], ps_s[:].rearrange("p a h n -> p (a h) n"), ACT.Copy).then_inc(s_taken, 1)

                def softmax(c):
                    act.wait_ge(arg_done, c + 1)
                    nc.scalar.activation(gate[:, c % 3], gate[:, c % 3], ACT.Exp).then_inc(exp_done, 1)

                def gelu(c):
                    act.wait_ge(dots_done, c + 1)
                    nc.scalar.activation(dots[:, c % 2], dots[:, c % 2], ACT.Gelu_apprx_tanh).then_inc(gelu_done, 1)

                def turn(c, i, first):
                    g = i + c * TURNS
                    for r in range(RING):
                        if not first:
                            act.wait_ge(v_used, (g - 1) * RING + r + 1)
                        nc.scalar.activation(diag[:, r], K.ident, ACT.Copy,
                                             scale=weight[:, c % 2, bass.ds(i * RING + r, 1)]).then_inc(diag_done, 1)

                def diags(c):
                    act.wait_ge(w_done, c + 1)
                    if c == 0:
                        turn(c, 0, True)
                    with act.Fori(1 if c == 0 else 0, TURNS) as i:
                        turn(c, i, False)
                    act.wait_ge(y_done, c + 1)
                    nc.scalar.activation(y_tok[:, c].rearrange("p (a n) -> p a n", a=2), ps_y[:, c % 2],
                                         ACT.Copy).then_inc(y_taken, 1)

                take(0)
                softmax(0)
                take(1)
                gelu(0)
                for c in range(NCH):
                    if c + 1 < NCH:
                        softmax(c + 1)
                    if c + 2 < NCH:
                        take(c + 2)
                    diags(c)
                    if c + 1 < NCH:
                        gelu(c + 1)

            @block.vector
            def _(dve):
                link = lambda ins: K.dve.link(dve, ins)

                def top16(vals, idx, src, lists):
                    def step(half, ls):
                        o = slice(8 * half, 8 * half + 8)
                        for l in ls:
                            ins = nc.vector.max(vals(l)[:, o], src(l))
                        link(ins)
                        for l in ls:
                            ins = nc.vector.max_index(idx(l)[:, o], vals(l)[:, o], src(l))
                            if half == 0:
                                ins = nc.vector.match_replace(src(l), vals(l)[:, o], src(l), -3.0e38)
                        link(ins)
                    size = lists // 4
                    return [lambda h=h, b=b: step(h, range(b * size, (b + 1) * size))
                            for b in range(4) for h in range(2)]

                shape = [P, HEADS_P, TOPK, TOPK]
                flat = cand[:].rearrange("p h a b -> p h (a b)")

                def pairs(c):
                    link(nc.vector.tensor_tensor(cand[:], bc(top[:, 0:HEADS_P].unsqueeze(3), shape),
                                                 bc(top[:, HEADS_P:].unsqueeze(2), shape), ALU.add))

                def rows_of(c):
                    if c >= 3:
                        dve.wait_ge(w_done, c - 2)
                    nc.vector.tensor_tensor(gate[:, c % 3], best[:], bc(best[:, :, 0:1], [P, HEADS_P, TOPK]),
                                            ALU.subtract).then_inc(arg_done, 1)
                    nc.vector.tensor_scalar(row_i[:, 0], best_i[:], 4, None, ALU.logical_shift_right)
                    link(nc.vector.tensor_scalar(row_i[:, 1], best_i[:], TOPK - 1, None, ALU.bitwise_and))
                    nc.vector.tensor_copy(row_f[:], row_i[:])
                    link(nc.vector.tensor_copy(top_f[:], top_i[:]))

                def expert_half(a):
                    link(nc.vector.tensor_tensor(hot[:], bc(row_f[:, a].unsqueeze(3), shape),
                                                 bc(iota.unsqueeze(1).unsqueeze(1), shape), ALU.is_equal))
                    link(nc.vector.tensor_tensor(hot[:], hot[:],
                                                 bc(top_f[:, a * HEADS_P:(a + 1) * HEADS_P].unsqueeze(2), shape),
                                                 ALU.mult))
                    link(nc.vector.tensor_reduce(pick[:, a], hot[:], AX, ALU.add))

                def expert(c):
                    if c >= 3:
                        dve.wait_ge(v_used, (c - 2) * SLOTS)
                    nc.vector.scalar_tensor_tensor(
                        out=experts[:, c % 3], in0=pick[:, 0].rearrange("p h k -> p (h k)"), scalar=float(NKEYS),
                        in1=pick[:, 1].rearrange("p h k -> p (h k)"), op0=ALU.mult, op1=ALU.add).then_inc(routed, 1)

                def route(c):
                    steps = [lambda: dve.wait_ge(s_taken, c + 1)]
                    steps += top16(lambda l: top[:, l], lambda l: top_i[:, l], lambda l: s[:, l], 2 * HEADS_P)
                    steps += [lambda: pairs(c)]
                    steps += top16(lambda l: best[:, l], lambda l: best_i[:, l], lambda l: flat[:, l], HEADS_P)
                    return steps + [lambda: rows_of(c), lambda: expert_half(0), lambda: expert_half(1),
                                    lambda: expert(c)]

                def gates(c):
                    dve.wait_ge(exp_done, c + 1)
                    g = gate[:, c % 3]
                    link(nc.vector.tensor_reduce(zsum[:], g, AX, ALU.add))
                    link(nc.vector.reciprocal(zsum[:], zsum[:]))
                    link(nc.vector.tensor_tensor(g, g, bc(zsum[:].unsqueeze(2), [P, HEADS_P, TOPK]), ALU.mult))

                def turn(c, i):
                    g = i + c * TURNS
                    for r in range(RING):
                        dve.wait_ge(u_in[r], 16 * (g + 1))
                        nc.vector.tensor_tensor_reduce(out=u_rows[:, r], in0=u_rows[:, r], in1=h_tok[:, c], scale=1.0,
                                                       scalar=0.0, op0=ALU.mult, op1=ALU.add,
                                                       accum_out=dot8[:, 0, r:r + 1]).then_inc(u_used, 1)
                    dve.wait_ge(u_used, (g + 1) * RING)
                    nc.vector.tensor_copy(dots[:, c % 2, bass.ts(i, RING)], dot8[:, 0]).then_inc(dot_moved, 1)
                    dve.wait_ge(dot_moved, g + 1)

                def weights(c):
                    gates(c)
                    dve.wait_ge(gelu_done, c + 1)
                    if c >= 2:
                        dve.wait_ge(diag_done, (c - 1) * SLOTS)
                    nc.vector.tensor_tensor(weight[:, c % 2], dots[:, c % 2],
                                            gate[:, c % 3].rearrange("p h k -> p (h k)"), ALU.mult).then_inc(w_done, 1)

                for step in route(0):
                    step()
                for c in range(NCH):
                    if c == NCH - 1:
                        with dve.Fori(0, TURNS) as i:
                            turn(c, i)
                    else:
                        steps = route(c + 1)
                        for i in range(TURNS):
                            turn(c, i)
                            a, b = (len(steps) * i // (TURNS - 1), len(steps) * (i + 1) // (TURNS - 1))
                            for step in steps[a:b]:
                                step()
                    dve.wait_ge(dot_moved, (c + 1) * TURNS)
                    dve.sem_inc(dots_done, 1)
                    weights(c)


def final_stage(nc, K, A):
    with ExitStack() as ctx:
        x3 = ctx.enter_context(nc.sbuf_tensor("fi_x3", [P, KD, T], F32))
        y = ctx.enter_context(nc.sbuf_tensor("fi_y", [P, KD, T], F32))
        y_tok = K.hT[:].rearrange("p k t -> p (k t)").rearrange("p (c d) -> p c d", c=NCH)
        x_in, t_done, t_taken, y_out = (K.sem("fi_" + x) for x in ("x_in", "t_done", "t_taken", "y_out"))
        with ExitStack() as c1:
            ps = c1.enter_context(nc.psum_tensor("fi_ps", [P, 2, 2, 512], F32))
            with nc.Block() as block:
                @block.sync
                def _(sp):
                    sp.dma_start(x3[:], A["x_scratch"]).then_inc(x_in, 16)

                @block.tensor
                def _(pe):
                    for c in range(NCH):
                        if c >= 2:
                            pe.wait_ge(t_taken, c - 1)
                        for k in range(KD):
                            last = nc.tensor.transpose(ps[:, c % 2, k // 4, (k % 4) * P:(k % 4 + 1) * P],
                                                       y_tok[:, c, k * P:(k + 1) * P], K.ident)
                        last.then_inc(t_done, 1)

                @block.vector
                def _(dve):
                    dve.wait_ge(x_in, 16)
                    for c in range(NCH):
                        dve.wait_ge(t_done, c + 1)
                        s = min(c, 1)
                        for k in range(KD):
                            xs = x3[:, k, c * P:(c + 1) * P]
                            ins = nc.vector.scalar_tensor_tensor(
                                out=xs, in0=ps[:, c % 2, k // 4, (k % 4) * P:(k % 4 + 1) * P],
                                scalar=K.mod[:, 5 * KD + k, s:s + 1], in1=xs, op0=ALU.mult, op1=ALU.add)
                        ins.then_inc(t_taken, 1)
        norm_stage(nc, K, A, 2, x3, y, "nf")
        with nc.Block() as block:
            @block.sync
            def _(sp):
                sp.dma_start(A["out_y"], y[:]).then_inc(y_out, 16)
                sp.wait_ge(y_out, 16)


STAGES = ["ada", "norm1", "hgrn", "hyena", "rwkv", "merge", "norm2", "peer", "final"]


def build(nc, A, upto="final", dump=None):
    with ExitStack() as ctx:
        K = Kern()

        def sb(name, shape, dt=F32):
            return ctx.enter_context(nc.sbuf_tensor(name, shape, dt))
        K.par = sb("par", [P, NPAR])
        K.con = sb("con", [P, NCONST])
        K.mod = sb("mod", [P, 48, 2])
        K.gain = sb("gain", [P, 2, KD, 2])
        K.lb = sb("lb", [P, 3, 8])
        K.hT = sb("hT", [P, KD, T])
        K.nc, K.taken = nc, []
        K.dve = Order(nc.alloc_semaphore("dve_order"))
        K.ident = K.con[:, CCOL["ident"]:CCOL["ident"] + P]
        K.ones = K.con[:, CCOL["ones"]:CCOL["ones"] + P]
        K.blk64 = K.con[:, CCOL["blk64"]:CCOL["blk64"] + P]
        load_stage(nc, K, A)
        K.end_stage()
        with ExitStack() as c2:
            K.xT = c2.enter_context(nc.sbuf_tensor("xT", [P, KD, T], F32))
            norm_stage(nc, K, A, 0, K.xT, K.hT, "n1", load=A["x"])
        with ExitStack() as c2:
            K.yT = [c2.enter_context(nc.sbuf_tensor(f"yT{b}", [P, 4, T], F32)) for b in range(3)]
            if "hgrn" in K_RUN:
                hgrn_stage(nc, K, A)
                K.end_stage()
            if "hyena" in K_RUN:
                hyena_stage(nc, K, A)
                K.end_stage()
            if "rwkv" in K_RUN:
                rwkv_stage(nc, K, A)
                K.end_stage()
            if dump is not None:
                dump(nc, K, A)
            if "merge" in K_RUN:
                merge_stage(nc, K, A)
                K.end_stage()
        if dump is not None:
            dump(nc, K, A)
        if "peer" in K_RUN:
            peer_stage(nc, K, A)
            K.end_stage()
            final_stage(nc, K, A)


K_RUN = {"hgrn", "hyena", "rwkv", "merge", "peer"}


def chan(v):
    v = np.asarray(v).reshape(-1)
    return v.reshape(-1, P).T


def host_consts():
    con = np.zeros((P, NCONST), np.float32)
    con[:, CCOL["ident"]:CCOL["ident"] + P] = np.eye(P)
    con[:, CCOL["ones"]:CCOL["ones"] + P] = 1.0
    con[:, CCOL["blk64"]:CCOL["blk64"] + P] = np.kron(np.eye(2), np.ones((64, 64)))
    tl = np.linspace(0.0, 1.0, LS, dtype=np.float32)
    con[:, CCOL["tneg"]] = -np.linspace(0.0, 1.0, LP, dtype=np.float32)
    for c in range(4):
        con[:, CCOL["tneg"] + 1 + c] = -tl[c * P:(c + 1) * P]
    con[:, CCOL["iota"]:CCOL["iota"] + TOPK] = np.arange(TOPK)
    s, t = np.meshgrid(np.arange(P), np.arange(P), indexing="ij")
    hg = np.zeros((P, 2, NL + 1, P), np.float32)
    for v, w in enumerate(LEVELS):
        same = (s // (2 * w)) == (t // (2 * w))
        hg[:, 0, v] = same & (s % (2 * w) < w) & (t % (2 * w) >= w)
        hg[:, 1, v] = same & (t % (2 * w) < w) & (s % (2 * w) >= w)
    hg[:, :, NL] = np.eye(P)[:, None]
    reset = np.ones((P, NCH, 129), np.float32)
    reset[:, :, 0] = 0.0
    return con, hg, reset.reshape(P, RESET_W)


def rwkv_masks():
    r, c = np.meshgrid(np.arange(P), np.arange(P), indexing="ij")
    m = np.zeros((P, 2, KINDS, P), np.float32)
    for d, before in enumerate((r < c, r > c)):
        m[:, d, LBT] = m[:, d, LKT] = before
        m[:, d, MBR] = m[:, d, MKR] = before | (r == c)
        m[:, d, LB] = before.T
    b = np.zeros((P, 4, P), np.float32)
    b[:, 0] = (r // 16) == (c // 16)
    for i, w in enumerate((16, 32, 64)):
        b[:, 1 + i] = ((r // (2 * w)) == (c // (2 * w))) & ((r // w) != (c // w))
    return m, b


def dft_tables(L):
    t, k = np.arange(L), np.arange(L)
    ang = np.pi / (2 * L) * ((np.outer(t, 2 * k + 1)) % (4 * L))
    tab = np.stack([np.cos(ang), np.sin(ang)], 1).astype(np.float32)
    n = L // P
    fwd = tab.reshape(n, P, 2, L).transpose(1, 0, 2, 3)
    inv = tab.transpose(2, 1, 0).reshape(n, P, 2, L).transpose(1, 0, 2, 3)
    return fwd, inv


def filter_features(L):
    f = np.float32
    t = np.linspace(0.0, 1.0, L, dtype=f)[:, None]
    bands = np.linspace(1e-4, BANDS - 1, BANDS, dtype=f)[None, :]
    ang = (f(2 * math.pi / L) * np.arange(L, dtype=f))[:, None] * bands
    return np.concatenate([t, np.cos(ang), -np.sin(ang)], axis=1).astype(f).T


def layout(inputs):
    g = {k: np.asarray(v) for k, v in inputs.items()}
    con, hg, reset = host_consts()
    pad64 = lambda v: np.concatenate([np.asarray(v).reshape(64, 1), np.zeros((64, 1), np.float32)])
    par = np.concatenate([
        chan(g["b_ada"]), chan(g["norm1"]), chan(g["norm2"]), chan(g["final_norm"]), chan(g["hgrn_lb_logits"]),
        chan(g["hgrn_norm"]), chan(g["hy_conv_w"]), chan(g["hy_conv_b"]), chan(g["hy_bias"]), chan(g["rw_mu"]),
        chan(g["rw_w0"]), chan(g["rw_a0"]), chan(g["rw_kk"]), chan(g["rw_ka"]), chan(g["rw_rk"]),
        chan(g["rw_ln_g"]), chan(g["rw_ln_b"]), pad64(g["hy_b1"]), pad64(g["hy_freq1"]), pad64(g["hy_b2"]),
        pad64(g["hy_freq2"])], axis=1)
    x = np.concatenate([g["x_prompt"][0], g["x_sample"][0]])
    w_in = g["w_in"][0]
    tiles = w_in.reshape(KD, P, -1, P).transpose(2, 1, 0, 3)
    a = {
        "params": par, "consts": con, "hg_mask": hg, "reset": reset,
        "c": np.stack([g["c_ctx"], g["c"][0]], 1).reshape(KD, P, 2).transpose(1, 0, 2).reshape(P, 16),
        "w_ada": g["w_ada"][0].reshape(KD, P, 8, 768).transpose(2, 1, 0, 3).reshape(8, P, KD * 768),
        "x": x.T.reshape(KD, P, T).transpose(1, 0, 2),
        "w_in": tiles,
        "w_i": w_in[:, 1536:2048].reshape(KD, P, W).transpose(1, 0, 2),
        "state_hgrn": g["state_hgrn"][0, 0].reshape(8, P, DK).transpose(1, 0, 2),
    }
    rw_mask, rw_bmask = rwkv_masks()
    fwd, inv = dft_tables(LS)
    fwd_p, inv_p = dft_tables(LP)
    a.update({
        "fwd": fwd, "inv": inv, "fwd_p": fwd_p[:, 0], "inv_p": inv_p[:, 0],
        "zf": np.concatenate([filter_features(LP), filter_features(LS)], axis=1),
        "hy_w1": g["hy_w1"][0], "hy_w2": g["hy_w2"][0], "hy_w3": g["hy_w3"][0],
        "w_branch": g["w_branch"][0].reshape(3, KW, P, KD, P).transpose(3, 0, 2, 1, 4).reshape(24, P, KW, P),
        "w_out": g["w_out"][0].reshape(KD, P, KD, P).transpose(2, 1, 0, 3),
        "p_wq": g["p_wq"][0].reshape(KD, P, HEADS_P, P).transpose(2, 1, 0, 3),
        "p_keys": np.concatenate([g["p_key1"][0].T, g["p_key2"][0].T]),
        "p_u": g["p_u"][0], "p_v": g["p_v"][0],
        "rw_w2": g["rw_w2"].reshape(P, W), "rw_a2": g["rw_a2"].reshape(P, W), "rw_g2": g["rw_g2"][0],
        "rw_mask": rw_mask, "rw_bmask": rw_bmask,
        "state_rwkv": g["state_rwkv"][0, 0].transpose(0, 1, 3, 2).reshape(8, P, HD).transpose(1, 0, 2),
        "delta": np.broadcast_to(g["hy_delta"], (P, W)),
    })
    return {k: np.ascontiguousarray(v, dtype=v.dtype) for k, v in a.items()}


SCRATCH = {"x_scratch": (P, KD, T), "y_scratch": (2, P, KW, T), "gate_scratch": (len(GATES), P, T)}
OUTS = {"out_hgrn": (8, P, DK), "out_rwkv": (8, P, HD), "out_y": (P, KD, T)}


def kernel(**inputs):
    import concourse.bacc as bacc
    from concourse.bass_utils import run_bass_kernel_spmd

    nc = bacc.Bacc("TRN2", target_bir_lowering=False, num_devices=1)
    arrays = layout(inputs)
    A = {k: nc.dram_tensor("in_" + k, v.shape, mybir.dt.from_np(v.dtype), kind="ExternalInput").ap()
         for k, v in arrays.items()}
    for k, s in OUTS.items():
        A[k] = nc.dram_tensor(k, s, F32, kind="ExternalOutput").ap()
    for k, s in SCRATCH.items():
        A[k] = nc.dram_tensor(k, s, F32, kind="Internal").ap()
    build(nc, A)
    r = run_bass_kernel_spmd(nc, [{"in_" + k: v for k, v in arrays.items()}], core_ids=[0]).results[0]
    y = r["out_y"].transpose(1, 0, 2).reshape(D, T).T
    return (np.ascontiguousarray(y[None, :LP]), np.ascontiguousarray(y[None, LP:]),
            r["out_hgrn"].reshape(1, 1, 2, HEADS_A, DK, DK),
            np.ascontiguousarray(r["out_rwkv"].reshape(2, 8, HD, HD).transpose(0, 1, 3, 2)[None, None]))
```

```python
import math
from contextlib import ExitStack

import numpy as np
import concourse.bass as bass
from concourse import mybir

F32 = mybir.dt.float32
I32 = mybir.dt.int32
U32 = mybir.dt.uint32
ALU = mybir.AluOpType
ACT = mybir.ActivationFunctionType
AX = mybir.AxisListType.X

P = 128
D = 1024
KD = D // P
LP, LS = 128, 512
T = LP + LS
NCH = T // P
HALF = T // 2
SEG = [(0, LP), (LP, T)]
GRID_W = 64
W = 512
KW = W // P
DK = 128
HEADS_A = 4
HD = 64
BANDS = 16
EMB = 1 + 2 * BANDS
FFN = 64
A_TILES, B_TILES, C_TILES = 20, 12, 15
G_TILE0 = A_TILES + B_TILES + C_TILES
HEADS_P, NKEYS, TOPK = 8, 128, 16
SLOTS = HEADS_P * TOPK
EPS = 1e-6
GN_EPS = 64e-5
LEVELS = [64, 32, 16, 8, 4, 2, 1]
NL = len(LEVELS)

PARAMS = [("b_ada", 48), ("norm1", 8), ("norm2", 8), ("final", 8), ("lb", 8), ("hgrn_norm", 1),
          ("conv_w", 36), ("conv_b", 12), ("hy_bias", 4), ("mu", 15), ("w0", 8), ("a0", 8), ("kk", 4),
          ("ka", 4), ("rk", 4), ("ln_g", 4), ("ln_b", 4), ("b1", 1), ("freq1", 1), ("b2", 1), ("freq2", 1)]
PCOL, _n = {}, 0
for _name, _w in PARAMS:
    PCOL[_name] = _n
    _n += _w
NPAR = _n
CONSTS = [("ident", P), ("ones", P), ("blk64", P), ("tneg", NCH), ("iota", TOPK)]
CCOL, _n = {}, 0
for _name, _w in CONSTS:
    CCOL[_name] = _n
    _n += _w
NCONST = _n
RESET_W = NCH * 129


EPSILONS = {"rms": EPS, "unit": 1e-12, "group": GN_EPS}


def rsqrt_log(K, out, x, scale, eps):
    col = list(EPSILONS).index(eps)
    return K.nc.scalar.activation(out, x, ACT.Ln, scale=scale, bias=K.eps[:, col:col + 1])


def rsqrt_exp(K, out):
    return K.nc.scalar.activation(out, out, ACT.Exp, scale=-0.5)


class Order:

    def __init__(self, sem):
        self.sem, self.n = sem, 0

    def link(self, eng, ins):
        ins.then_inc(self.sem, 1)
        self.n += 1
        eng.wait_ge(self.sem, self.n)


class Kern:

    def sem(self, name):
        self.taken.append(self.nc.alloc_semaphore(name))
        return self.taken[-1]

    def end_stage(self):
        self.nc.clear_and_free_semaphores(self.taken)
        self.nc.all_engine_barrier()
        self.taken = []


def bc(ap, shape):
    return ap.broadcast_to(shape)


def load_stage(nc, K, A):
    CH = 8
    CW = 6 * D // CH
    CP = CW // 2
    with ExitStack() as ctx:
        wt = ctx.enter_context(nc.sbuf_tensor("ada_w", [P, 3, KD * CW], F32))
        cT = ctx.enter_context(nc.sbuf_tensor("ada_c", [P, KD * 2], F32))
        sc = ctx.enter_context(nc.sbuf_tensor("ada_silu", [P, KD * 2], F32))
        rows = ctx.enter_context(nc.sbuf_tensor("ada_rows", [2, 6 * D], F32))
        ps_r = ctx.enter_context(nc.psum_tensor("ada_psr", [2, 4, 512], F32))
        ps = ctx.enter_context(nc.psum_tensor("ada_ps", [P, 512], F32))
        c_in, silu_done, ada_used, row_taken, turned, mod_done = (K.sem(x) for x in (
            "c_in", "silu_done", "ada_used", "row_taken", "turned", "mod_done"))
        w_in = [K.sem(f"ada_in{i}") for i in range(3)]
        params_in = K.sem("params_in")
        with nc.Block() as block:
            @block.sync
            def _(sp):
                sp.dma_start(cT[:], A["c"]).then_inc(c_in, 16)
                for i in range(CH):
                    if i == 3:
                        sp.dma_start(K.par[:], A["params"]).then_inc(params_in, 16)
                        sp.dma_start(K.con[:], A["consts"]).then_inc(params_in, 16)
                    if i >= 3:
                        sp.wait_ge(ada_used, 2 * (i - 2))
                    sp.dma_start(wt[:, i % 3, :], A["w_ada"][i]).then_inc(w_in[i % 3], 16)
                sp.wait_ge(params_in, 32)

            @block.scalar
            def _(act):
                act.wait_ge(c_in, 16)
                nc.scalar.activation(sc[:], cT[:], ACT.Silu).then_inc(silu_done, 1)
                for n in range(2 * CH):
                    act.wait_ge(ada_used, n + 1)
                    nc.scalar.activation(rows[:, n * CP:(n + 1) * CP], ps_r[:, n % 4, 0:CP],
                                         ACT.Copy).then_inc(row_taken, 1)

            @block.tensor
            def _(pe):
                pe.wait_ge(silu_done, 1)
                for n in range(2 * CH):
                    i = n // 2
                    if n % 2 == 0:
                        pe.wait_ge(w_in[i % 3], 16 * (i // 3 + 1))
                    if n >= 4:
                        pe.wait_ge(row_taken, n - 3)
                    for k in range(KD):
                        o = k * CW + (n % 2) * CP
                        last = nc.tensor.matmul(ps_r[:, n % 4, 0:CP], sc[:, 2 * k:2 * k + 2], wt[:, i % 3, o:o + CP],
                                                start=(k == 0), stop=(k == KD - 1))
                    last.then_inc(ada_used, 1)
                pe.wait_ge(params_in, 32)
                pe.wait_ge(row_taken, 2 * CH)
                for m in range(48):
                    last = nc.tensor.transpose(ps[:, 2 * m:2 * m + 2], rows[:, m * P:(m + 1) * P], K.ident[0:2, 0:2])
                last.then_inc(turned, 1)

            @block.vector
            def _(dve):
                dve.wait_ge(turned, 1)
                dve.wait_ge(params_in, 32)
                b = K.par[:, PCOL["b_ada"]:PCOL["b_ada"] + 48]
                K.dve.link(dve, nc.vector.tensor_tensor(K.mod[:], ps[:, 0:96].rearrange("p (m s) -> p m s", s=2),
                                                        bc(b.unsqueeze(2), [P, 48, 2]), ALU.add))
                for n, part, name in ((0, 1, "norm1"), (1, 4, "norm2")):
                    g = K.par[:, PCOL[name]:PCOL[name] + KD]
                    K.dve.link(dve, nc.vector.scalar_tensor_tensor(
                        out=K.gain[:, n], in0=K.mod[:, part * KD:(part + 1) * KD, :], scalar=1.0,
                        in1=bc(g.unsqueeze(2), [P, KD, 2]), op0=ALU.add, op1=ALU.mult))
                lg = K.par[:, PCOL["lb"]:PCOL["lb"] + 8]
                K.dve.link(dve, nc.vector.tensor_tensor(K.lb[:, 0], lg, lg, ALU.subtract))
                nc.vector.memset(K.lb[:, 2], 0.0).then_inc(mod_done, 1)
                for i, value in enumerate(EPSILONS.values()):
                    nc.vector.memset(K.eps[:, i:i + 1], value)

        sm = [K.sem(f"lb_step{i}") for i in range(2)]
        with nc.Block() as block:
            @block.scalar
            def _(act):
                nc.scalar.activation(K.lb[:, 1], K.lb[:, 0], ACT.Exp).then_inc(sm[0], 1)

            @block.vector
            def _(dve):
                dve.wait_ge(sm[0], 1)
                K.dve.link(dve, nc.vector.reciprocal(K.lb[:, 0], K.lb[:, 1]))
                K.dve.link(dve, nc.vector.tensor_tensor(K.lb[:, 1], K.lb[:, 1], K.lb[:, 0], ALU.mult))
                K.dve.link(dve, nc.vector.tensor_tensor(K.lb[:, 0], K.lb[:, 1], K.lb[:, 1], ALU.subtract))
                K.dve.link(dve, nc.vector.tensor_scalar(K.lb[:, 1], K.lb[:, 0], -1.0, 1.0, ALU.mult, ALU.add))


def norm_stage(nc, K, A, n, src, dst, name, load=None, store=None):
    with ExitStack() as ctx:
        sq = ctx.enter_context(nc.sbuf_tensor(name + "_sq", [P, KD, T], F32))
        rstd = ctx.enter_context(nc.sbuf_tensor(name + "_rstd", [P, T], F32))
        ps = ctx.enter_context(nc.psum_tensor(name + "_ps", [P, 2, 512], F32))
        x_in, sq_done, sum_done, log_done, root_done, scaled, stored = (K.sem(name + x) for x in (
            "_x_in", "_sq_done", "_sum_done", "_log_done", "_root_done", "_scaled", "_stored"))
        with nc.Block() as block:
            @block.sync
            def _(sp):
                if load is not None:
                    sp.dma_start(src[:], load).then_inc(x_in, 16)
                if store is not None:
                    sp.dma_start(store, src[:]).then_inc(stored, 16)
                    sp.wait_ge(stored, 16)
                if n == 2:
                    for k in range(KD):
                        sp.wait_ge(scaled, k + 1)
                        sp.dma_start(A["out_y"][:, k], dst[:, k]).then_inc(stored, 16)
                    sp.wait_ge(stored, 16 * KD)

            @block.scalar
            def _(act):
                if load is not None:
                    act.wait_ge(x_in, 16)
                for k in range(KD):
                    nc.scalar.activation(sq[:, k], src[:, k], ACT.Square).then_inc(sq_done, 1)
                act.wait_ge(sum_done, 1)
                rsqrt_log(K, halves(rstd[:]), ps[:, :, 0:HALF], 1.0 / D, "rms").then_inc(log_done, 1)
                act.wait_ge(log_done, 1)
                rsqrt_exp(K, rstd[:]).then_inc(root_done, 1)
                if n < 2:
                    for k in range(KD):
                        act.wait_ge(scaled, k + 1)
                        for s, (a, b) in enumerate(SEG):
                            shift = K.mod[:, (0, 3)[n] * KD + k, s:s + 1]
                            nc.scalar.activation(dst[:, k, a:b], dst[:, k, a:b], ACT.Identity, bias=shift)

            @block.tensor
            def _(pe):
                for k in range(KD):
                    pe.wait_ge(sq_done, k + 1)
                    for c in range(2):
                        last = nc.tensor.matmul(ps[:, c, 0:HALF], K.ones, sq[:, k, c * HALF:(c + 1) * HALF],
                                                start=(k == 0), stop=(k == KD - 1))
                last.then_inc(sum_done, 1)

            @block.vector
            def _(dve):
                dve.wait_ge(root_done, 1)
                for k in range(KD):
                    if n == 2:
                        pieces = [(0, T, K.par[:, PCOL["final"] + k:PCOL["final"] + k + 1])]
                    else:
                        pieces = [(a, b, K.gain[:, n, k, s:s + 1]) for s, (a, b) in enumerate(SEG)]
                    for a, b, g in pieces:
                        ins = nc.vector.scalar_tensor_tensor(out=dst[:, k, a:b], in0=src[:, k, a:b], scalar=g,
                                                             in1=rstd[:, a:b], op0=ALU.mult, op1=ALU.mult)
                    ins.then_inc(scaled, 1)


class Projection:
    RING, BANKS = 4, 2

    def __init__(self, nc, ctx, K, A, name, tiles, array="w_in"):
        self.array = array
        self.nc, self.K, self.A, self.tiles = nc, K, A, tiles
        self.w = ctx.enter_context(nc.sbuf_tensor(name + "_w", [P, self.RING, KD, P], F32))
        self.ps = ctx.enter_context(nc.psum_tensor(name + "_ps", [P, self.BANKS, 2, 512], F32))
        self.w_in = [K.sem(f"{name}_w_in{i}") for i in range(self.RING)]
        self.proj_done = K.sem(name + "_proj_done")
        self.proj_taken = K.sem(name + "_proj_taken")

    def load(self, sp, i):
        if i >= self.RING:
            sp.wait_ge(self.proj_done, i - self.RING + 1)
        sp.dma_start(self.w[:, i % self.RING], self.A[self.array][self.tiles[i]]).then_inc(
            self.w_in[i % self.RING], 16)

    def mm(self, pe, i):
        nc = self.nc
        pe.wait_ge(self.w_in[i % self.RING], 16 * (i // self.RING + 1))
        if i >= self.BANKS:
            pe.wait_ge(self.proj_taken, i - self.BANKS + 1)
        for k in range(KD):
            for c in range(2):
                last = nc.tensor.matmul(self.ps[:, i % self.BANKS, c, 0:HALF], self.w[:, i % self.RING, k],
                                        self.K.hT[:, k, c * HALF:(c + 1) * HALF],
                                        start=(k == 0), stop=(k == KD - 1))
        last.then_inc(self.proj_done, 1)

    def out(self, i):
        return self.ps[:, i % self.BANKS, :, 0:HALF]


def halves(ap):
    return ap.rearrange("p (c n) -> p c n", c=2)


HY_AHEAD = 10


def hyena_raw(K, i):
    return K.yT[1 + i // 4][:, i % 4] if i < 8 else K.raw[:, i - 8]


def hgrn_stage(nc, K, A):
    with ExitStack() as ctx:
        def sb(name, shape):
            return ctx.enter_context(nc.sbuf_tensor("hg_" + name, shape, F32))

        def sem(name):
            return K.sem("hg_" + name)
        qT = sb("q", [P, 4, T])
        fT = sb("f", [P, 8, T])
        gT = sb("g", [P, 4, T])
        i_tok = sb("i", [P, NCH, W])
        with ExitStack() as pctx:
            pr = Projection(nc, pctx, K, A, "hg", [t for t in range(A_TILES) if not 12 <= t < 16])
            w_i = pctx.enter_context(nc.sbuf_tensor("hg_wi", [P, KD, W], F32))
            ps_i = pctx.enter_context(nc.psum_tensor("hg_psi", [P, 2, W], F32))
            wi_in, i_done, i_taken = sem("wi_in"), sem("i_done"), sem("i_taken")
            NT = len(pr.tiles)
            with nc.Block() as block:
                @block.sync
                def _(sp):
                    for i in range(NT):
                        pr.load(sp, i)
                        if i == 3:
                            sp.dma_start(w_i[:], A["w_i"]).then_inc(wi_in, 16)

                @block.tensor
                def _(pe):
                    for i in range(NT):
                        pr.mm(pe, i)
                    pe.wait_ge(wi_in, 16)
                    for c in range(NCH):
                        if c >= 2:
                            pe.wait_ge(i_taken, c - 1)
                        for k in range(KD):
                            last = nc.tensor.matmul(ps_i[:, c % 2], K.hT[:, k, c * P:(c + 1) * P], w_i[:, k],
                                                    start=(k == 0), stop=(k == KD - 1))
                        last.then_inc(i_done, 1)

                @block.scalar
                def _(act):
                    for i in range(NT):
                        act.wait_ge(pr.proj_done, i + 1)
                        if i < 4:
                            dst, fn = qT[:, i], ACT.Silu
                        elif i < 12:
                            dst, fn = fT[:, i - 4], ACT.Sigmoid
                        else:
                            dst, fn = gT[:, i - 12], ACT.Silu
                        nc.scalar.activation(halves(dst), pr.out(i), fn).then_inc(pr.proj_taken, 1)

                @block.vector
                def _(dve):
                    for c in range(NCH):
                        dve.wait_ge(i_done, c + 1)
                        nc.vector.tensor_copy(i_tok[:, c], ps_i[:, c % 2]).then_inc(i_taken, 1)

        NE = NL + 2
        mask = sb("mask", [P, 2, NL + 1, P])
        reset = sb("reset", [P, RESET_W])
        lf = sb("lf", [P, RESET_W])
        cum = sb("cum", [P, RESET_W])
        kT = sb("k", [P, 2, NCH, P])
        E = sb("E", [P, 2, NE, NCH, P])
        dec = sb("dec", [P, 2, NCH])
        att = sb("att", [P, 2, NL + 1, P])
        khat = sb("khat", [P, 2, NCH, P])
        S = sb("S", [P, 3, DK])
        S_in = sb("S_in", [P, 8, DK])
        ps_s = ctx.enter_context(nc.psum_tensor("hg_pss", [P, 2, NL + 1, P], F32))
        ps_t = ctx.enter_context(nc.psum_tensor("hg_pst", [P, 1024], F32))
        ps_o = ctx.enter_context(nc.psum_tensor("hg_pso", [P, 512], F32))
        ps_d = ps_t[:, 6 * P:7 * P]
        ps_y = ctx.enter_context(nc.psum_tensor("hg_psy", [P, 512], F32))
        hy_w = sb("hy_w", [P, 2, KD, P])
        hy_in = [sem(f"hy_in{i}") for i in range(2)]
        hy_mm, hy_taken = sem("hy_mm"), sem("hy_taken")
        (const_in, s_in, logs, dec_sub, exp_done, x_ready, s_done, att_ready, tr_done, khat_ready, o_done, o_taken,
         ds_done, st_ready, st_out, f_ready, cum_done) = (sem(x) for x in (
             "const_in", "s_in", "logs", "dec_sub", "exp_done", "x_ready", "s_done", "att_ready", "tr_done",
             "khat_ready", "o_done", "o_taken", "ds_done", "st_ready", "st_out", "f_ready", "cum_done"))
        cumv = cum[:].rearrange("p (c t) -> p c t", t=129)
        lfv = lf[:].rearrange("p (c t) -> p c t", t=129)

        def order(d):
            return [0] + ([1, 2, 3, 4] if d == 0 else [4, 3, 2, 1])

        steps = [(g, g // 4, g % 4, c) for g in range(8) for c in order(g // 4)]
        with nc.Block() as block:
            @block.sync
            def _(sp):
                sp.dma_start(mask[:], A["hg_mask"]).then_inc(const_in, 16)
                sp.dma_start(reset[:], A["reset"]).then_inc(const_in, 16)
                sp.dma_start(S_in[:], A["state_hgrn"]).then_inc(s_in, 16)

                def hyena_load(i):
                    if i >= 2:
                        sp.wait_ge(hy_mm, 2 * (i - 1))
                    sp.dma_start(hy_w[:, i % 2], A["w_in"][A_TILES + i]).then_inc(hy_in[i % 2], 16)

                for i in range(4):
                    hyena_load(i)
                for g in range(8):
                    sp.wait_ge(st_ready, 4 * g + 1)
                    sp.dma_start(A["out_hgrn"][g], S[:, 0]).then_inc(st_out, 16)
                    if 4 + g < HY_AHEAD:
                        hyena_load(4 + g)
                sp.wait_ge(st_out, 16 * 8)

            @block.scalar
            def _(act):
                def take_hyena(n):
                    i, c = n // 2, n % 2
                    act.wait_ge(hy_mm, n + 1)
                    nc.scalar.activation(hyena_raw(K, i)[:, c * HALF:(c + 1) * HALF], ps_y[:, 0:HALF],
                                         ACT.Copy).then_inc(hy_taken, 1)

                for g in range(8):
                    act.wait_ge(f_ready, g + 1)
                    if g >= 1:
                        act.wait_ge(cum_done, g)
                    nc.scalar.activation(lfv[:, :, 1:129], fT[:, g].rearrange("p (c t) -> p c t", t=P),
                                         ACT.Ln).then_inc(logs, 1)
                    take_hyena(0 if g == 0 else 2 + 2 * g)
                    act.wait_ge(dec_sub, 2 * g + 1)
                    nc.scalar.activation(E[:, g % 2, 0:4], E[:, g % 2, 0:4], ACT.Exp).then_inc(exp_done, 1)
                    act.wait_ge(dec_sub, 2 * g + 2)
                    nc.scalar.activation(dec[:, g % 2], cumv[:, :, 128], ACT.Exp)
                    nc.scalar.activation(E[:, g % 2, 4:NE], E[:, g % 2, 4:NE], ACT.Exp).then_inc(exp_done, 1)
                    for n in (range(1, 4) if g == 0 else [3 + 2 * g]):
                        take_hyena(n)
                    act.wait_ge(tr_done, g + 1)
                    nc.scalar.activation(khat[:, g % 2], ps_t[:, 0:T].rearrange("p (c t) -> p c t", t=P),
                                         ACT.Copy).then_inc(khat_ready, 1)
                for n in range(18, 20):
                    take_hyena(n)

            @block.tensor
            def _(pe):
                def hyena(n, first, end):
                    i, c = n // 2, n % 2
                    for k in range(first, end):
                        if k == 0:
                            if c == 0:
                                pe.wait_ge(hy_in[i % 2], 16 * (i // 2 + 1))
                            if n:
                                pe.wait_ge(hy_taken, n)
                        last = nc.tensor.matmul(ps_y[:, 0:HALF], hy_w[:, i % 2, k],
                                                K.hT[:, k, c * HALF:(c + 1) * HALF],
                                                start=(k == 0), stop=(k == KD - 1))
                    if end == KD:
                        last.then_inc(hy_mm, 1)

                HYENA_SHARE = [(0, 0, 8), (1, 0, 2), (1, 2, 4), (1, 4, 6), (1, 6, 8)]

                def scores(n):
                    g, d, h, c = steps[n]
                    b = g % 2
                    if n % NCH == 0:
                        pe.wait_ge(x_ready, g + 1)
                        if g >= 1:
                            pe.wait_ge(khat_ready, g)
                        for cc in range(NCH):
                            last = nc.tensor.transpose(ps_t[:, cc * P:(cc + 1) * P], E[:, b, NL + 1, cc], K.ident)
                        last.then_inc(tr_done, 1)
                    if n >= 2:
                        pe.wait_ge(att_ready, n - 1)
                    for v in range(NL):
                        nc.tensor.matmul(ps_s[:, n % 2, v], E[:, b, v, c], E[:, b, v, c], start=True, stop=True)
                    nc.tensor.matmul(ps_s[:, n % 2, NL], kT[:, b, c], qT[:, h, c * P:(c + 1) * P],
                                     start=True, stop=True).then_inc(s_done, 1)

                def outputs(n):
                    g, d, h, c = steps[n]
                    b = g % 2
                    iv = i_tok[:, c, h * P:(h + 1) * P]
                    half, a, z = HYENA_SHARE[n % NCH]
                    if n % NCH == 0:
                        hyena(4 + 2 * g + half, a, z)
                    pe.wait_ge(khat_ready, g + 1)
                    if n % NCH != NCH - 1:
                        if n >= 1:
                            pe.wait_ge(st_ready, 4 * g + n % NCH)
                        nc.tensor.matmul(ps_d[:, 0:P], khat[:, b, c], iv, start=True, stop=True).then_inc(ds_done, 1)
                    if n % NCH:
                        hyena(4 + 2 * g + half, a, z)
                    pe.wait_ge(att_ready, n + 1)
                    if n >= 1:
                        pe.wait_ge(o_taken, n)
                    first = n % NCH == 0
                    for v in range(NL + 1):
                        last = nc.tensor.matmul(ps_o[:, 0:P], iv, att[:, n % 2, v], start=(v == 0),
                                                stop=(v == NL and first))
                    if not first:
                        k = n % NCH
                        if k == 1:
                            pe.wait_ge(s_in, 16)
                            src = S_in[:, g]
                        else:
                            pe.wait_ge(st_ready, 4 * g + k)
                            src = S[:, 1 + k % 2]
                        last = nc.tensor.matmul(ps_o[:, 0:P], src, E[:, b, NL, c], start=False, stop=True)
                    last.then_inc(o_done, 1)

                for n in range(4):
                    hyena(n, 0, KD)
                scores(0)
                for n in range(len(steps)):
                    if n + 1 < len(steps) and (n + 1) % NCH:
                        scores(n + 1)
                    outputs(n)
                    if n + 1 < len(steps) and (n + 1) % NCH == 0:
                        scores(n + 1)

            @block.vector
            def _(dve):
                link = lambda ins: K.dve.link(dve, ins)
                nc.vector.memset(lfv[:, :, 0:1], 0.0)
                dve.wait_ge(const_in, 32)

                def prepare(g):
                    d, h, b = g // 4, g % 4, g % 2
                    inc, exc = cumv[:, :, 1:129], cumv[:, :, 0:128]
                    q = qT[:, h].rearrange("p (c t) -> p c t", t=P)
                    lo, hi = (kT[:, b], q) if d == 0 else (q, kT[:, b])

                    def gates():
                        link(nc.vector.tensor_scalar(fT[:, g], fT[:, g], K.lb[:, 1, g:g + 1], K.lb[:, 0, g:g + 1],
                                                     ALU.mult, ALU.add))
                        if g >= 2:
                            dve.wait_ge(o_done, NCH * (g - 1))
                        link(nc.vector.tensor_scalar(kT[:, b], fT[:, g].rearrange("p (c t) -> p c t", t=P), -1.0,
                                                     1.0, ALU.mult, ALU.add))
                        nc.vector.tensor_scalar(fT[:, g], fT[:, g], 2.0 ** -63, None, ALU.max).then_inc(f_ready, 1)

                    def sums():
                        dve.wait_ge(logs, g + 1)
                        if g >= 1:
                            dve.wait_ge(exp_done, 2 * g)
                        nc.vector.tensor_tensor_scan(cum[:], reset[:], lf[:], 0.0, ALU.mult, ALU.add).then_inc(
                            cum_done, 1)
                        dve.wait_ge(cum_done, g + 1)

                    def level(v):
                        w = LEVELS[v]
                        out = E[:, b, v].rearrange("p c (n t) -> p c n t", t=2 * w)
                        at = (inc if d == 0 else exc).rearrange("p c (n t) -> p c n t", t=2 * w)
                        mid = exc.rearrange("p c (n t) -> p c n t", t=2 * w)[:, :, :, w:w + 1]
                        mid = bc(mid, [P, NCH, 64 // w, w])
                        L, R = slice(0, w), slice(w, 2 * w)
                        nc.vector.tensor_tensor(out[:, :, :, L], mid, at[:, :, :, L], ALU.subtract)
                        ins = nc.vector.tensor_tensor(out[:, :, :, R], at[:, :, :, R], mid, ALU.subtract)
                        if v == 3:
                            ins.then_inc(dec_sub, 1)

                    def to_ends():
                        zero = bc(cumv[:, :, 0:1], [P, NCH, P])
                        end = bc(cumv[:, :, 128:129], [P, NCH, P])
                        if d == 0:
                            nc.vector.tensor_tensor(E[:, b, NL], inc, zero, ALU.subtract)
                            nc.vector.tensor_tensor(E[:, b, NL + 1], end, inc, ALU.subtract).then_inc(dec_sub, 1)
                        else:
                            nc.vector.tensor_tensor(E[:, b, NL], end, exc, ALU.subtract)
                            nc.vector.tensor_tensor(E[:, b, NL + 1], exc, zero, ALU.subtract).then_inc(dec_sub, 1)

                    def scale(v):
                        w = LEVELS[v]
                        dve.wait_ge(exp_done, 2 * g + (1 if v < 4 else 2))
                        x = E[:, b, v].rearrange("p c (n t) -> p c n t", t=2 * w)
                        for src, s in ((lo, slice(0, w)), (hi, slice(w, 2 * w))):
                            y = src.rearrange("p c (n t) -> p c n t", t=2 * w)[:, :, :, s]
                            nc.vector.tensor_tensor(x[:, :, :, s], x[:, :, :, s], y, ALU.mult)

                    def scale_ends():
                        nc.vector.tensor_tensor(E[:, b, NL], E[:, b, NL], q, ALU.mult)
                        nc.vector.tensor_tensor(E[:, b, NL + 1], E[:, b, NL + 1], kT[:, b], ALU.mult).then_inc(
                            x_ready, 1)
                    return [[gates], [sums] + [lambda v=v: level(v) for v in range(4)],
                            [lambda v=v: level(v) for v in range(4, NL)] + [to_ends],
                            [lambda v=v: scale(v) for v in range(4)],
                            [lambda v=v: scale(v) for v in range(4, NL)] + [scale_ends]]

                def chunk(n, meanwhile):
                    g, d, h, c = steps[n]
                    dve.wait_ge(s_done, n + 1)
                    if n >= 2:
                        dve.wait_ge(o_done, n - 1)
                    nc.vector.tensor_tensor(att[:, n % 2], ps_s[:, n % 2], mask[:, d], ALU.mult).then_inc(att_ready, 1)
                    k = n % NCH
                    if k != NCH - 1:
                        dve.wait_ge(ds_done, 4 * g + k + 1)
                        if k == 0:
                            if g >= 1:
                                dve.wait_ge(st_out, 16 * g)
                            nc.vector.tensor_copy(S[:, 0], ps_d[:, 0:P]).then_inc(st_ready, 1)
                        else:
                            src = S_in[:, g] if k == 1 else S[:, 1 + k % 2]
                            if k == 1:
                                dve.wait_ge(s_in, 16)
                            else:
                                dve.wait_ge(st_ready, 4 * g + k)
                            if k == 3:
                                dve.wait_ge(o_done, n - 1)
                            nc.vector.scalar_tensor_tensor(
                                out=S[:, 1 + (k + 1) % 2], in0=src, scalar=dec[:, g % 2, c:c + 1], in1=ps_d[:, 0:P],
                                op0=ALU.mult, op1=ALU.add).then_inc(st_ready, 1)
                    for step in meanwhile:
                        step()
                    dve.wait_ge(o_done, n + 1)
                    o = K.yT[0][:, h, c * P:(c + 1) * P]
                    if d == 0:
                        nc.vector.tensor_copy(o, ps_o[:, 0:P]).then_inc(o_taken, 1)
                    else:
                        nc.vector.tensor_tensor(o, o, ps_o[:, 0:P], ALU.add).then_inc(o_taken, 1)

                for steps_of in prepare(0):
                    for step in steps_of:
                        step()
                for g in range(8):
                    ahead = prepare(g + 1) if g < 7 else [[]] * NCH
                    for k in range(NCH):
                        chunk(NCH * g + k, ahead[k])

        head_norm_stage(nc, K, K.yT[0], K.ones, 1.0 / DK, "hgn", gT, E[:, 0].rearrange("p e c t -> p (e c t)"),
                        ps_s[:].rearrange("p s v n -> p s (v n)").rearrange("p s (c n) -> p s c n", c=2))


def head_norm_stage(nc, K, y, sums, scale, name, gate, tmp, ps):
    sq = tmp[:, 0:4 * T].rearrange("p (h t) -> p h t", h=4)
    sq_done, sum_done, log_done, root_done = (K.sem(name + x) for x in (
        "_sq_done", "_sum_done", "_log_done", "_root_done"))
    rstd = sq
    with nc.Block() as block:
        @block.scalar
        def _(act):
            for h in range(4):
                nc.scalar.activation(sq[:, h], y[:, h], ACT.Square).then_inc(sq_done, 1)
            for h in range(4):
                act.wait_ge(sum_done, h + 1)
                rsqrt_log(K, halves(rstd[:, h]), ps[:, h % 2, :, 0:HALF], scale, "rms").then_inc(log_done, 1)
            for h in range(4):
                act.wait_ge(log_done, h + 1)
                rsqrt_exp(K, rstd[:, h]).then_inc(root_done, 1)

        @block.tensor
        def _(pe):
            for h in range(4):
                pe.wait_ge(sq_done, h + 1)
                if h >= 2:
                    pe.wait_ge(log_done, h - 1)
                for c in range(2):
                    last = nc.tensor.matmul(ps[:, h % 2, c, 0:HALF], sums, sq[:, h, c * HALF:(c + 1) * HALF],
                                            start=True, stop=True)
                last.then_inc(sum_done, 1)

        @block.vector
        def _(dve):
            for h in range(4):
                dve.wait_ge(root_done, h + 1)
                K.dve.link(dve, nc.vector.scalar_tensor_tensor(
                    out=y[:, h], in0=y[:, h], scalar=K.par[:, PCOL["hgrn_norm"]:PCOL["hgrn_norm"] + 1],
                    in1=rstd[:, h], op0=ALU.mult, op1=ALU.mult))
                K.dve.link(dve, nc.vector.tensor_tensor(y[:, h], y[:, h], gate[:, h], ALU.mult))


def tok0(c):
    return 1 if c == 0 else 2 + P * c


PADW = T + 3
SEQ_OF = [[0], [1, 2, 3, 4]]


def sin_steps(nc, K, dve, x, n, bias, freq):
    magic, c1 = 1.5 * 2.0 ** 23, 6.28125
    c2 = 2.0 * math.pi - c1
    pi = 3.1415925
    link = lambda ins: K.dve.link(dve, ins)
    link(nc.vector.tensor_scalar(x, x, bias, freq, ALU.add, ALU.mult))
    link(nc.vector.tensor_scalar(n, x, 1.0 / (2.0 * math.pi), magic, ALU.mult, ALU.add))
    link(nc.vector.tensor_scalar(n, n, -magic, None, ALU.add))
    link(nc.vector.scalar_tensor_tensor(out=x, in0=n, scalar=-c1, in1=x, op0=ALU.mult, op1=ALU.add))
    link(nc.vector.scalar_tensor_tensor(out=x, in0=n, scalar=-c2, in1=x, op0=ALU.mult, op1=ALU.add))
    return nc.vector.tensor_scalar(x, x, pi, -pi, ALU.min, ALU.max)


def hyena_stage(nc, K, A):
    with ExitStack() as ctx:
        def sb(name, shape):
            return ctx.enter_context(nc.sbuf_tensor("hy_" + name, shape, F32))

        def sem(name):
            return K.sem("hy_" + name)
        par = lambda name, i=0, rows=P: K.par[0:rows, PCOL[name] + i:PCOL[name] + i + 1]
        u = sb("u", [P, 12, PADW])
        z_tok = sb("z_tok", [P, NCH, W])
        with ExitStack() as c1:
            pr = Projection(nc, c1, K, A, "hy", list(range(A_TILES + HY_AHEAD, A_TILES + B_TILES)))
            padded = sem("padded")
            R = c1.enter_context(nc.sbuf_tensor("hy_raw", [P, 2, PADW], F32))
            ps_t = c1.enter_context(nc.psum_tensor("hy_pst", [P, 2, 512], F32))
            zeroed, conv, z_done, zt_done, zt_taken = (sem(x) for x in (
                "zeroed", "conv", "z_done", "zt_done", "zt_taken"))
            with nc.Block() as block:
                @block.sync
                def _(sp):
                    for i in range(B_TILES - HY_AHEAD):
                        pr.load(sp, i)

                @block.tensor
                def _(pe):
                    for i in range(B_TILES - HY_AHEAD):
                        pr.mm(pe, i)
                    pe.wait_ge(z_done, 1)
                    for c in range(NCH):
                        if c >= 2:
                            pe.wait_ge(zt_taken, c - 1)
                        for j in range(KW):
                            last = nc.tensor.transpose(ps_t[:, c % 2, j * P:(j + 1) * P],
                                                       u[:, 8 + j, tok0(c):tok0(c) + P], K.ident)
                        last.then_inc(zt_done, 1)

                @block.scalar
                def _(act):
                    act.wait_ge(zeroed, 1)
                    for i in range(12):
                        if i >= 2:
                            act.wait_ge(conv, i - 1)
                        b = i % 2
                        if i < HY_AHEAD:
                            o, taken = halves(hyena_raw(K, i)), padded
                        else:
                            act.wait_ge(pr.proj_done, i - HY_AHEAD + 1)
                            o, taken = pr.out(i - HY_AHEAD), pr.proj_taken
                        nc.scalar.activation(R[:, b, 1:1 + LP], o[:, 0, 0:LP], ACT.Copy)
                        nc.scalar.activation(R[:, b, 2 + LP:2 + HALF], o[:, 0, LP:HALF], ACT.Copy)
                        nc.scalar.activation(R[:, b, 2 + HALF:2 + T], o[:, 1], ACT.Copy).then_inc(taken, 1)
                    for c in range(NCH):
                        act.wait_ge(zt_done, c + 1)
                        nc.scalar.activation(z_tok[:, c], ps_t[:, c % 2], ACT.Copy).then_inc(zt_taken, 1)

                @block.vector
                def _(dve):
                    link = lambda ins: K.dve.link(dve, ins)
                    nc.vector.memset(R[:], 0.0).then_inc(zeroed, 1)
                    for i in range(12):
                        if i < HY_AHEAD:
                            dve.wait_ge(padded, i + 1)
                        else:
                            dve.wait_ge(pr.proj_taken, i - HY_AHEAD + 1)
                        b, uo = i % 2, u[:, i, 1:PADW - 1]
                        link(nc.vector.tensor_scalar(uo, R[:, b, 1:PADW - 1], par("conv_w", 12 + i), par("conv_b", i),
                                                     ALU.mult, ALU.add))
                        link(nc.vector.scalar_tensor_tensor(out=uo, in0=R[:, b, 0:PADW - 2], scalar=par("conv_w", i),
                                                            in1=uo, op0=ALU.mult, op1=ALU.add))
                        nc.vector.scalar_tensor_tensor(out=uo, in0=R[:, b, 2:PADW], scalar=par("conv_w", 24 + i),
                                                       in1=uo, op0=ALU.mult, op1=ALU.add).then_inc(conv, 1)
                    dve.wait_ge(conv, 12)
                    nc.vector.tensor_tensor(u[:, 8:12, 1:PADW - 1], u[:, 8:12, 1:PADW - 1], u[:, 4:8, 1:PADW - 1],
                                            ALU.mult).then_inc(z_done, 1)
        fwd = sb("fwd", [P, 4, 2, LS])
        inv = sb("inv", [P, 4, 2, LS])
        fwd_p = sb("fwd_p", [P, 2, LP])
        inv_p = sb("inv_p", [P, 2, LP])
        H = sb("H", [P, NCH, 2, W])
        G = sb("G", [P, NCH, 2, W])
        inorm = sb("inorm", [P, 2, W])
        tables_in = sem("tables_in")
        with ExitStack() as c1:
            def tb(name, shape):
                return c1.enter_context(nc.sbuf_tensor("hy_" + name, shape, F32))
            zf, w1, w2 = tb("zf", [EMB, T]), tb("w1", [EMB, FFN]), tb("w2", [FFN, FFN])
            w3, dl = tb("w3", [FFN, 2 * W]), tb("dl", [P, W])
            f1, f2, turns = tb("f1", [FFN, T]), tb("f2", [FFN, T]), tb("turns", [FFN, T])
            Et = tb("Et", [P, 2, W])
            ps_f = c1.enter_context(nc.psum_tensor("hy_psf", [P, 2, 512], F32))
            ps_h = c1.enter_context(nc.psum_tensor("hy_psh", [P, 2, 2, 512], F32))
            ps_n = c1.enter_context(nc.psum_tensor("hy_psn", [P, 2, 512], F32))
            f_in, ffn_mm, ffn_arg, ffn_act, dabs, env, hf_mm, hf_taken, abs_done, sums, zrow = (
                sem(x) for x in ("f_in", "ffn_mm", "ffn_arg", "ffn_act", "dabs", "env", "hf_mm", "hf_taken",
                                 "abs_done", "sums", "zrow"))
            with nc.Block() as block:
                @block.sync
                def _(sp):
                    for t, n in ((zf, "zf"), (w1, "hy_w1"), (w2, "hy_w2"), (w3, "hy_w3"), (dl, "delta")):
                        sp.dma_start(t[:], A[n]).then_inc(f_in, 16)
                    for t, n in ((fwd, "fwd"), (inv, "inv"), (fwd_p, "fwd_p"), (inv_p, "inv_p")):
                        sp.dma_start(t[:], A[n]).then_inc(tables_in, 16)
                    sp.wait_ge(tables_in, 64)

                @block.tensor
                def _(pe):
                    pe.wait_ge(f_in, 80)
                    for layer, (w, x) in enumerate(((w1, zf), (w2, f1))):
                        if layer:
                            pe.wait_ge(ffn_act, 1)
                        for c in range(2):
                            last = nc.tensor.matmul(ps_f[0:FFN, c, 0:HALF], w[:], x[:, c * HALF:(c + 1) * HALF],
                                                    start=True, stop=True)
                        last.then_inc(ffn_mm, 1)
                    pe.wait_ge(ffn_act, 2)
                    for c in range(NCH):
                        if c >= 2:
                            pe.wait_ge(hf_taken, c - 1)
                        for s in range(2):
                            last = nc.tensor.matmul(ps_h[:, c % 2, s], f2[:, c * P:(c + 1) * P],
                                                    w3[:, s * W:(s + 1) * W], start=True, stop=True)
                        last.then_inc(hf_mm, 1)
                    for q, chunks in enumerate(SEQ_OF):
                        for c in chunks:
                            pe.wait_ge(abs_done, c + 1)
                            for s in range(2):
                                last = nc.tensor.matmul(ps_n[:, q], K.ones, G[:, c, s],
                                                        start=(c == chunks[0] and s == 0),
                                                        stop=(c == chunks[-1] and s == 1))
                        last.then_inc(sums, 1)

                @block.scalar
                def _(act):
                    act.wait_ge(f_in, 80)
                    nc.scalar.activation(dl[:], dl[:], ACT.Abs).then_inc(dabs, 1)
                    for layer, f in enumerate((f1, f2)):
                        act.wait_ge(ffn_arg, layer + 1)
                        nc.scalar.activation(f[:], f[:], ACT.Sin).then_inc(ffn_act, 1)
                    act.wait_ge(dabs, 1)
                    for c in range(NCH):
                        if c >= 2:
                            act.wait_ge(hf_taken, c - 1)
                        tn = K.con[:, CCOL["tneg"] + c:CCOL["tneg"] + c + 1]
                        nc.scalar.activation(Et[:, c % 2], dl[:], ACT.Exp, scale=tn).then_inc(env, 1)
                    for c in range(NCH):
                        act.wait_ge(zrow, c + 1)
                        nc.scalar.activation(G[:, c], H[:, c], ACT.Abs).then_inc(abs_done, 1)

                @block.vector
                def _(dve):
                    link = lambda ins: K.dve.link(dve, ins)
                    for layer, f in enumerate((f1, f2)):
                        dve.wait_ge(ffn_mm, layer + 1)
                        link(nc.vector.tensor_copy(halves(f[:]), ps_f[0:FFN, :, 0:HALF]))
                        sin_steps(nc, K, dve, f[:], turns[:], par("b1" if layer == 0 else "b2", 0, FFN),
                                  par("freq1" if layer == 0 else "freq2", 0, FFN)).then_inc(ffn_arg, 1)
                    for c in range(NCH):
                        dve.wait_ge(hf_mm, c + 1)
                        dve.wait_ge(env, c + 1)
                        ins = nc.vector.tensor_tensor(H[:, c], ps_h[:, c % 2],
                                                      bc(Et[:, c % 2].unsqueeze(1), [P, 2, W]), ALU.mult)
                        ins.then_inc(hf_taken, 1)
                        dve.wait_ge(hf_taken, c + 1)
                        if c < 2:
                            nc.vector.memset(H[0:1, c, 1, :], 0.0).then_inc(zrow, 1)
                        else:
                            dve.sem_inc(zrow, 1)
                    dve.wait_ge(abs_done, NCH)
                    link(nc.vector.tensor_tensor(H[:, :, 0], H[:, :, 0], H[:, :, 1], ALU.add))
                    link(nc.vector.scalar_tensor_tensor(out=H[:, :, 1], in0=H[:, :, 1], scalar=2.0, in1=H[:, :, 0],
                                                        op0=ALU.mult, op1=ALU.subtract))
                    dve.wait_ge(sums, 2)
                    for q, L in enumerate((LP, LS)):
                        link(nc.vector.tensor_scalar(inorm[:, q], ps_n[:, q], float(L), None, ALU.mult))
                    link(nc.vector.reciprocal(inorm[:], inorm[:]))
        Z = sb("Z", [P, NCH, 2, W])
        t1 = sb("t1", [P, 2, W])
        with ExitStack() as c1:
            ps_k = c1.enter_context(nc.psum_tensor("hy_psk", [P, 2, 2, 512], F32))
            ps_z = c1.enter_context(nc.psum_tensor("hy_psz", [P, 2, 2, 512], F32))
            k_mm, k_taken, z_mm, z_taken, y_done, inv_mm, inv_taken = (sem(x) for x in (
                "k_mm", "k_taken", "z_mm", "z_taken", "y_done", "inv_mm", "inv_taken"))
            tiles = [(q, f) for q in range(2) for f in SEQ_OF[q]]
            with nc.Block() as block:
                @block.tensor
                def _(pe):
                    for n, (q, f) in enumerate(tiles):
                        for ps, src, mm, taken in ((ps_k, None, k_mm, k_taken), (ps_z, z_tok, z_mm, z_taken)):
                            if n >= 2:
                                pe.wait_ge(taken, n - 1)
                            for s in range(2):
                                chunks = SEQ_OF[q]
                                for c in chunks:
                                    tab = (fwd_p[:, s, :] if q == 0 else
                                           fwd[:, c - 1, s, (f - 1) * P:f * P])
                                    rhs = H[:, c, s] if src is None else src[:, c]
                                    last = nc.tensor.matmul(ps[:, n % 2, s], tab, rhs, start=(c == chunks[0]),
                                                            stop=(c == chunks[-1]))
                            last.then_inc(mm, 1)
                    pe.wait_ge(y_done, NCH)
                    n = 0
                    for j in range(KW):
                        for q in range(2):
                            if n >= 4:
                                pe.wait_ge(inv_taken, n - 3)
                            chunks = SEQ_OF[q]
                            L = LS if q else LP
                            for f in chunks:
                                for s in range(2):
                                    tab = inv_p[:, s] if q == 0 else inv[:, f - 1, s]
                                    last = nc.tensor.matmul(ps_k[:, (n // 2) % 2, n % 2, 0:L],
                                                            Z[:, f, s, j * P:(j + 1) * P], tab,
                                                            start=(f == chunks[0] and s == 0),
                                                            stop=(f == chunks[-1] and s == 1))
                            last.then_inc(inv_mm, 1)
                            n += 1

                @block.scalar
                def _(act):
                    for n, (q, f) in enumerate(tiles):
                        act.wait_ge(z_mm, n + 1)
                        nc.scalar.activation(Z[:, f], ps_z[:, n % 2], ACT.Copy).then_inc(z_taken, 1)

                @block.vector
                def _(dve):
                    link = lambda ins: K.dve.link(dve, ins)
                    for n, (q, f) in enumerate(tiles):
                        dve.wait_ge(k_mm, n + 1)
                        nc.vector.tensor_tensor(G[:, f], ps_k[:, n % 2],
                                                bc(inorm[:, q].unsqueeze(1), [P, 2, W]), ALU.mult).then_inc(k_taken, 1)
                        dve.wait_ge(z_taken, n + 1)
                        dve.wait_ge(k_taken, n + 1)
                        nc.vector.tensor_tensor(t1[:, 0], Z[:, f, 1], G[:, f, 1], ALU.mult)
                        link(nc.vector.tensor_tensor(t1[:, 1], Z[:, f, 0], G[:, f, 1], ALU.mult))
                        link(nc.vector.tensor_tensor(Z[:, f], Z[:, f], bc(G[:, f, 0:1], [P, 2, W]), ALU.mult))
                        nc.vector.tensor_tensor(Z[:, f, 0], Z[:, f, 0], t1[:, 0], ALU.add)
                        link(nc.vector.tensor_tensor(Z[:, f, 1], Z[:, f, 1], t1[:, 1], ALU.subtract))
                        dve.sem_inc(y_done, 1)
                    n = 0
                    for j in range(KW):
                        for q in range(2):
                            dve.wait_ge(inv_mm, n + 1)
                            a, b = SEG[q]
                            cols = slice(a + 1 + q, b + 1 + q)
                            y = K.yT[1][:, j, a:b]
                            nc.vector.scalar_tensor_tensor(
                                out=y, in0=u[:, 8 + j, cols], scalar=par("hy_bias", j),
                                in1=ps_k[:, (n // 2) % 2, n % 2, 0:b - a], op0=ALU.mult, op1=ALU.add).then_inc(inv_taken, 1)
                            dve.wait_ge(inv_taken, n + 1)
                            link(nc.vector.tensor_tensor(y, y, u[:, j, cols], ALU.mult))
                            n += 1


KINDS = 5
LBT, MBR, LKT, MKR, LB = range(KINDS)
KAPPA = -math.exp(-0.5)


MERGE_ORDER = [(m, b) for m in range(KD) for b in range(3)]
GATES = [G_TILE0 + KD * b + m for m, b in MERGE_ORDER]


class Uses:
    SLOTS = 3

    def __init__(self, K):
        self.sems = {"v": K.sem("rw_read_by_vector"), "s": K.sem("rw_read_by_scalar")}
        self.mm_done = K.sem("rw_mm_done")
        self.owner, self.value, self.index = [], [], {}
        self.count = {"v": 0, "s": 0}

    def add(self, key, owner):
        self.index[key] = len(self.owner)
        self.owner.append(owner)
        self.count[owner] += 1
        self.value.append(self.count[owner])

    def slot(self, key):
        return self.index[key] % self.SLOTS

    def wait_read(self, eng, key):
        n = self.index[key]
        eng.wait_ge(self.sems[self.owner[n]], self.value[n])

    def wait_free(self, pe, key):
        n = self.index[key] - self.SLOTS
        if n >= 0:
            pe.wait_ge(self.sems[self.owner[n]], self.value[n])

    def wait_mm(self, eng, key):
        eng.wait_ge(self.mm_done, self.index[key] + 1)

    def read(self, ins, key):
        ins.then_inc(self.sems[self.owner[self.index[key]]], 1)


def rwkv_stage(nc, K, A):
    with ExitStack() as ctx:
        def sb(name, shape):
            return ctx.enter_context(nc.sbuf_tensor("rw_" + name, shape, F32))

        def sem(name):
            return K.sem("rw_" + name)
        par = lambda name, i=0: K.par[:, PCOL[name] + i:PCOL[name] + i + 1]
        rT, kT, vT, kk = (sb(x, [P, 4, T]) for x in ("r", "k", "v", "kk"))
        v_tok = sb("v_tok", [P, NCH, W])
        lo = sb("lo", [P, 3, T])
        w2, a2 = (sb(x, [P, W]) for x in ("w2", "a2"))
        omka = sb("omka", [P, 4])
        ld_in = sem("ld_in")
        with ExitStack() as c1:
            pr = Projection(nc, c1, K, A, "rw", list(range(A_TILES + B_TILES, G_TILE0)))
            pp = c1.enter_context(nc.sbuf_tensor("rw_pp", [P, 2, LP + 2], F32))
            gp = c1.enter_context(nc.sbuf_tensor("rw_gp", [P, 2, 10, GRID_W + 2], F32))
            side = c1.enter_context(nc.sbuf_tensor("rw_side", [P, 2, LS], F32))
            zeroed, mixed, lo_act, y_out = sem("zeroed"), sem("mixed"), sem("lo_act"), sem("y_out")
            with nc.Block() as block:
                @block.sync
                def _(sp):
                    for b in range(2):
                        sp.dma_start(A["y_scratch"][b], K.yT[b][:]).then_inc(y_out, 16)
                    for i in range(C_TILES):
                        pr.load(sp, i)
                        if i == 3:
                            for t, n in ((w2, "rw_w2"), (a2, "rw_a2")):
                                sp.dma_start(t[:], A[n]).then_inc(ld_in, 16)
                    sp.wait_ge(y_out, 32)

                @block.tensor
                def _(pe):
                    for i in range(C_TILES):
                        pr.mm(pe, i)

                @block.scalar
                def _(act):
                    act.wait_ge(zeroed, 1)
                    for i in range(C_TILES):
                        act.wait_ge(pr.proj_done, i + 1)
                        if i >= 2:
                            act.wait_ge(mixed, i - 1)
                        b, o = i % 2, pr.out(i)
                        r0 = (HALF - LP) // GRID_W
                        nc.scalar.activation(pp[:, b, 1:1 + LP], o[:, 0, 0:LP], ACT.Copy)
                        nc.scalar.activation(gp[:, b, 1:1 + r0, 1:1 + GRID_W],
                                             o[:, 0, LP:HALF].rearrange("p (r c) -> p r c", c=GRID_W), ACT.Copy)
                        nc.scalar.activation(gp[:, b, 1 + r0:9, 1:1 + GRID_W],
                                             o[:, 1].rearrange("p (r c) -> p r c", c=GRID_W),
                                             ACT.Copy).then_inc(pr.proj_taken, 1)
                    act.wait_ge(mixed, C_TILES)
                    nc.scalar.activation(lo[:, 0], lo[:, 0], ACT.Tanh)
                    nc.scalar.activation(lo[:, 2], lo[:, 2], ACT.Sigmoid).then_inc(lo_act, 1)

                @block.vector
                def _(dve):
                    link = lambda ins: K.dve.link(dve, ins)
                    nc.vector.memset(pp[:], 0.0)
                    nc.vector.memset(gp[:], 0.0).then_inc(zeroed, 1)
                    for i in range(C_TILES):
                        dve.wait_ge(pr.proj_taken, i + 1)
                        b = i % 2
                        dst = (rT, kT, vT)[i // 4][:, i % 4] if i < 12 else lo[:, i - 12]
                        own_p, own_s = pp[:, b, 1:1 + LP], gp[:, b, 1:9, 1:1 + GRID_W]
                        dp, ds = dst[:, 0:LP], dst[:, LP:T].rearrange("p (r c) -> p r c", c=GRID_W)
                        sd = side[:, b].rearrange("p (r c) -> p r c", c=GRID_W)
                        nc.vector.tensor_tensor(dp, pp[:, b, 0:LP], pp[:, b, 2:LP + 2], ALU.add)
                        nc.vector.tensor_tensor(ds, gp[:, b, 0:8, 1:1 + GRID_W], gp[:, b, 2:10, 1:1 + GRID_W], ALU.add)
                        link(nc.vector.tensor_tensor(sd, gp[:, b, 1:9, 0:GRID_W], gp[:, b, 1:9, 2:2 + GRID_W], ALU.add))
                        nc.vector.scalar_tensor_tensor(out=dp, in0=dp, scalar=0.5, in1=own_p, op0=ALU.mult,
                                                       op1=ALU.subtract)
                        link(nc.vector.tensor_tensor(ds, ds, sd, ALU.add))
                        link(nc.vector.scalar_tensor_tensor(out=ds, in0=ds, scalar=0.25, in1=own_s, op0=ALU.mult,
                                                            op1=ALU.subtract))
                        nc.vector.scalar_tensor_tensor(out=dp, in0=dp, scalar=par("mu", i), in1=own_p,
                                                       op0=ALU.mult, op1=ALU.add)
                        nc.vector.scalar_tensor_tensor(out=ds, in0=ds, scalar=par("mu", i), in1=own_s,
                                                       op0=ALU.mult, op1=ALU.add).then_inc(mixed, 1)
        with ExitStack() as c1:
            sq = c1.enter_context(nc.sbuf_tensor("rw_sq", [P, 4, T], F32))
            ps = c1.enter_context(nc.psum_tensor("rw_ps0", [P, 2, 2, 512], F32))
            ps_t = c1.enter_context(nc.psum_tensor("rw_pst", [P, 2, 512], F32))
            kk_done, sq_done, sum_done, ms_done, root, v_done, v_taken = (sem(x) for x in (
                "kk_done", "sq_done", "sum_done", "ms_done", "root", "v_done", "v_taken"))
            with nc.Block() as block:
                @block.tensor
                def _(pe):
                    for j in range(4):
                        pe.wait_ge(sq_done, j + 1)
                        if j >= 2:
                            pe.wait_ge(ms_done, j - 1)
                        for c in range(2):
                            last = nc.tensor.matmul(ps[:, j % 2, c, 0:HALF], K.blk64,
                                                    sq[:, j, c * HALF:(c + 1) * HALF], start=True, stop=True)
                        last.then_inc(sum_done, 1)
                    for c in range(NCH):
                        if c >= 2:
                            pe.wait_ge(v_taken, c - 1)
                        for j in range(4):
                            last = nc.tensor.transpose(ps_t[:, c % 2, j * P:(j + 1) * P],
                                                       vT[:, j, c * P:(c + 1) * P], K.ident)
                        last.then_inc(v_done, 1)

                @block.scalar
                def _(act):
                    for j in range(4):
                        act.wait_ge(kk_done, j + 1)
                        nc.scalar.activation(sq[:, j], kk[:, j], ACT.Square).then_inc(sq_done, 1)
                    for j in range(4):
                        act.wait_ge(sum_done, j + 1)
                        rsqrt_log(K, halves(sq[:, j]), ps[:, j % 2, :, 0:HALF], 1.0, "unit").then_inc(ms_done, 1)
                    for j in range(4):
                        act.wait_ge(ms_done, j + 1)
                        rsqrt_exp(K, sq[:, j]).then_inc(root, 1)
                    for c in range(NCH):
                        act.wait_ge(v_done, c + 1)
                        nc.scalar.activation(v_tok[:, c], ps_t[:, c % 2], ACT.Copy).then_inc(v_taken, 1)

                @block.vector
                def _(dve):
                    link = lambda ins: K.dve.link(dve, ins)
                    for j in range(4):
                        nc.vector.tensor_scalar(kk[:, j], kT[:, j], par("kk", j), None, ALU.mult).then_inc(kk_done, 1)
                    nc.vector.tensor_scalar(omka[:], K.par[:, PCOL["ka"]:PCOL["ka"] + 4], -1.0, 1.0, ALU.mult, ALU.add)
                    for j in range(4):
                        dve.wait_ge(root, j + 1)
                        link(nc.vector.tensor_tensor(kk[:, j], kk[:, j], sq[:, j], ALU.mult))
        with ExitStack() as c1:
            def wb(name, shape):
                return c1.enter_context(nc.sbuf_tensor("rw_" + name, shape, F32))
            mask = wb("mask", [P, 2, KINDS, P])
            bmask = wb("bmask", [P, 4, P])
            reset, lf, cum = (wb(x, [P, RESET_W]) for x in ("reset", "lf", "cum"))
            rate = wb("rate", [P, NCH, P])
            AR = wb("AR", [P, NCH, 2, P])
            bT, kd, b_tok, kd_tok = (wb(x, [P, NCH, P]) for x in ("bT", "kd", "b_tok", "kd_tok"))
            ends = wb("ends", [P, 2, NCH])
            sys_ = wb("sys", [P, 2, NCH, KINDS, P])
            own = [K.yT[b][:].rearrange("p k t -> p (k t)").rearrange("p (n h c t) -> p n h c t", n=2, h=2, c=NCH)
                   for b in range(2)]
            D_, U_, D2, U2 = (own[n // 2][:, n % 2] for n in range(4))
            gate_w = wb("gate_w", [P, 2, KD, P])
            gate = wb("gate", [P, T])
            D4, U4, X_, C_ = (wb(x, [P, 2, NCH, P]) for x in ("D4", "U4", "X", "C"))
            R1, SA = wb("R1", [P, P]), wb("SA", [P, P])
            S0 = wb("S0", [P, 8, HD])
            STp, tS, Sout = wb("STp", [P, HD]), wb("tS", [P, HD]), wb("Sout", [P, HD])
            ring = c1.enter_context(nc.psum_tensor("rw_ring", [P, Uses.SLOTS, 1024], F32))
            gate_ps = c1.enter_context(nc.psum_tensor("rw_gate_ps", [P, 2, 512], F32))
            use = Uses(K)
            gate_w_in = [sem(f"gate_w_in{i}") for i in range(2)]
            gate_mm, gate_taken, gate_out = sem("gate_mm"), sem("gate_taken"), sem("gate_out")
            c_in, s0_in, exps, exp_done, ops_ready, s_out, s_ready, pool_done, ends_used = (
                sem(x) for x in ("c_in", "s0_in", "exps", "exp_done", "ops_ready",
                                 "s_out", "s_ready", "pool_done", "ends_used"))

            def order(d):
                return [0] + ([1, 2, 3, 4] if d == 0 else [4, 3, 2, 1])
            STEPS = [("U2", "s"), ("D2", "v"), ("X1", "v"), ("U4", "s"), ("D4", "s"), ("X2", "v"), ("D8", "s"),
                     ("X3", "v")]
            for lv in range(3):
                STEPS += [(f"Y{lv}", "s"), (f"W{lv}", "s"), (f"J{lv}", "v")]
            STEPS = [(name, owner, hh) for hh in range(2) for name, owner in STEPS[:2]] + [
                (name, owner, hh) for name, owner in STEPS[2:] for hh in range(2)]
            for x in ("w", "a"):
                use.add((0, x), "s")
            for w in range(8):
                for x in ("bt", "kt"):
                    use.add((w, x), "s")
                for hh in range(2):
                    for c in range(NCH):
                        use.add((w, "sys", hh, c), "v")
                for x, owner, hh in STEPS:
                    use.add((w, x, hh), owner)
                if w < 7:
                    for x in ("w", "a"):
                        use.add((w + 1, x), "s")
                for k in range(NCH):
                    for x in ("R1", "SA", "Y", "S"):
                        if x == "S" and k == NCH - 1:
                            continue
                        use.add((w, x, k), "v")

            def flat(key, n=T):
                return ring[:, use.slot(key), 0:n]

            def chunks(key):
                return flat(key).rearrange("p (c t) -> p c t", t=P)
            POOL = [(x, hh) for hh in range(2) for x in ("D", "U")] + [
                (x, hh) for x in ("X0", "C0", "C1", "C2") for hh in range(2)]

            def pool_count(w, name, hh):
                return len(POOL) * w + POOL.index((name, hh)) + 1

            with nc.Block() as block:
                @block.sync
                def _(sp):
                    for t, n in ((mask, "rw_mask"), (bmask, "rw_bmask"), (reset, "reset")):
                        sp.dma_start(t[:], A[n]).then_inc(c_in, 16)
                    sp.dma_start(S0[:], A["state_rwkv"]).then_inc(s0_in, 16)

                    def gate_load(i):
                        if i >= 2:
                            sp.wait_ge(gate_mm, i - 1)
                        sp.dma_start(gate_w[:, i % 2], A["w_in"][GATES[i]]).then_inc(gate_w_in[i % 2], 16)

                    for i in range(2):
                        gate_load(i)
                    for w in range(8):
                        for i in range(3 * w, 3 * w + 3):
                            if i == 3 * w + 1:
                                sp.wait_ge(s_ready, w + 1)
                                sp.dma_start(A["out_rwkv"][w], Sout[:]).then_inc(s_out, 16)
                            if i + 2 < len(GATES):
                                gate_load(i + 2)
                            sp.wait_ge(gate_taken, i + 1)
                            sp.dma_start(A["gate_scratch"][i], gate[:]).then_inc(gate_out, 16)
                    sp.wait_ge(s_out, 16 * 8)
                    sp.wait_ge(gate_out, 16 * len(GATES))

                @block.tensor
                def _(pe):
                    pe.wait_ge(ld_in, 32)
                    pe.wait_ge(c_in, 48)

                    def product(key, pairs, n=NCH):
                        use.wait_free(pe, key)
                        out = chunks(key)
                        for c in range(n):
                            last = pairs(out[:, c], c)
                        last.then_inc(use.mm_done, 1)

                    def gates(i, first, end):
                        for n in range(first, end):
                            k, c = n // 2, n % 2
                            if n == 0:
                                pe.wait_ge(gate_w_in[i % 2], 16 * (i // 2 + 1))
                                if i:
                                    pe.wait_ge(gate_taken, i)
                            last = nc.tensor.matmul(gate_ps[:, c, 0:HALF], gate_w[:, i % 2, k],
                                                    K.hT[:, k, c * HALF:(c + 1) * HALF],
                                                    start=(k == 0), stop=(k == KD - 1))
                            if n == 2 * KD - 1:
                                last.then_inc(gate_mm, 1)

                    BEGUN = 2

                    def gates_in_scan(w, point):
                        i, q = 3 * w + 1 + point // 8, point % 8
                        begun = BEGUN if point < 8 else 0
                        if q < 7:
                            gates(i, begun + (2 * KD - begun) * q // 7, begun + (2 * KD - begun) * (q + 1) // 7)

                    def decays(w):
                        d, j = w // 4, w % 4
                        rows = slice(64 * d, 64 * d + 64)
                        for key, wt, x in (((w, "w"), w2, lo[rows, 0]), ((w, "a"), a2, lo[rows, 1])):
                            use.wait_free(pe, key)
                            o = ring[:, use.slot(key)].rearrange("p (c n) -> p c n", c=2)
                            for c in range(2):
                                last = nc.tensor.matmul(o[:, c, 0:HALF], wt[rows, j * P:(j + 1) * P],
                                                        x[:, c * HALF:(c + 1) * HALF], start=True, stop=True)
                            last.then_inc(use.mm_done, 1)

                    decays(0)
                    for w in range(8):
                        d, j = w // 4, w % 4
                        gates(3 * w, 0, 2 * KD)
                        pe.wait_ge(ops_ready, w + 1)
                        for key, src in (((w, "bt"), bT), ((w, "kt"), kd)):
                            product(key, lambda o, c: nc.tensor.transpose(o, src[:, c], K.ident))
                        for hh in range(2):
                            hp = slice(64 * hh, 64 * hh + 64)
                            for c in range(NCH):
                                key = (w, "sys", hh, c)
                                use.wait_free(pe, key)
                                o = flat(key)
                                ar = AR[hp, c].rearrange("p a t -> p (a t)")
                                nc.tensor.matmul(o[:, 0:2 * P], bT[hp, c], ar, start=True, stop=True)
                                nc.tensor.matmul(o[:, 2 * P:4 * P], kd[hp, c], ar, start=True, stop=True)
                                nc.tensor.matmul(o[:, 4 * P:5 * P], AR[hp, c, 0], bT[hp, c], start=True,
                                                 stop=True).then_inc(use.mm_done, 1)

                        gates(3 * w + 1, 0, BEGUN)
                        mm = lambda l, r: (lambda o, c: nc.tensor.matmul(o, l[:, c], r[:, c], start=True, stop=True))
                        for name, owner, hh in STEPS:
                            key = (w, name, hh)
                            D, U, DD, UU, D4h, U4h, X, C = (x[:, hh] for x in (D_, U_, D2, U2, D4, U4, X_, C_))
                            if name == "U2":
                                pe.wait_ge(pool_done, pool_count(w, "U", hh))
                                product(key, mm(D, U))
                            elif name == "D2":
                                product(key, mm(U, D))
                            elif name == "X1":
                                pe.wait_ge(pool_done, pool_count(w, "X0", hh))
                                use.wait_read(pe, (w, "D2", hh))
                                product(key, mm(DD, X))
                            elif name == "U4":
                                use.wait_read(pe, (w, "U2", hh))
                                product(key, mm(DD, UU))
                            elif name == "D4":
                                product(key, mm(UU, DD))
                            elif name == "X2":
                                use.wait_read(pe, (w, "D4", hh))
                                use.wait_read(pe, (w, "X1", hh))
                                product(key, mm(D4h, X))
                            elif name == "D8":
                                use.wait_read(pe, (w, "U4", hh))
                                product(key, mm(U4h, D4h))
                            elif name == "X3":
                                use.wait_read(pe, (w, "D8", hh))
                                use.wait_read(pe, (w, "X2", hh))
                                product(key, mm(D, X))
                            else:
                                lv = int(name[1])
                                Cl = (C, D4h, U4h)[lv]
                                if name[0] == "Y":
                                    use.wait_read(pe, (w, "X3" if lv == 0 else f"J{lv - 1}", hh))
                                    product(key, lambda o, c: nc.tensor.transpose(o, X[:, c], K.ident))
                                elif name[0] == "W":
                                    pe.wait_ge(pool_done, pool_count(w, f"C{lv}", hh))
                                    product(key, mm(Cl, X))
                                else:
                                    use.wait_read(pe, (w, f"W{lv}", hh))
                                    product(key, mm(UU, DD))
                        if w < 7:
                            decays(w + 1)
                        for k, c in enumerate(order(d)):
                            hps = [slice(64 * hh, 64 * hh + 64) for hh in range(2)]
                            v_of = lambda hh: v_tok[:, c, (2 * j + hh) * HD:(2 * j + hh + 1) * HD]
                            with_state = k > 0
                            key = (w, "R1", k)
                            use.wait_free(pe, key)
                            gates_in_scan(w, 3 * k)
                            if k == 0:
                                use.wait_read(pe, (w, "J2", 1))
                            else:
                                pe.wait_ge(ends_used, 4 * w + k)
                            for hh, hp in enumerate(hps):
                                o = ring[:, use.slot(key), hh * 512:hh * 512 + HD]
                                if with_state:
                                    nc.tensor.matmul(o, AR[hp, c, 0], STp[hp, :], start=True, stop=False)
                                last = nc.tensor.matmul(o, sys_[:, hh, c, LKT], v_of(hh), start=not with_state,
                                                        stop=True)
                            last.then_inc(use.mm_done, 1)
                            gates_in_scan(w, 3 * k + 1)
                            use.wait_read(pe, key)
                            key = (w, "SA", k)
                            use.wait_free(pe, key)
                            for hh in range(2):
                                last = nc.tensor.matmul(ring[:, use.slot(key), hh * 512:hh * 512 + HD], X_[:, hh, c],
                                                        R1[:, hh * HD:(hh + 1) * HD], start=True, stop=True)
                            last.then_inc(use.mm_done, 1)
                            gates_in_scan(w, 3 * k + 2)
                            use.wait_read(pe, key)
                            key = (w, "Y", k)
                            use.wait_free(pe, key)
                            for hh, hp in enumerate(hps):
                                o = flat(key)[hp, 0:P]
                                sa = SA[:, hh * HD:(hh + 1) * HD]
                                if with_state:
                                    nc.tensor.matmul(o, STp[hp, :], AR[hp, c, 1], start=True, stop=False)
                                nc.tensor.matmul(o, sa, sys_[:, hh, c, MBR], start=not with_state, stop=False)
                                last = nc.tensor.matmul(o, v_of(hh), sys_[:, hh, c, MKR], start=False, stop=True)
                            last.then_inc(use.mm_done, 1)
                            if k == NCH - 1:
                                continue
                            key = (w, "S", k)
                            use.wait_free(pe, key)
                            for hh, hp in enumerate(hps):
                                o = flat(key)[hp, 0:HD]
                                sa = SA[:, hh * HD:(hh + 1) * HD]
                                nc.tensor.matmul(o, b_tok[:, c, hp], sa, start=True, stop=False)
                                last = nc.tensor.matmul(o, kd_tok[:, c, hp], v_of(hh), start=False, stop=True)
                            last.then_inc(use.mm_done, 1)

                @block.scalar
                def _(act):
                    lfv = lf[:].rearrange("p (c t) -> p c t", t=129)

                    def take(key, dst):
                        use.wait_mm(act, key)
                        use.read(nc.scalar.activation(dst, chunks(key), ACT.Copy), key)

                    def take_gate(i):
                        act.wait_ge(gate_mm, i + 1)
                        if i:
                            act.wait_ge(gate_out, 16 * i)
                        nc.scalar.activation(halves(gate[:]), gate_ps[:, :, 0:HALF],
                                             ACT.Copy).then_inc(gate_taken, 1)

                    def take_decays(w):
                        d, j = w // 4, w % 4
                        if w:
                            act.wait_ge(ops_ready, w)
                        for key, bias in (((w, "w"), par("w0", 4 * d + j)), ((w, "a"), par("a0", 4 * d + j))):
                            use.wait_mm(act, key)
                            pieces = ring[:, use.slot(key)].rearrange("p (c n) -> p c n", c=2)
                            if key[1] == "w":
                                nc.scalar.activation(lfv[:, 0:2, 1:129],
                                                     pieces[:, 0, 0:2 * P].rearrange("p (c t) -> p c t", t=P),
                                                     ACT.Sigmoid, bias=bias)
                                nc.scalar.activation(lfv[:, 2, 1:65], pieces[:, 0, 2 * P:HALF], ACT.Sigmoid, bias=bias)
                                nc.scalar.activation(lfv[:, 2, 65:129], pieces[:, 1, 0:64], ACT.Sigmoid, bias=bias)
                                ins = nc.scalar.activation(lfv[:, 3:5, 1:129],
                                                           pieces[:, 1, 64:HALF].rearrange("p (c t) -> p c t", t=P),
                                                           ACT.Sigmoid, bias=bias)
                            else:
                                ins = nc.scalar.activation(rate[:].rearrange("p c t -> p (c t)").rearrange(
                                    "p (c n) -> p c n", c=2), pieces[:, :, 0:HALF], ACT.Sigmoid, bias=bias)
                            use.read(ins, key)

                    take_decays(0)
                    for w in range(8):
                        act.wait_ge(exps, w + 1)
                        nc.scalar.activation(AR[:], AR[:], ACT.Exp, scale=KAPPA)
                        nc.scalar.activation(ends[:], ends[:], ACT.Exp, scale=KAPPA)
                        nc.scalar.activation(bT[:], bT[:], ACT.Exp, scale=KAPPA).then_inc(exp_done, 1)
                        take_gate(3 * w)
                        take((w, "bt"), b_tok[:])
                        take((w, "kt"), kd_tok[:])
                        for name, owner, hh in STEPS:
                            if owner != "s":
                                continue
                            dst = {"U2": U2, "U4": U4, "D4": D4, "D8": D_}.get(name)
                            if dst is None:
                                dst = U2 if name[0] == "Y" else D2
                            take((w, name, hh), dst[:, hh])
                        if w < 7:
                            take_decays(w + 1)
                        take_gate(3 * w + 1)
                        take_gate(3 * w + 2)

                @block.gpsimd
                def _(pool):
                    pool.wait_ge(c_in, 48)
                    for w in range(8):
                        for name, hh in POOL:
                            def msk(i):
                                return bc(bmask[:, i].unsqueeze(1), [P, NCH, P])
                            if name in "DU":
                                use.wait_read(pool, (w, "sys", hh, NCH - 1))
                                src, dst = (LB, D_) if name == "D" else (LBT, U_)
                                ins = nc.gpsimd.tensor_tensor(dst[:, hh], sys_[:, hh, :, src], msk(0), ALU.mult)
                            elif name == "X0":
                                pool.wait_ge(pool_done, pool_count(w, "U", hh))
                                ins = nc.gpsimd.tensor_tensor(
                                    X_[:, hh], U_[:, hh], bc(K.ident.unsqueeze(1), [P, NCH, P]), ALU.add)
                            else:
                                lv = int(name[1])
                                if lv == 1:
                                    use.wait_mm(pool, (w, "D8", hh))
                                if lv == 2:
                                    use.wait_mm(pool, (w, "D8", hh))
                                ins = nc.gpsimd.tensor_tensor((C_, D4, U4)[lv][:, hh], sys_[:, hh, :, LB],
                                                              msk(1 + lv), ALU.mult)
                            ins.then_inc(pool_done, 1)

                @block.vector
                def _(dve):
                    link = lambda ins: K.dve.link(dve, ins)
                    lfv = lf[:].rearrange("p (c t) -> p c t", t=129)
                    cumv = cum[:].rearrange("p (c t) -> p c t", t=129)
                    link(nc.vector.memset(lfv[:, :, 0:1], 0.0))
                    dve.wait_ge(c_in, 48)
                    inc, exc = cumv[:, :, 1:129], cumv[:, :, 0:128]
                    mid, end = cumv[:, :, 64:65], cumv[:, :, 128:129]

                    def sums(w):
                        use.wait_read(dve, (w, "w"))
                        link(nc.vector.tensor_tensor_scan(cum[:], reset[:], lf[:], 0.0, ALU.mult, ALU.add))

                    sums(0)
                    for w in range(8):
                        d, j = w // 4, w % 4
                        m = bc(mid, [P, NCH, P])
                        if d == 0:
                            nc.vector.tensor_tensor(AR[:, :, 0], exc, m, ALU.subtract)
                            nc.vector.tensor_tensor(AR[:, :, 1], inc, m, ALU.subtract)
                            nc.vector.tensor_tensor(bT[:], m, inc, ALU.subtract)
                            pre, post = 0, 1
                        else:
                            nc.vector.tensor_tensor(AR[:, :, 0], m, inc, ALU.subtract)
                            nc.vector.tensor_tensor(AR[:, :, 1], m, exc, ALU.subtract)
                            nc.vector.tensor_tensor(bT[:], exc, m, ALU.subtract)
                            pre, post = 1, 0
                        nc.vector.tensor_copy(ends[:, pre].unsqueeze(2), mid)
                        nc.vector.tensor_tensor(ends[:, post].unsqueeze(2), end, mid, ALU.subtract).then_inc(exps, 1)
                        dve.wait_ge(exp_done, w + 1)
                        use.wait_read(dve, (w, "a"))
                        of = lambda x: x[:, j].rearrange("p (c t) -> p c t", t=P)
                        link(nc.vector.scalar_tensor_tensor(out=AR[:, :, 0], in0=AR[:, :, 0], scalar=-1.0, in1=of(kk),
                                                            op0=ALU.mult, op1=ALU.mult))
                        nc.vector.tensor_tensor(AR[:, :, 1], AR[:, :, 1], of(rT), ALU.mult)
                        link(nc.vector.tensor_scalar(kd[:], rate[:], par("ka", j), omka[:, j:j + 1], ALU.mult, ALU.add))
                        link(nc.vector.tensor_tensor(kd[:], kd[:], of(kT), ALU.mult))
                        link(nc.vector.tensor_tensor(kd[:], kd[:], bT[:], ALU.mult))
                        link(nc.vector.tensor_tensor(bT[:], bT[:], rate[:], ALU.mult))
                        nc.vector.tensor_tensor(bT[:], bT[:], of(kk), ALU.mult).then_inc(ops_ready, 1)
                        for hh in range(2):
                            for c in range(NCH):
                                key = (w, "sys", hh, c)
                                use.wait_mm(dve, key)
                                if w and hh == 0 and c == 0:
                                    dve.wait_ge(pool_done, len(POOL) * w)
                                use.read(nc.vector.tensor_tensor(
                                    sys_[:, hh, c], flat(key).rearrange("p (k t) -> p k t", t=P), mask[:, d],
                                    ALU.mult), key)
                        for name, owner, hh in STEPS:
                            if owner != "v":
                                continue
                            key = (w, name, hh)
                            use.wait_mm(dve, key)
                            if name == "D2":
                                use.read(nc.vector.tensor_copy(D2[:, hh], chunks(key)), key)
                            else:
                                if name == "X1":
                                    dve.wait_ge(pool_done, pool_count(w, "X0", hh))
                                use.read(nc.vector.tensor_tensor(X_[:, hh], X_[:, hh], chunks(key), ALU.add), key)
                        seq = order(d)
                        if w == 0:
                            dve.wait_ge(s0_in, 16)
                        for k, c in enumerate(seq):
                            for x, dst in (("R1", R1), ("SA", SA)):
                                key = (w, x, k)
                                use.wait_mm(dve, key)
                                both = ring[:, use.slot(key)].rearrange("p (h n) -> p h n", h=2)[:, :, 0:HD]
                                use.read(nc.vector.tensor_copy(dst[:].rearrange("p (h n) -> p h n", h=2), both), key)
                            key = (w, "Y", k)
                            use.wait_mm(dve, key)
                            y = K.yT[2][:, j, c * P:(c + 1) * P]
                            if d == 0:
                                use.read(nc.vector.tensor_copy(y, flat(key, P)), key)
                            else:
                                use.read(nc.vector.tensor_tensor(y, y, flat(key, P), ALU.add), key)
                            if k == NCH - 1:
                                if w < 7:
                                    sums(w + 1)
                                continue
                            key = (w, "S", k)
                            use.wait_mm(dve, key)
                            ps = flat(key, HD)
                            cn = seq[k + 1]
                            if k == 0:
                                if w:
                                    dve.wait_ge(s_out, 16 * w)
                                use.read(nc.vector.tensor_scalar(Sout[:], ps, ends[:, 1, c:c + 1], None, ALU.mult), key)
                                use.wait_read(dve, key)
                                dve.sem_inc(s_ready, 1)
                                nc.vector.tensor_scalar(STp[:], S0[:, w], ends[:, 0, cn:cn + 1], None,
                                                        ALU.mult).then_inc(ends_used, 1)
                            else:
                                ins = nc.vector.tensor_tensor(tS[:], ps, STp[:], ALU.add)
                                use.read(ins, key)
                                use.wait_read(dve, key)
                                nc.vector.tensor_scalar(STp[:], tS[:], ends[:, 1, c:c + 1], ends[:, 0, cn:cn + 1],
                                                        ALU.mult, ALU.mult).then_inc(ends_used, 1)
        with ExitStack() as c1:
            t1 = c1.enter_context(nc.sbuf_tensor("rw_t1", [P, 4, T], F32))
            ps = c1.enter_context(nc.psum_tensor("rw_ps1", [P, 4, 2, 512], F32))
            y = K.yT[2]
            y_in = sem("y_in")
            g2 = c1.enter_context(nc.sbuf_tensor("rw_g2", [P, W], F32))
            gn = {x: sem("gn_" + x) for x in ("mean", "cent", "sq", "var", "log", "root", "rk", "bon", "bond", "gmm", "norm")}
            with nc.Block() as block:
                @block.sync
                def _(sp):
                    sp.dma_start(g2[:], A["rw_g2"]).then_inc(ld_in, 16)
                    for b in range(2):
                        sp.dma_start(K.yT[b][:], A["y_scratch"][b]).then_inc(y_in, 16)
                    sp.wait_ge(y_in, 32)

                @block.tensor
                def _(pe):
                    def sums(w_, src, j, s, done):
                        for c in range(2):
                            last = nc.tensor.matmul(ps[:, s, c, 0:HALF], w_, src[:, c * HALF:(c + 1) * HALF],
                                                    start=True, stop=True)
                        last.then_inc(done, 1)
                    for j in range(4):
                        if j:
                            pe.wait_ge(gn["cent"], j)
                        sums(K.blk64, y[:, j], j, 0, gn["mean"])
                        pe.wait_ge(gn["sq"], j + 1)
                        if j:
                            pe.wait_ge(gn["log"], j)
                        sums(K.blk64, t1[:, j], j, 1, gn["var"])
                        pe.wait_ge(gn["rk"], j + 1)
                        if j:
                            pe.wait_ge(gn["bond"], j)
                        sums(K.blk64, kk[:, j], j, 2, gn["bon"])
                        if j:
                            pe.wait_ge(gn["norm"], j)
                        pe.wait_ge(ld_in, 48)
                        sums(g2[:, j * P:(j + 1) * P], lo[:, 2], j, 3, gn["gmm"])

                @block.scalar
                def _(act):
                    for j in range(4):
                        act.wait_ge(gn["cent"], j + 1)
                        nc.scalar.activation(t1[:, j], y[:, j], ACT.Square).then_inc(gn["sq"], 1)
                        act.wait_ge(gn["var"], j + 1)
                        rsqrt_log(K, halves(t1[:, j]), ps[:, 1, :, 0:HALF], 1.0 / HD, "group").then_inc(
                            gn["log"], 1)
                        act.wait_ge(gn["log"], j + 1)
                        rsqrt_exp(K, t1[:, j]).then_inc(gn["root"], 1)

                @block.vector
                def _(dve):
                    link = lambda ins: K.dve.link(dve, ins)
                    for j in range(4):
                        link(nc.vector.scalar_tensor_tensor(out=kk[:, j], in0=rT[:, j], scalar=par("rk", j),
                                                            in1=kT[:, j], op0=ALU.mult, op1=ALU.mult))
                        dve.sem_inc(gn["rk"], 1)
                        dve.wait_ge(gn["mean"], j + 1)
                        nc.vector.scalar_tensor_tensor(out=halves(y[:, j]), in0=ps[:, 0, :, 0:HALF], scalar=-1.0 / HD,
                                                       in1=halves(y[:, j]), op0=ALU.mult, op1=ALU.add).then_inc(gn["cent"], 1)
                        dve.wait_ge(gn["bon"], j + 1)
                        ins = nc.vector.tensor_tensor(halves(vT[:, j]), halves(vT[:, j]), ps[:, 2, :, 0:HALF], ALU.mult)
                        ins.then_inc(gn["bond"], 1)
                        dve.wait_ge(gn["root"], j + 1)
                        link(nc.vector.tensor_tensor(y[:, j], y[:, j], t1[:, j], ALU.mult))
                        link(nc.vector.tensor_scalar(y[:, j], y[:, j], par("ln_g", j), par("ln_b", j), ALU.mult, ALU.add))
                        link(nc.vector.tensor_tensor(y[:, j], y[:, j], vT[:, j], ALU.add))
                        dve.wait_ge(gn["gmm"], j + 1)
                        nc.vector.tensor_tensor(halves(y[:, j]), halves(y[:, j]), ps[:, 3, :, 0:HALF],
                                                ALU.mult).then_inc(gn["norm"], 1)


def merge_stage(nc, K, A):
    with ExitStack() as ctx:
        def sb(name, shape):
            return ctx.enter_context(nc.sbuf_tensor("mg_" + name, shape, F32))

        def sem(name):
            return K.sem("mg_" + name)
        x2 = sb("x2", [P, KD, T])
        x_in = sem("x_in")
        with ExitStack() as c1:
            merged = c1.enter_context(nc.sbuf_tensor("mg_merged", [P, KD, T], F32))
            gate = c1.enter_context(nc.sbuf_tensor("mg_gate", [P, 4, T], F32))
            part = c1.enter_context(nc.sbuf_tensor("mg_part", [P, 2, T], F32))
            wb = c1.enter_context(nc.sbuf_tensor("mg_wb", [P, 4, KW, P], F32))
            wo = c1.enter_context(nc.sbuf_tensor("mg_wo", [P, 4, KD, P], F32))
            ps = c1.enter_context(nc.psum_tensor("mg_psb", [P, 4, 2, 512], F32))
            g_in, wb_in, wo_in = ([sem(f"{x}{i}") for i in range(4)] for x in ("g_in", "wb_in", "wo_in"))
            br_mm, br_taken, gated, summed, out_mm, out_taken = (sem(x) for x in (
                "br_mm", "br_taken", "gated", "summed", "out_mm", "out_taken"))
            with nc.Block() as block:
                @block.sync
                def _(sp):
                    for i in range(24):
                        if i >= 4:
                            sp.wait_ge(br_mm, i - 3)
                        sp.dma_start(wb[:, i % 4], A["w_branch"][i]).then_inc(wb_in[i % 4], 16)
                        if i >= 4:
                            sp.wait_ge(br_taken, i - 3)
                        sp.dma_start(gate[:, i % 4], A["gate_scratch"][i]).then_inc(g_in[i % 4], 16)
                        if i == 12:
                            for m in range(4):
                                sp.dma_start(wo[:, m], A["w_out"][m]).then_inc(wo_in[m], 16)
                            sp.dma_start(x2[:], A["x"]).then_inc(x_in, 16)
                    for m in range(4, KD):
                        sp.wait_ge(out_mm, m - 3)
                        sp.dma_start(wo[:, m % 4], A["w_out"][m]).then_inc(wo_in[m % 4], 16)

                @block.tensor
                def _(pe):
                    for i, (m, b) in enumerate(MERGE_ORDER):
                        pe.wait_ge(wb_in[i % 4], 16 * (i // 4 + 1))
                        if i >= 4:
                            pe.wait_ge(br_taken, i - 3)
                        for k in range(KW):
                            for c in range(2):
                                last = nc.tensor.matmul(ps[:, i % 4, c, 0:HALF], wb[:, i % 4, k],
                                                        K.yT[b][:, k, c * HALF:(c + 1) * HALF],
                                                        start=(k == 0), stop=(k == KW - 1))
                        last.then_inc(br_mm, 1)
                    pe.wait_ge(summed, 24)
                    for m in range(KD):
                        pe.wait_ge(wo_in[m % 4], 16 * (m // 4 + 1))
                        if m >= 4:
                            pe.wait_ge(out_taken, m - 3)
                        for k in range(KD):
                            for s, (a, b) in enumerate(SEG):
                                last = nc.tensor.matmul(ps[:, m % 4, s, 0:b - a], wo[:, m % 4, k], merged[:, k, a:b],
                                                        start=(k == 0), stop=(k == KD - 1))
                        last.then_inc(out_mm, 1)

                @block.scalar
                def _(act):
                    for i in range(24):
                        act.wait_ge(g_in[i % 4], 16 * (i // 4 + 1))
                        nc.scalar.activation(gate[:, i % 4], gate[:, i % 4], ACT.Sigmoid).then_inc(gated, 1)

                @block.vector
                def _(dve):
                    for i, (m, b) in enumerate(MERGE_ORDER):
                        dve.wait_ge(br_mm, i + 1)
                        dve.wait_ge(gated, i + 1)
                        dst = merged[:, m] if b == 0 else part[:, b - 1]
                        nc.vector.tensor_tensor(halves(dst), ps[:, i % 4, :, 0:HALF], halves(gate[:, i % 4]),
                                                ALU.mult).then_inc(br_taken, 1)
                        if b:
                            dve.wait_ge(br_taken, i + 1)
                            dve.wait_ge(summed, i)
                            nc.vector.tensor_tensor(merged[:, m], merged[:, m], dst, ALU.add).then_inc(summed, 1)
                        else:
                            dve.sem_inc(summed, 1)
                    dve.wait_ge(x_in, 16)
                    for m in range(KD):
                        dve.wait_ge(out_mm, m + 1)
                        for s, (a, b) in enumerate(SEG):
                            ins = nc.vector.scalar_tensor_tensor(
                                out=x2[:, m, a:b], in0=ps[:, m % 4, s, 0:b - a], scalar=K.mod[:, 2 * KD + m, s:s + 1],
                                in1=x2[:, m, a:b], op0=ALU.mult, op1=ALU.add)
                        ins.then_inc(out_taken, 1)
        norm_stage(nc, K, A, 1, x2, K.hT, "n2", store=A["x_scratch"])


RING = 8
TURNS = SLOTS // RING


def peer_stage(nc, K, A, x3):
    with ExitStack() as ctx:
        def sb(name, shape, dt=F32):
            return ctx.enter_context(nc.sbuf_tensor("pr_" + name, shape, dt))

        def sem(name):
            return K.sem("pr_" + name)
        h_tok = sb("h_tok", [P, NCH, D])
        qT = sb("q", [P, HEADS_P, T])
        keys = sb("keys", [P, NKEYS])
        keys_in = sem("keys_in")
        y_tok = K.hT[:].rearrange("p k t -> p (k t)").rearrange("p (c d) -> p c d", c=NCH)
        s = sb("s", [P, 2 * HEADS_P, NKEYS])
        cand = sb("cand", [P, HEADS_P, TOPK, TOPK])
        hot = sb("hot", [P, HEADS_P, TOPK, TOPK])
        top = sb("top", [P, 2 * HEADS_P, TOPK])
        top_i = sb("top_i", [P, 2 * HEADS_P, TOPK], U32)
        top_f = sb("top_f", [P, 2 * HEADS_P, TOPK])
        best = sb("best", [P, HEADS_P, TOPK])
        best_i = sb("best_i", [P, HEADS_P, TOPK], U32)
        row_i = sb("row_i", [P, 2, HEADS_P, TOPK], U32)
        row_f = sb("row_f", [P, 2, HEADS_P, TOPK])
        pick = sb("pick", [P, 2, HEADS_P, TOPK])
        zsum = sb("zsum", [P, HEADS_P])
        gate = sb("gate", [P, 3, HEADS_P, TOPK])
        experts = sb("experts", [P, 3, SLOTS], I32)
        now_u, now_v = sb("now_u", [P, 2, RING], I32), sb("now_v", [P, 2, RING], I32)
        u_rows, v_rows = sb("u_rows", [P, RING, D]), sb("v_rows", [P, RING, D])
        wq = v_rows[:].rearrange("p h (k n) -> p h k n", k=KD)
        dot8, act8, weight = (sb(x, [P, RING]) for x in ("dot8", "act8", "weight"))
        diag = sb("diag", [P, RING, P])
        ps_s = ctx.enter_context(nc.psum_tensor("pr_pss", [P, 2, HEADS_P, NKEYS], F32))
        ps_y = ctx.enter_context(nc.psum_tensor("pr_psy", [P, 2, 2, 512], F32))
        u_in = [sem(f"u_in{i}") for i in range(RING)]
        v_in = [sem(f"v_in{i}") for i in range(RING)]
        (s_mm, s_taken, arg_done, exp_done, routed, u_used, dots_done, gelu_done, w_done, diag_done, v_used, y_done,
         y_taken, now_done, slot_free, prep_mm, prep_taken, x_in, t_done, added) = (sem(x) for x in (
             "s_mm", "s_taken", "arg_done", "exp_done", "routed", "u_used", "dots_done", "gelu_done", "w_done",
             "diag_done", "v_used", "y_done", "y_taken", "now_done", "slot_free", "prep_mm",
             "prep_taken", "x_in", "t_done", "added"))
        wq_in = [sem(f"wq_in{i}") for i in range(HEADS_P)]
        iota = K.con[:, CCOL["iota"]:CCOL["iota"] + TOPK]
        PARTS = [(0, 0, HEADS_P // 2), (0, HEADS_P // 2, HEADS_P)] + [(c, 0, HEADS_P) for c in range(1, NCH)]
        parts_to = lambda c: c + 2
        PREP = [("q0", 0), ("tok", 0)] + [("q", h) for h in range(0, HEADS_P, 2)] + [("tok", c) for c in range(1, NCH)]
        with nc.Block() as block:
            @block.sync
            def _(sp):
                for h in range(HEADS_P):
                    sp.dma_start(wq[:, h], A["p_wq"][h]).then_inc(wq_in[h], 16)
                sp.dma_start(keys[:], A["p_keys"]).then_inc(keys_in, 16)
                sp.wait_ge(prep_mm, 1)
                sp.dma_start(x3[:], A["x_scratch"]).then_inc(x_in, 16)

            @block.gpsimd
            def _(pool):
                def turn(c, i, half, order, table, now, rows, arrived, used, first):
                    g = i + c * TURNS
                    nc.gpsimd.tensor_copy(now[:, half], experts[:, c % 3, bass.ds(i * RING, RING)]).then_inc(
                        now_done, 1)
                    pool.wait_ge(now_done, order + (moved[0] + 1))
                    for r in range(RING):
                        if not first:
                            pool.wait_ge(used, (g - 1) * RING + r + 1)
                            pool.sem_inc(slot_free, 1)
                        elif rows is v_rows:
                            pool.wait_ge(prep_mm, PREP.index(("q", r // 2 * 2)) + 1)
                        nc.gpsimd.indirect_dma_start(
                            out=rows[:, r], out_offset=None, in_=table,
                            in_offset=bass.IndirectOffsetOnAxis(ap=now[:, half, r:r + 1], axis=0)).then_inc(
                                arrived[r], 16)

                tables = ((A["p_u"], now_u, u_rows, u_in, u_used), (A["p_v"], now_v, v_rows, v_in, v_used))
                moved = [0]

                def both(c, i, half, g2, first):
                    for o, table in enumerate(tables):
                        turn(c, i, half, g2 + o, *table, first)

                def pairs_of_turns(c, first, end):
                    with pool.Fori(first, end) as i:
                        for half in range(2):
                            both(c, i * 2 + half, half, i * 4 + 2 * half, False)

                pool.wait_ge(routed, 1)
                for half in range(2):
                    both(0, half, half, 2 * half, half == 0)
                pairs_of_turns(0, 1, TURNS // 4)
                pool.wait_ge(routed, 2)
                pairs_of_turns(0, TURNS // 4, TURNS // 2)
                moved[0] += 2 * TURNS
                for c in range(1, NCH):
                    pool.wait_ge(routed, parts_to(c))
                    pairs_of_turns(c, 0, TURNS // 2)
                    moved[0] += 2 * TURNS

            @block.tensor
            def _(pe):
                def prep(n):
                    what, x = PREP[n]
                    out = ps_y[:, n % 2]
                    if n >= 2:
                        pe.wait_ge(prep_taken, n - 1)
                    if what == "q0":
                        for h in range(HEADS_P):
                            pe.wait_ge(wq_in[h], 16)
                            for k in range(KD):
                                last = nc.tensor.matmul(out[:, h // 4, (h % 4) * P:(h % 4 + 1) * P], wq[:, h, k],
                                                        K.hT[:, k, 0:P], start=(k == 0), stop=(k == KD - 1))
                    elif what == "q":
                        for a in range(2):
                            for k in range(KD):
                                last = nc.tensor.matmul(out[:, a], wq[:, x + a, k], K.hT[:, k, P:T],
                                                        start=(k == 0), stop=(k == KD - 1))
                    else:
                        for k in range(KD):
                            last = nc.tensor.transpose(out[:, k // 4, (k % 4) * P:(k % 4 + 1) * P],
                                                       K.hT[:, k, x * P:(x + 1) * P], K.ident)
                    last.then_inc(prep_mm, 1)

                def scores(c):
                    if c:
                        pe.wait_ge(s_taken, c)
                    for h in range(HEADS_P):
                        for a in range(2):
                            hp = slice(64 * a, 64 * a + 64)
                            last = nc.tensor.matmul(ps_s[:, a, h], qT[hp, h, c * P:(c + 1) * P], keys[hp, :],
                                                    start=True, stop=True)
                            last.then_inc(s_mm, 1)

                def turn(c, i, first):
                    g = i + c * TURNS
                    for r in range(RING):
                        pe.wait_ge(v_in[r], 16 * (g + 1))
                        pe.wait_ge(diag_done, g * RING + r + 1)
                        for a in range(2):
                            last = nc.tensor.matmul(ps_y[:, c % 2, a], diag[:, r], v_rows[:, r, a * 512:(a + 1) * 512],
                                                    start=(first and r == 0), stop=False, skip_group_check=True)
                        last.then_inc(v_used, 1)

                def combine(c):
                    if c >= 2:
                        pe.wait_ge(added, c - 1)
                    turn(c, 0, True)
                    with pe.Fori(1, TURNS) as i:
                        turn(c, i, False)
                    pe.wait_ge(v_used, (c + 1) * SLOTS)
                    pe.sem_inc(y_done, 1)
                    pe.wait_ge(y_taken, c + 1)
                    for k in range(KD):
                        last = nc.tensor.transpose(ps_y[:, c % 2, k // 4, (k % 4) * P:(k % 4 + 1) * P],
                                                   y_tok[:, c, k * P:(k + 1) * P], K.ident)
                    last.then_inc(t_done, 1)

                prep(0)
                pe.wait_ge(keys_in, 16)
                pe.wait_ge(prep_taken, 1)
                scores(0)
                for n in range(1, len(PREP)):
                    prep(n)
                pe.wait_ge(prep_taken, len(PREP))
                scores(1)
                for c in range(NCH):
                    if 1 <= c < NCH - 1:
                        scores(c + 1)
                    combine(c)

            @block.scalar
            def _(act):
                def take(c):
                    act.wait_ge(s_mm, 16 * (c + 1))
                    if c:
                        act.wait_ge(routed, parts_to(c - 1))
                    nc.scalar.activation(s[:], ps_s[:].rearrange("p a h n -> p (a h) n"), ACT.Copy).then_inc(s_taken, 1)

                def softmax(part):
                    c, h0, h1 = PARTS[part]
                    act.wait_ge(arg_done, part + 1)
                    nc.scalar.activation(gate[:, c % 3, h0:h1], gate[:, c % 3, h0:h1], ACT.Exp).then_inc(exp_done, 1)

                def turn(c, i, first):
                    g = i + c * TURNS
                    act.wait_ge(dots_done, g + 1)
                    nc.scalar.activation(act8[:], dot8[:], ACT.Gelu_apprx_tanh).then_inc(gelu_done, 1)
                    act.wait_ge(w_done, g + 1)
                    for r in range(RING):
                        if not first:
                            act.wait_ge(v_used, (g - 1) * RING + r + 1)
                        nc.scalar.activation(diag[:, r], K.ident, ACT.Copy,
                                             scale=weight[:, r:r + 1]).then_inc(diag_done, 1)

                def turns(c, first, end):
                    with act.Fori(first, end) as i:
                        turn(c, i, False)

                def take_y(c):
                    act.wait_ge(y_done, c + 1)
                    nc.scalar.activation(y_tok[:, c].rearrange("p (a n) -> p a n", a=2), ps_y[:, c % 2],
                                         ACT.Copy).then_inc(y_taken, 1)

                def prep(n):
                    what, x = PREP[n]
                    act.wait_ge(prep_mm, n + 1)
                    if what == "q0":
                        dst, src = qT[:, :, 0:P].rearrange("p (a h) t -> p a h t", a=2), ps_y[:, n % 2].rearrange(
                            "p a (h t) -> p a h t", t=P)
                    elif what == "q":
                        dst, src = qT[:, x:x + 2, P:T], ps_y[:, n % 2]
                    else:
                        dst, src = h_tok[:, x].rearrange("p (a n) -> p a n", a=2), ps_y[:, n % 2]
                    nc.scalar.activation(dst, src, ACT.Copy).then_inc(prep_taken, 1)

                prep(0)
                take(0)
                for n in range(1, len(PREP)):
                    prep(n)
                softmax(0)
                turn(0, 0, True)
                turns(0, 1, TURNS // 2)
                softmax(1)
                take(1)
                turns(0, TURNS // 2, TURNS)
                take_y(0)
                for c in range(1, NCH):
                    softmax(parts_to(c) - 1)
                    if c + 1 < NCH:
                        take(c + 1)
                    turns(c, 0, TURNS)
                    take_y(c)

            @block.vector
            def _(dve):
                link = lambda ins: K.dve.link(dve, ins)

                def top16(vals, idx, src, lists):
                    def step(half, ls):
                        o = slice(8 * half, 8 * half + 8)
                        for l in ls:
                            ins = nc.vector.max(vals(l)[:, o], src(l))
                        link(ins)
                        for l in ls:
                            ins = nc.vector.max_index(idx(l)[:, o], vals(l)[:, o], src(l))
                            if half == 0:
                                ins = nc.vector.match_replace(src(l), vals(l)[:, o], src(l), -3.0e38)
                        link(ins)
                    blocks = [lists[b:b + 4] for b in range(0, len(lists), 4)]
                    return [lambda h=h, b=b: step(h, b) for b in blocks for h in range(2)]

                flat = cand[:].rearrange("p h a b -> p h (a b)")
                shape = lambda hs: [P, hs.stop - hs.start, TOPK, TOPK]
                of_key = lambda hs, a: slice(a * HEADS_P + hs.start, a * HEADS_P + hs.stop)

                def pairs(hs):
                    link(nc.vector.tensor_tensor(cand[:, hs], bc(top[:, of_key(hs, 0)].unsqueeze(3), shape(hs)),
                                                 bc(top[:, of_key(hs, 1)].unsqueeze(2), shape(hs)), ALU.add))

                def rows_of(c, hs):
                    if c >= 3:
                        dve.wait_ge(w_done, (c - 2) * TURNS)
                    nc.vector.tensor_tensor(gate[:, c % 3, hs], best[:, hs], bc(best[:, hs, 0:1], shape(hs)[:3]),
                                            ALU.subtract).then_inc(arg_done, 1)
                    nc.vector.tensor_scalar(row_i[:, 0, hs], best_i[:, hs], 4, None, ALU.logical_shift_right)
                    link(nc.vector.tensor_scalar(row_i[:, 1, hs], best_i[:, hs], TOPK - 1, None, ALU.bitwise_and))
                    nc.vector.tensor_copy(row_f[:, :, hs], row_i[:, :, hs])
                    for a in range(2):
                        ins = nc.vector.tensor_copy(top_f[:, of_key(hs, a)], top_i[:, of_key(hs, a)])
                    link(ins)

                def expert_half(a, hs):
                    link(nc.vector.tensor_tensor(hot[:, hs], bc(row_f[:, a, hs].unsqueeze(3), shape(hs)),
                                                 bc(iota.unsqueeze(1).unsqueeze(1), shape(hs)), ALU.is_equal))
                    link(nc.vector.tensor_tensor(hot[:, hs], hot[:, hs],
                                                 bc(top_f[:, of_key(hs, a)].unsqueeze(2), shape(hs)), ALU.mult))
                    link(nc.vector.tensor_reduce(pick[:, a, hs], hot[:, hs], AX, ALU.add))

                def expert(c, hs):
                    if c >= 3:
                        dve.wait_ge(v_used, (c - 2) * SLOTS)
                    nc.vector.scalar_tensor_tensor(
                        out=experts[:, c % 3, hs.start * TOPK:hs.stop * TOPK],
                        in0=pick[:, 0, hs].rearrange("p h k -> p (h k)"), scalar=float(NKEYS),
                        in1=pick[:, 1, hs].rearrange("p h k -> p (h k)"), op0=ALU.mult, op1=ALU.add).then_inc(routed, 1)

                def route(part):
                    c, h0, h1 = PARTS[part]
                    hs = slice(h0, h1)
                    heads = list(range(h0, h1))
                    steps = [lambda: dve.wait_ge(s_taken, c + 1)]
                    steps += top16(lambda l: top[:, l], lambda l: top_i[:, l], lambda l: s[:, l],
                                   heads + [HEADS_P + h for h in heads])
                    steps += [lambda: pairs(hs)]
                    steps += top16(lambda l: best[:, l], lambda l: best_i[:, l], lambda l: flat[:, l], heads)
                    return steps + [lambda: rows_of(c, hs), lambda: expert_half(0, hs), lambda: expert_half(1, hs),
                                    lambda: expert(c, hs)]

                def gates(part):
                    c, h0, h1 = PARTS[part]
                    dve.wait_ge(exp_done, part + 1)
                    g, z = gate[:, c % 3, h0:h1], zsum[:, h0:h1]
                    link(nc.vector.tensor_reduce(z, g, AX, ALU.add))
                    link(nc.vector.reciprocal(z, z))
                    link(nc.vector.tensor_tensor(g, g, bc(z.unsqueeze(2), [P, h1 - h0, TOPK]), ALU.mult))

                def turn(c, i, part=None):
                    g = i + c * TURNS
                    for r in range(RING):
                        dve.wait_ge(u_in[r], 16 * (g + 1))
                        nc.vector.tensor_tensor_reduce(out=u_rows[:, r], in0=u_rows[:, r], in1=h_tok[:, c], scale=1.0,
                                                       scalar=0.0, op0=ALU.mult, op1=ALU.add,
                                                       accum_out=dot8[:, r:r + 1]).then_inc(u_used, 1)
                    dve.wait_ge(u_used, (g + 1) * RING)
                    dve.sem_inc(dots_done, 1)
                    if part is not None:
                        gates(part)
                    dve.wait_ge(gelu_done, g + 1)
                    if part != 0:
                        dve.wait_ge(diag_done, g * RING)
                    flat_gate = gate[:, c % 3].rearrange("p h k -> p (h k)")
                    nc.vector.tensor_tensor(weight[:], act8[:], flat_gate[:, bass.ts(i, RING)],
                                            ALU.mult).then_inc(w_done, 1)
                    dve.wait_ge(w_done, g + 1)

                def residual(c):
                    dve.wait_ge(x_in, 16)
                    dve.wait_ge(t_done, c + 1)
                    for k in range(KD):
                        xs = x3[:, k, c * P:(c + 1) * P]
                        gate_c = K.mod[:, 5 * KD + k, min(c, 1):min(c, 1) + 1]
                        ins = nc.vector.scalar_tensor_tensor(
                            out=xs, in0=ps_y[:, c % 2, k // 4, (k % 4) * P:(k % 4 + 1) * P], scalar=gate_c, in1=xs,
                            op0=ALU.mult, op1=ALU.add)
                    ins.then_inc(added, 1)

                def turns(c, first, end, steps):
                    for i in range(first, end):
                        turn(c, i)
                        if c and i == 1:
                            residual(c - 1)
                        n = i - first
                        for step in steps[len(steps) * n // (end - first - 1):
                                          len(steps) * (n + 1) // (end - first - 1)]:
                            step()

                for step in route(0):
                    step()
                dve.wait_ge(prep_taken, PREP.index(("tok", 0)) + 1)
                turn(0, 0, 0)
                turns(0, 1, TURNS // 2, route(1))
                turn(0, TURNS // 2, 1)
                turns(0, TURNS // 2 + 1, TURNS, route(2))
                dve.wait_ge(prep_taken, len(PREP))
                for c in range(1, NCH - 1):
                    turn(c, 0, parts_to(c) - 1)
                    turns(c, 1, TURNS, route(parts_to(c)))
                turn(NCH - 1, 0, parts_to(NCH - 1) - 1)
                residual(NCH - 2)
                with dve.Fori(1, TURNS) as i:
                    turn(NCH - 1, i)
                residual(NCH - 1)
                dve.wait_ge(added, NCH)


def final_stage(nc, K, A, x3):
    norm_stage(nc, K, A, 2, x3, x3, "nf")


def build(nc, A):
    with ExitStack() as ctx:
        K = Kern()

        def sb(name, shape, dt=F32):
            return ctx.enter_context(nc.sbuf_tensor(name, shape, dt))
        K.par = sb("par", [P, NPAR])
        K.con = sb("con", [P, NCONST])
        K.mod = sb("mod", [P, 48, 2])
        K.gain = sb("gain", [P, 2, KD, 2])
        K.lb = sb("lb", [P, 3, 8])
        K.eps = sb("eps", [P, len(EPSILONS)])
        K.hT = sb("hT", [P, KD, T])
        K.nc, K.taken = nc, []
        K.dve = Order(nc.alloc_semaphore("dve_order"))
        K.ident = K.con[:, CCOL["ident"]:CCOL["ident"] + P]
        K.ones = K.con[:, CCOL["ones"]:CCOL["ones"] + P]
        K.blk64 = K.con[:, CCOL["blk64"]:CCOL["blk64"] + P]
        load_stage(nc, K, A)
        K.end_stage()
        with ExitStack() as c2:
            K.xT = c2.enter_context(nc.sbuf_tensor("xT", [P, KD, T], F32))
            norm_stage(nc, K, A, 0, K.xT, K.hT, "n1", load=A["x"])
        with ExitStack() as c2:
            K.yT = [c2.enter_context(nc.sbuf_tensor(f"yT{b}", [P, 4, T], F32)) for b in range(3)]
            with nc.sbuf_tensor("raw", [P, HY_AHEAD - 8, T], F32) as K.raw:
                hgrn_stage(nc, K, A)
                K.end_stage()
                hyena_stage(nc, K, A)
                K.end_stage()
            rwkv_stage(nc, K, A)
            K.end_stage()
            merge_stage(nc, K, A)
            K.end_stage()
        with nc.sbuf_tensor("x3", [P, KD, T], F32) as x3:
            peer_stage(nc, K, A, x3)
            K.end_stage()
            final_stage(nc, K, A, x3)


def chan(v):
    v = np.asarray(v).reshape(-1)
    return v.reshape(-1, P).T


def host_consts():
    con = np.zeros((P, NCONST), np.float32)
    con[:, CCOL["ident"]:CCOL["ident"] + P] = np.eye(P)
    con[:, CCOL["ones"]:CCOL["ones"] + P] = 1.0
    con[:, CCOL["blk64"]:CCOL["blk64"] + P] = np.kron(np.eye(2), np.ones((64, 64)))
    tl = np.linspace(0.0, 1.0, LS, dtype=np.float32)
    con[:, CCOL["tneg"]] = -np.linspace(0.0, 1.0, LP, dtype=np.float32)
    for c in range(4):
        con[:, CCOL["tneg"] + 1 + c] = -tl[c * P:(c + 1) * P]
    con[:, CCOL["iota"]:CCOL["iota"] + TOPK] = np.arange(TOPK)
    s, t = np.meshgrid(np.arange(P), np.arange(P), indexing="ij")
    hg = np.zeros((P, 2, NL + 1, P), np.float32)
    for v, w in enumerate(LEVELS):
        same = (s // (2 * w)) == (t // (2 * w))
        hg[:, 0, v] = same & (s % (2 * w) < w) & (t % (2 * w) >= w)
        hg[:, 1, v] = same & (t % (2 * w) < w) & (s % (2 * w) >= w)
    hg[:, :, NL] = np.eye(P)[:, None]
    reset = np.ones((P, NCH, 129), np.float32)
    reset[:, :, 0] = 0.0
    return con, hg, reset.reshape(P, RESET_W)


def rwkv_masks():
    r, c = np.meshgrid(np.arange(P), np.arange(P), indexing="ij")
    m = np.zeros((P, 2, KINDS, P), np.float32)
    for d, before in enumerate((r < c, r > c)):
        m[:, d, LBT] = m[:, d, LKT] = before
        m[:, d, MBR] = m[:, d, MKR] = before | (r == c)
        m[:, d, LB] = before.T
    b = np.zeros((P, 4, P), np.float32)
    b[:, 0] = (r // 16) == (c // 16)
    for i, w in enumerate((16, 32, 64)):
        b[:, 1 + i] = ((r // (2 * w)) == (c // (2 * w))) & ((r // w) != (c // w))
    return m, b


def dft_tables(L):
    t, k = np.arange(L), np.arange(L)
    ang = np.pi / (2 * L) * ((np.outer(t, 2 * k + 1)) % (4 * L))
    tab = np.stack([np.cos(ang), np.sin(ang)], 1).astype(np.float32)
    n = L // P
    fwd = tab.reshape(n, P, 2, L).transpose(1, 0, 2, 3)
    inv = tab.transpose(2, 1, 0).reshape(n, P, 2, L).transpose(1, 0, 2, 3)
    return fwd, inv


def filter_features(L):
    f = np.float32
    t = np.linspace(0.0, 1.0, L, dtype=f)[:, None]
    bands = np.linspace(1e-4, BANDS - 1, BANDS, dtype=f)[None, :]
    ang = (f(2 * math.pi / L) * np.arange(L, dtype=f))[:, None] * bands
    return np.concatenate([t, np.cos(ang), -np.sin(ang)], axis=1).astype(f).T


def layout(inputs):
    g = {k: np.asarray(v) for k, v in inputs.items()}
    con, hg, reset = host_consts()
    pad64 = lambda v: np.concatenate([np.asarray(v).reshape(64, 1), np.zeros((64, 1), np.float32)])
    par = np.concatenate([
        chan(g["b_ada"]), chan(g["norm1"]), chan(g["norm2"]), chan(g["final_norm"]), chan(g["hgrn_lb_logits"]),
        chan(g["hgrn_norm"]), chan(g["hy_conv_w"]), chan(g["hy_conv_b"]), chan(g["hy_bias"]), chan(g["rw_mu"]),
        chan(g["rw_w0"]), chan(g["rw_a0"]), chan(g["rw_kk"]), chan(g["rw_ka"]), chan(g["rw_rk"]),
        chan(g["rw_ln_g"]), chan(g["rw_ln_b"]), pad64(g["hy_b1"]), pad64(g["hy_freq1"]), pad64(g["hy_b2"]),
        pad64(g["hy_freq2"])], axis=1)
    x = np.concatenate([g["x_prompt"][0], g["x_sample"][0]])
    w_in = g["w_in"][0]
    tiles = w_in.reshape(KD, P, -1, P).transpose(2, 1, 0, 3)
    a = {
        "params": par, "consts": con, "hg_mask": hg, "reset": reset,
        "c": np.stack([g["c_ctx"], g["c"][0]], 1).reshape(KD, P, 2).transpose(1, 0, 2).reshape(P, 16),
        "w_ada": g["w_ada"][0].reshape(KD, P, 8, 768).transpose(2, 1, 0, 3).reshape(8, P, KD * 768),
        "x": x.T.reshape(KD, P, T).transpose(1, 0, 2),
        "w_in": tiles,
        "w_i": w_in[:, 1536:2048].reshape(KD, P, W).transpose(1, 0, 2),
        "state_hgrn": g["state_hgrn"][0, 0].reshape(8, P, DK).transpose(1, 0, 2),
    }
    rw_mask, rw_bmask = rwkv_masks()
    fwd, inv = dft_tables(LS)
    fwd_p, inv_p = dft_tables(LP)
    a.update({
        "fwd": fwd, "inv": inv, "fwd_p": fwd_p[:, 0], "inv_p": inv_p[:, 0],
        "zf": np.concatenate([filter_features(LP), filter_features(LS)], axis=1),
        "hy_w1": g["hy_w1"][0], "hy_w2": g["hy_w2"][0], "hy_w3": g["hy_w3"][0],
        "w_branch": g["w_branch"][0].reshape(3, KW, P, KD, P).transpose(3, 0, 2, 1, 4).reshape(24, P, KW, P),
        "w_out": g["w_out"][0].reshape(KD, P, KD, P).transpose(2, 1, 0, 3),
        "p_wq": g["p_wq"][0].reshape(KD, P, HEADS_P, P).transpose(2, 1, 0, 3),
        "p_keys": np.concatenate([g["p_key1"][0].T, g["p_key2"][0].T]),
        "p_u": g["p_u"][0], "p_v": g["p_v"][0],
        "rw_w2": g["rw_w2"].reshape(P, W), "rw_a2": g["rw_a2"].reshape(P, W), "rw_g2": g["rw_g2"][0],
        "rw_mask": rw_mask, "rw_bmask": rw_bmask,
        "state_rwkv": g["state_rwkv"][0, 0].transpose(0, 1, 3, 2).reshape(8, P, HD).transpose(1, 0, 2),
        "delta": np.broadcast_to(g["hy_delta"], (P, W)),
    })
    return {k: np.ascontiguousarray(v, dtype=v.dtype) for k, v in a.items()}


SCRATCH = {"x_scratch": (P, KD, T), "y_scratch": (2, P, KW, T), "gate_scratch": (len(GATES), P, T)}
OUTS = {"out_hgrn": (8, P, DK), "out_rwkv": (8, P, HD), "out_y": (P, KD, T)}


def kernel(**inputs):
    import concourse.bacc as bacc
    from concourse.bass_utils import run_bass_kernel_spmd

    nc = bacc.Bacc("TRN2", target_bir_lowering=False, num_devices=1)
    arrays = layout(inputs)
    A = {k: nc.dram_tensor("in_" + k, v.shape, mybir.dt.from_np(v.dtype), kind="ExternalInput").ap()
         for k, v in arrays.items()}
    for k, s in OUTS.items():
        A[k] = nc.dram_tensor(k, s, F32, kind="ExternalOutput").ap()
    for k, s in SCRATCH.items():
        A[k] = nc.dram_tensor(k, s, F32, kind="Internal").ap()
    build(nc, A)
    r = run_bass_kernel_spmd(nc, [{"in_" + k: v for k, v in arrays.items()}], core_ids=[0]).results[0]
    y = r["out_y"].transpose(1, 0, 2).reshape(D, T).T
    return (np.ascontiguousarray(y[None, :LP]), np.ascontiguousarray(y[None, LP:]),
            r["out_hgrn"].reshape(1, 1, 2, HEADS_A, DK, DK),
            np.ascontiguousarray(r["out_rwkv"].reshape(2, 8, HD, HD).transpose(0, 1, 3, 2)[None, None]))
```
